# Optimizing a Trainium2 kernel written in Bass

```python
import math
import jax, jax.numpy as jnp
from jax import lax
import numpy as np

D_MODEL = 1024
BATCH = 1
SEQ = 256
DEPTH = 2

MEM_LEN = 256
HEAD_DIM = 64
SELF_WIDTH = 3 * D_MODEL // 4
N_MOBA_HEADS = SELF_WIDTH // HEAD_DIM
N_DIFF_HEADS = SELF_WIDTH // (2 * HEAD_DIM)
N_MEM_HEADS = 4
MEM_WIDTH = N_MEM_HEADS * HEAD_DIM
A_IN = 3 * SELF_WIDTH + MEM_WIDTH
B_IN = SELF_WIDTH + MEM_WIDTH
D_FF = 4 * D_MODEL
MOBA_BLOCK = 256
MOBA_TOPK = 3
Q_BLOCK = 128
MOBA_Q_CHUNK = 32
ROPE_THETA = 10000.0
EPS = 1e-6
NEG = -1e30
N_A_LAYERS = DEPTH // 2
N_B_LAYERS = DEPTH - N_A_LAYERS


def _rmsnorm(x, g):
    xf = x.astype(jnp.float32)
    y = xf * lax.rsqrt(jnp.mean(xf * xf, axis=-1, keepdims=True) + EPS)
    return (y * g.astype(jnp.float32)).astype(x.dtype)

def _rope_tables(n):
    half = HEAD_DIM // 2
    inv = 1.0 / (ROPE_THETA ** (jnp.arange(half, dtype=jnp.float32) / half))
    ang = jnp.arange(n, dtype=jnp.float32)[:, None] * inv[None, :]
    return jnp.cos(ang), jnp.sin(ang)

def _apply_rope(x, cos, sin):
    half = HEAD_DIM // 2
    shp = (x.shape[1],) + (1,) * (x.ndim - 3) + (half,)
    c = cos.reshape(shp)
    s = sin.reshape(shp)
    xf = x.astype(jnp.float32)
    x1, x2 = xf[..., :half], xf[..., half:]
    return jnp.concatenate([x1 * c - x2 * s, x2 * c + x1 * s], axis=-1).astype(x.dtype)

def _sq_relu_mlp(h, w_up, w_down):
    u = jax.nn.relu(h @ w_up)
    return (u * u) @ w_down

def _memory_attention(qm, mem, mem_norm, w_mem_kv):
    B, S = qm.shape[:2]
    M = mem.shape[1]
    kv = _rmsnorm(mem, mem_norm) @ w_mem_kv
    mk = kv[..., :MEM_WIDTH].reshape(B, M, N_MEM_HEADS, HEAD_DIM).astype(jnp.float32)
    mv = kv[..., MEM_WIDTH:].reshape(B, M, N_MEM_HEADS, HEAD_DIM).astype(jnp.float32)
    s = jnp.einsum('bshd,bmhd->bhsm', qm.astype(jnp.float32), mk) * (HEAD_DIM ** -0.5)
    p = jax.nn.softmax(s, axis=-1)
    o = jnp.einsum('bhsm,bmhd->bshd', p, mv)
    return o.reshape(B, S, MEM_WIDTH).astype(qm.dtype)

def _diff_attention(q, k, v, lam, lam_init, subln):
    B, S, H, _, d = q.shape
    nq = S // Q_BLOCK
    kf = k.astype(jnp.float32)
    vf = v.astype(jnp.float32)
    qb = q.astype(jnp.float32).reshape(B, nq, Q_BLOCK, H, 2, d).transpose(1, 0, 2, 3, 4, 5)
    kpos = jnp.arange(S)
    scale = d ** -0.5

    def block(args):
        qi, i = args
        s = jnp.einsum('bqhcd,bkhcd->bhcqk', qi, kf) * scale
        qpos = i * Q_BLOCK + jnp.arange(Q_BLOCK)
        s = jnp.where(kpos[None, :] <= qpos[:, None], s, NEG)
        p = jax.nn.softmax(s, axis=-1)
        w = p[:, :, 0] - lam * p[:, :, 1]
        return jnp.einsum('bhqk,bkhe->bqhe', w, vf)

    o = lax.map(block, (qb, jnp.arange(nq)))
    o = o.transpose(1, 0, 2, 3, 4).reshape(B, S, H, 2 * d)
    o = _rmsnorm(o, subln) * (1.0 - lam_init)
    return o.reshape(B, S, H * 2 * d).astype(v.dtype)

def _moba_attention(q, kbh, vbh, kmean):
    B, S, H, d = q.shape
    NB = kbh.shape[2]
    ksel = min(MOBA_TOPK, NB)
    C = MOBA_Q_CHUNK
    nc = S // C
    qc = q.astype(jnp.float32).transpose(0, 2, 1, 3).reshape(B, H, nc, C, d).transpose(2, 0, 1, 3, 4)
    b_ix = jnp.arange(B)[:, None, None, None]
    h_ix = jnp.arange(H)[None, :, None, None]
    scale = d ** -0.5

    def chunk(args):
        qi, i = args
        qpos = i * C + jnp.arange(C)
        cur = (i * C) // MOBA_BLOCK
        gate = jnp.einsum('bhqd,bhnd->bhqn', qi, kmean)
        gate = jnp.where(jnp.arange(NB) < cur, gate, NEG)
        _, idx = lax.top_k(gate, ksel)
        valid = idx < cur
        k_sel = kbh[b_ix, h_ix, idx]
        v_sel = vbh[b_ix, h_ix, idx]
        s_sel = jnp.einsum('bhqd,bhqnkd->bhqnk', qi, k_sel) * scale
        s_sel = jnp.where(valid[..., None], s_sel, NEG).reshape(B, H, C, ksel * MOBA_BLOCK)
        k_own = lax.dynamic_index_in_dim(kbh, cur, axis=2, keepdims=False)
        v_own = lax.dynamic_index_in_dim(vbh, cur, axis=2, keepdims=False)
        s_own = jnp.einsum('bhqd,bhkd->bhqk', qi, k_own) * scale
        kpos = cur * MOBA_BLOCK + jnp.arange(MOBA_BLOCK)
        s_own = jnp.where(kpos[None, :] <= qpos[:, None], s_own, NEG)
        p = jax.nn.softmax(jnp.concatenate([s_sel, s_own], axis=-1), axis=-1)
        p_sel = p[..., :ksel * MOBA_BLOCK].reshape(B, H, C, ksel, MOBA_BLOCK)
        p_own = p[..., ksel * MOBA_BLOCK:]
        return (jnp.einsum('bhqnk,bhqnkd->bhqd', p_sel, v_sel)
                + jnp.einsum('bhqk,bhkd->bhqd', p_own, v_own))

    o = lax.map(chunk, (qc, jnp.arange(nc)))
    return o.transpose(1, 0, 3, 2, 4).reshape(B, S, H * d).astype(q.dtype)

def first_inputs(seed: int = 0) -> dict:
    key = jax.random.key(seed)
    ks = iter(jax.random.split(key, 40))

    def nrm(shape, scale):
        return jax.random.normal(next(ks), shape, jnp.float32) * scale

    def gain(shape):
        return 1.0 + nrm(shape, 0.02)

    NA, NBL, D = N_A_LAYERS, N_B_LAYERS, D_MODEL
    return {
        "x": nrm((BATCH, SEQ, D), 1.0),
        "mem": nrm((BATCH, MEM_LEN, D), 1.0),
        "a_norm_attn": gain((NA, D)),
        "a_w_in": nrm((NA, D, A_IN), D ** -0.5),
        "a_lambda": nrm((NA, 4, HEAD_DIM), 0.1),
        "a_subln": gain((NA, 2 * HEAD_DIM)),
        "a_mem_norm": gain((NA, D)),
        "a_w_mem_kv": nrm((NA, D, 2 * MEM_WIDTH), D ** -0.5),
        "a_w_out": nrm((NA, D, D), D ** -0.5),
        "a_norm_mlp": gain((NA, D)),
        "a_w_up": nrm((NA, D, D_FF), D ** -0.5),
        "a_w_down": nrm((NA, D_FF, D), D_FF ** -0.5),
        "kv_norm": gain((D,)),
        "w_kv": nrm((D, 2 * SELF_WIDTH), D ** -0.5),
        "b_norm_attn": gain((NBL, D)),
        "b_w_in": nrm((NBL, D, B_IN), D ** -0.5),
        "b_mem_norm": gain((NBL, D)),
        "b_w_mem_kv": nrm((NBL, D, 2 * MEM_WIDTH), D ** -0.5),
        "b_w_out": nrm((NBL, D, D), D ** -0.5),
        "b_norm_mlp": gain((NBL, D)),
        "b_w_up": nrm((NBL, D, D_FF), D ** -0.5),
        "b_w_down": nrm((NBL, D_FF, D), D_FF ** -0.5),
        "final_norm": gain((D,)),
    }

def first_block(x, mem, a_norm_attn, a_w_in, a_lambda, a_subln, a_mem_norm, a_w_mem_kv,
              a_w_out, a_norm_mlp, a_w_up, a_w_down, kv_norm, w_kv, b_norm_attn, b_w_in,
              b_mem_norm, b_w_mem_kv, b_w_out, b_norm_mlp, b_w_up, b_w_down, final_norm):
    B, S, _ = x.shape
    cos, sin = _rope_tables(S)
    kbh = vbh = kmean = None
    for layer in range(DEPTH):
        if layer < N_A_LAYERS:
            i = layer
            h = _rmsnorm(x, a_norm_attn[i])
            z = h @ a_w_in[i]
            w = SELF_WIDTH
            q = z[..., :w].reshape(B, S, N_DIFF_HEADS, 2, HEAD_DIM)
            k = z[..., w:2 * w].reshape(B, S, N_DIFF_HEADS, 2, HEAD_DIM)
            v = z[..., 2 * w:3 * w].reshape(B, S, N_DIFF_HEADS, 2 * HEAD_DIM)
            qm = z[..., 3 * w:].reshape(B, S, N_MEM_HEADS, HEAD_DIM)
            q = _apply_rope(q, cos, sin)
            k = _apply_rope(k, cos, sin)
            lam_init = 0.8 - 0.6 * math.exp(-0.3 * layer)
            lp = a_lambda[i].astype(jnp.float32)
            lam = jnp.exp(jnp.sum(lp[0] * lp[1])) - jnp.exp(jnp.sum(lp[2] * lp[3])) + lam_init
            o_self = _diff_attention(q, k, v, lam, lam_init, a_subln[i])
            o_mem = _memory_attention(qm, mem, a_mem_norm[i], a_w_mem_kv[i])
            x = x + jnp.concatenate([o_self, o_mem], axis=-1) @ a_w_out[i]
            x = x + _sq_relu_mlp(_rmsnorm(x, a_norm_mlp[i]), a_w_up[i], a_w_down[i])
        else:
            j = layer - N_A_LAYERS
            if j == 0:
                hk = _rmsnorm(x, kv_norm)
                kv = hk @ w_kv
                ks_ = _apply_rope(kv[..., :SELF_WIDTH].reshape(B, S, N_MOBA_HEADS, HEAD_DIM), cos, sin)
                vs_ = kv[..., SELF_WIDTH:].reshape(B, S, N_MOBA_HEADS, HEAD_DIM)
                n_blk = -(-S // MOBA_BLOCK)
                pad = n_blk * MOBA_BLOCK - S
                padw = ((0, 0), (0, pad), (0, 0), (0, 0))
                kbh = jnp.pad(ks_.astype(jnp.float32), padw).reshape(
                    B, n_blk, MOBA_BLOCK, N_MOBA_HEADS, HEAD_DIM).transpose(0, 3, 1, 2, 4)
                vbh = jnp.pad(vs_.astype(jnp.float32), padw).reshape(
                    B, n_blk, MOBA_BLOCK, N_MOBA_HEADS, HEAD_DIM).transpose(0, 3, 1, 2, 4)
                kmean = jnp.mean(kbh, axis=3)
            h = _rmsnorm(x, b_norm_attn[j])
            z = h @ b_w_in[j]
            q = _apply_rope(z[..., :SELF_WIDTH].reshape(B, S, N_MOBA_HEADS, HEAD_DIM), cos, sin)
            qm = z[..., SELF_WIDTH:].reshape(B, S, N_MEM_HEADS, HEAD_DIM)
            o_self = _moba_attention(q, kbh, vbh, kmean).astype(x.dtype)
            o_mem = _memory_attention(qm, mem, b_mem_norm[j], b_w_mem_kv[j])
            x = x + jnp.concatenate([o_self, o_mem], axis=-1) @ b_w_out[j]
            x = x + _sq_relu_mlp(_rmsnorm(x, b_norm_mlp[j]), b_w_up[j], b_w_down[j])
    return _rmsnorm(x, final_norm)


N_HEADS = 16
HEAD_DIM_2 = D_MODEL // N_HEADS
D_FF_2 = ((8 * D_MODEL // 3 + 127) // 128) * 128
CONV_WIDTH = 3
CHUNK = 64
N_A_LAYERS_2 = DEPTH // 2
N_B_LAYERS_2 = DEPTH - N_A_LAYERS_2
RMS_EPS = 1e-6
FORGET_BIAS = 3.0


def rmsnorm(x, g):
    xf = x.astype(jnp.float32)
    y = xf * lax.rsqrt(jnp.mean(xf * xf, axis=-1, keepdims=True) + RMS_EPS)
    return (y * g.astype(jnp.float32)).astype(x.dtype)

def split_heads(t):
    b, s, _ = t.shape
    return t.reshape(b, s, N_HEADS, HEAD_DIM_2).transpose(0, 2, 1, 3)

def merge_heads(t):
    b, h, s, d = t.shape
    return t.transpose(0, 2, 1, 3).reshape(b, s, h * d)

def stick_breaking_attention(q, k, v):
    b, h, s, d = q.shape
    scale = HEAD_DIM_2 ** -0.5
    n_blocks = s // Q_BLOCK
    strict = jnp.arange(Q_BLOCK)[:, None] > jnp.arange(Q_BLOCK)[None, :]
    outs = []
    for qi in range(n_blocks):
        lo, hi = qi * Q_BLOCK, (qi + 1) * Q_BLOCK
        qb = q[:, :, lo:hi].astype(jnp.float32) * scale
        kd = k[:, :, lo:hi].astype(jnp.float32)
        vd = v[:, :, lo:hi].astype(jnp.float32)
        z = jnp.einsum('bhtd,bhsd->bhts', qb, kd)
        log_keep = jnp.where(strict, jax.nn.log_sigmoid(-z), 0.0)
        later = lax.cumsum(log_keep, axis=3, reverse=True) - log_keep
        attn = jnp.where(strict, jnp.exp(jax.nn.log_sigmoid(z) + later), 0.0)
        out = jnp.einsum('bhts,bhsd->bhtd', attn, vd)
        log_surv = jnp.sum(log_keep, axis=-1)
        if qi > 0:
            kp = k[:, :, :lo].astype(jnp.float32).reshape(b, h, qi, Q_BLOCK, d)
            vp = v[:, :, :lo].astype(jnp.float32).reshape(b, h, qi, Q_BLOCK, d)
            kp = jnp.flip(jnp.moveaxis(kp, 2, 0), axis=0)
            vp = jnp.flip(jnp.moveaxis(vp, 2, 0), axis=0)

            def step(carry, kv, qb=qb):
                acc, surv = carry
                kb, vb = kv
                zb = jnp.einsum('bhtd,bhsd->bhts', qb, kb)
                lk = jax.nn.log_sigmoid(-zb)
                lat = lax.cumsum(lk, axis=3, reverse=True) - lk + surv[..., None]
                wb = jnp.exp(jax.nn.log_sigmoid(zb) + lat)
                acc = acc + jnp.einsum('bhts,bhsd->bhtd', wb, vb)
                return (acc, surv + jnp.sum(lk, axis=-1)), None

            (out, _), _ = lax.scan(step, (out, log_surv), (kp, vp))
        outs.append(out)
    return jnp.concatenate(outs, axis=2).astype(v.dtype)

def forgetting_attention(q, k, v, fcum):
    s = q.shape[2]
    scale = HEAD_DIM_2 ** -0.5
    outs = []
    for qi in range(s // Q_BLOCK):
        lo, hi = qi * Q_BLOCK, (qi + 1) * Q_BLOCK
        qb = q[:, :, lo:hi].astype(jnp.float32) * scale
        kb = k[:, :, :hi].astype(jnp.float32)
        vb = v[:, :, :hi].astype(jnp.float32)
        logits = (jnp.einsum('bhtd,bhsd->bhts', qb, kb)
                  + fcum[:, :, lo:hi, None] - fcum[:, :, None, :hi])
        causal = (lo + jnp.arange(Q_BLOCK))[:, None] >= jnp.arange(hi)[None, :]
        p = jax.nn.softmax(jnp.where(causal, logits, -jnp.inf), axis=-1)
        outs.append(jnp.einsum('bhts,bhsd->bhtd', p, vb))
    return jnp.concatenate(outs, axis=2).astype(v.dtype)

def conv_ffn(x, w_up, conv_w, conv_b, w_down):
    hdn = x @ w_up
    hdn = lax.conv_general_dilated(
        hdn, conv_w[:, None, :], window_strides=(1,),
        padding=[(CONV_WIDTH - 1, 0)],
        dimension_numbers=('NWC', 'WIO', 'NWC'),
        feature_group_count=2 * D_FF_2) + conv_b
    gate, up = jnp.split(hdn, 2, axis=-1)
    return (jax.nn.gelu(gate, approximate=True) * up) @ w_down

def second_inputs(seed: int = 0) -> dict:
    key = jax.random.key(seed)
    ks = jax.random.split(key, 20)
    D, F, H = D_MODEL, D_FF_2, N_HEADS

    def w(k, shape, fan_in):
        return jax.random.normal(k, shape, jnp.float32) * fan_in ** -0.5

    def gain(k, shape):
        return 1.0 + 0.1 * jax.random.normal(k, shape, jnp.float32)

    return {
        "x": jax.random.normal(ks[0], (BATCH, SEQ, D), jnp.float32),
        "sb_pre_g": gain(ks[1], (N_A_LAYERS_2, D)),
        "sb_w_qkv": w(ks[2], (N_A_LAYERS_2, D, 3 * D), D),
        "sb_w_o": w(ks[3], (N_A_LAYERS_2, D, D), D),
        "sb_post_g": gain(ks[4], (N_A_LAYERS_2, D)),
        "kv_norm_g": gain(ks[5], (D,)),
        "w_kvf": w(ks[6], (D, 2 * D + H), D),
        "b_f": FORGET_BIAS + 0.5 * jax.random.normal(ks[7], (H,), jnp.float32),
        "fox_pre_g": gain(ks[8], (N_B_LAYERS_2, D)),
        "fox_w_q": w(ks[9], (N_B_LAYERS_2, D, D), D),
        "fox_w_o": w(ks[10], (N_B_LAYERS_2, D, D), D),
        "fox_post_g": gain(ks[11], (N_B_LAYERS_2, D)),
        "ffn_pre_g": gain(ks[12], (DEPTH, D)),
        "w_up": w(ks[13], (DEPTH, D, 2 * F), D),
        "conv_w": w(ks[14], (DEPTH, CONV_WIDTH, 2 * F), CONV_WIDTH),
        "conv_b": 0.02 * jax.random.normal(ks[15], (DEPTH, 2 * F), jnp.float32),
        "w_down": w(ks[16], (DEPTH, F, D), F),
        "ffn_post_g": gain(ks[17], (DEPTH, D)),
    }

def second_block(x, sb_pre_g, sb_w_qkv, sb_w_o, sb_post_g, kv_norm_g, w_kvf, b_f,
              fox_pre_g, fox_w_q, fox_w_o, fox_post_g,
              ffn_pre_g, w_up, conv_w, conv_b, w_down, ffn_post_g):
    D = D_MODEL
    h = x
    k_sh = v_sh = fcum_sh = None
    for layer in range(DEPTH):
        if layer < N_A_LAYERS_2:
            a = rmsnorm(h, sb_pre_g[layer])
            q, k, v = jnp.split(a @ sb_w_qkv[layer], 3, axis=-1)
            o = stick_breaking_attention(split_heads(q), split_heads(k), split_heads(v))
            h = h + rmsnorm(merge_heads(o) @ sb_w_o[layer], sb_post_g[layer])
        else:
            if layer == N_A_LAYERS_2:
                s_in = rmsnorm(h, kv_norm_g)
                kvf = s_in @ w_kvf
                k_sh = split_heads(kvf[..., :D])
                v_sh = split_heads(kvf[..., D:2 * D])
                log_f = jax.nn.log_sigmoid(kvf[..., 2 * D:].astype(jnp.float32)
                                           + b_f.astype(jnp.float32))
                fcum_sh = jnp.cumsum(jnp.transpose(log_f, (0, 2, 1)), axis=-1)
            j = layer - N_A_LAYERS_2
            a = rmsnorm(h, fox_pre_g[j])
            q = split_heads(a @ fox_w_q[j])
            o = forgetting_attention(q, k_sh, v_sh, fcum_sh)
            h = h + rmsnorm(merge_heads(o) @ fox_w_o[j], fox_post_g[j])
        f = conv_ffn(rmsnorm(h, ffn_pre_g[layer]), w_up[layer], conv_w[layer],
                     conv_b[layer], w_down[layer])
        h = h + rmsnorm(f, ffn_post_g[layer])
    return h


def setup_inputs(seed=0):
    out = dict(first_inputs(seed))
    for name, value in second_inputs(seed + 1).items():
        if name != "x":
            out[name + "_2"] = value
    return out


def reference(
    x, mem, a_norm_attn, a_w_in, a_lambda, a_subln, a_mem_norm, a_w_mem_kv, a_w_out, a_norm_mlp,
    a_w_up, a_w_down, kv_norm, w_kv, b_norm_attn, b_w_in, b_mem_norm, b_w_mem_kv, b_w_out,
    b_norm_mlp, b_w_up, b_w_down, final_norm, sb_pre_g_2, sb_w_qkv_2, sb_w_o_2, sb_post_g_2,
    kv_norm_g_2, w_kvf_2, b_f_2, fox_pre_g_2, fox_w_q_2, fox_w_o_2, fox_post_g_2, ffn_pre_g_2,
    w_up_2, conv_w_2, conv_b_2, w_down_2, ffn_post_g_2,
):
    x = first_block(
        x, mem, a_norm_attn, a_w_in, a_lambda, a_subln, a_mem_norm, a_w_mem_kv, a_w_out,
        a_norm_mlp, a_w_up, a_w_down, kv_norm, w_kv, b_norm_attn, b_w_in, b_mem_norm,
        b_w_mem_kv, b_w_out, b_norm_mlp, b_w_up, b_w_down, final_norm,
    )
    return second_block(
        x, sb_pre_g_2, sb_w_qkv_2, sb_w_o_2, sb_post_g_2, kv_norm_g_2, w_kvf_2, b_f_2,
        fox_pre_g_2, fox_w_q_2, fox_w_o_2, fox_post_g_2, ffn_pre_g_2, w_up_2, conv_w_2,
        conv_b_2, w_down_2, ffn_post_g_2,
    )


_drawn_inputs = setup_inputs


def setup_inputs(seed=0):
    import zlib

    import numpy as np

    out = dict(_drawn_inputs(seed))
    spreads = {}
    factors = {'a_lambda': 4.633,
     'a_subln': 2.685,
     'a_mem_norm': 8.0,
     'kv_norm': 6.894,
     'b_norm_attn': 8.0,
     'b_mem_norm': 8.0,
     'b_norm_mlp': 3.401,
     'fox_pre_g_2': 2.785}
    for name, (base, spread) in spreads.items():
        noise = np.random.default_rng([zlib.crc32(name.encode()), seed]).standard_normal(out[name].shape)
        drawn = base * np.exp(spread * noise) if base else spread * noise
        out[name] = __import__('jax').numpy.asarray(drawn.astype(out[name].dtype))
    for name, factor in factors.items():
        out[name] = (out[name] * factor).astype(out[name].dtype)
    return out
```

```python
import math
from contextlib import ExitStack

import numpy as np

import concourse.bass as bass
from concourse import mybir

P = 128
D = 1024
TOK = 256
KT = D // P
HEAD = 64
SELF_W = 3 * D // 4
MEM_W = D - SELF_W
D_FF = 4 * D
D_FF2 = ((8 * D // 3 + 127) // 128) * 128
HEADS2 = D // HEAD
NEG = -1e30
EPS = 1e-6
LAM_INIT = 0.8 - 0.6 * math.exp(-0.3 * 0)
RING = 4
SCALE = HEAD ** -0.5

GAINS = ["a_norm_attn", "a_mem_norm", "b_mem_norm", "a_norm_mlp", "kv_norm", "b_norm_attn", "b_norm_mlp",
         "final_norm", "sb_pre_g_2", "sb_post_g_2", "kv_norm_g_2", "fox_pre_g_2", "fox_post_g_2",
         "ffn_pre_g_2.0", "ffn_pre_g_2.1", "ffn_post_g_2.0", "ffn_post_g_2.1"]

ALL_K = (8,)
DOWN_K = (8, 8, 8, 8)
DOWN2_K = (6, 6, 5, 5)

GEMMS = [("mem_a", 4, ALL_K), ("mem_b", 4, ALL_K), ("qk_a", 12, ALL_K), ("vm_a", 8, ALL_K), ("out_a", 8, ALL_K),
         ("up_a", 32, ALL_K), ("down_a", 8, DOWN_K),
         ("q_b", 8, ALL_K), ("kv_b", 8, ALL_K), ("v_b", 4, ALL_K), ("out_b", 8, ALL_K), ("up_b", 32, ALL_K),
         ("down_b", 8, DOWN_K),
         ("qkv_sb", 24, ALL_K), ("out_sb", 8, ALL_K), ("up_sb", 44, ALL_K), ("down_sb", 8, DOWN2_K),
         ("kv_fox", 16, ALL_K), ("q_fox", 8, ALL_K), ("out_fox", 8, ALL_K), ("up_fox", 44, ALL_K),
         ("down_fox", 8, DOWN2_K)]


def stream_plan():
    plan, unit, tile = {}, 0, 0
    for name, tiles, ks in GEMMS:
        body = RING if len(ks) == 1 else 2
        plan[name] = dict(name=name, tiles=tiles, ks=ks, unit=unit, tile=tile, body=body, trips=tiles // body,
                          units=tiles * len(ks))
        unit += tiles * len(ks)
        tile += tiles
    return plan


ATTENTIONS = {"diff": 12, "mem_a": 4, "moba": 12, "mem_b": 4, "stick": 16, "forget": 16}


def attention_plan():
    plan, n, t, tiles = {}, 0, 0, 0
    for name, units in ATTENTIONS.items():
        rows = []
        for u in range(units):
            half = u % 2
            emits = name != "diff" or half == 1
            rows.append(dict(n=n, j=u // 2, half=half, emits=emits, t=t, tile=tiles, kind=name))
            n += 1
            t += emits
            tiles += half
        plan[name] = rows
    return plan


def build_program(nc, ins, out):
    f32, f32r = mybir.dt.float32, mybir.dt.float32r
    ALU, ACT, AX = mybir.AluOpType, mybir.ActivationFunctionType, mybir.AxisListType
    plan, heads = stream_plan(), attention_plan()
    order = [g[0] for g in GEMMS]

    ctx = ExitStack()
    with ctx:
        def sb(name, shape, dt=f32):
            return ctx.enter_context(nc.sbuf_tensor(name, shape, dt))

        def sem(name):
            return ctx.enter_context(nc.semaphore(name))

        raw = sb("raw", [P, RING, KT * P])
        w_hi = sb("w_hi", [P, RING, KT * P], f32r)
        w_lo = sb("w_lo", [P, RING, KT * P], f32r)
        X = sb("X", [P, KT, TOK])
        h1_hi = sb("h1_hi", [P, KT, TOK], f32r)
        h1_lo = sb("h1_lo", [P, KT, TOK], f32r)
        h2_hi = sb("h2_hi", [P, KT, TOK], f32r)
        h2_lo = sb("h2_lo", [P, KT, TOK], f32r)
        H = sb("H", [P, KT, TOK])
        ZM = sb("ZM", [P, KT, TOK])
        mv_tok = sb("mv_tok", [P, 2, 2, MEM_W])
        wf_hi = sb("wf_hi", [P, KT, P], f32r)
        wf_lo = sb("wf_lo", [P, KT, P], f32r)
        ident = sb("ident_sb", [P, P])
        ones = sb("ones_sb", [P, TOK])
        rope_c = sb("rope_c_sb", [P, TOK])
        rope_s = sb("rope_s_sb", [P, TOK])
        mask_in = sb("mask_in_sb", [P, 3 * P])
        mask_ex = sb("mask_ex_sb", [P, 3 * P])
        gains = sb("gains_sb", [P, len(GAINS), KT])
        subln = sb("subln_sb", [P, 1])
        subln_s = sb("subln_s", [P, 1])
        conv = sb("conv_sb", [P, 2, 4, 2 * D_FF2 // P])
        lam_in = sb("lam_in_sb", [P, 4, HEAD])
        lam_prod = sb("lam_prod", [P, 2, HEAD])
        lam_sum = sb("lam_sum", [P, 2])
        lam_exp = sb("lam_exp", [P, 2])
        neg_lam = sb("neg_lam", [P, 1])
        b_f = sb("b_f_sb", [P, 1])
        eps_col = sb("eps_col", [P, 1])
        sumsq = sb("sumsq", [P, TOK])
        square = sb("square", [P, 2, TOK])
        log_ms = sb("log_ms", [P, TOK])
        rstd = sb("rstd", [P, TOK])
        unit_max = sb("unit_max", [P, 4, 2])
        unit_bias = sb("unit_bias", [P, 4, 2])
        unit_sum = sb("unit_sum", [P, 4, 2])
        unit_rcp = sb("unit_rcp", [P, 4, 2])

        with ExitStack() as mlp:
            def mlp_sb(name, shape, dt=f32):
                return mlp.enter_context(nc.sbuf_tensor(name, shape, dt))

            a_hi = mlp_sb("a_hi", [P, D_FF // P, TOK], f32r)
            a_lo = mlp_sb("a_lo", [P, D_FF // P, TOK], f32r)
            c_buf2 = mlp_sb("conv_buf", [P, 4, TOK])
            prod = mlp_sb("prod", [P, 2, TOK])
        u_buf = H[:, 0:4, :]
        m_buf = H[:, 4:6, :]
        gate = H[:, 6:8, :]
        Z = sb("Z", [P, 24, TOK])
        ROT = sb("ROT", [P, 12, TOK])
        v_tok = sb("v_tok", [P, 2, D])
        s_buf = sb("s_buf", [P, 2, 2 * TOK])
        n_buf = sb("n_buf", [P, 2, 2 * TOK])
        c_buf = sb("c_buf", [P, 2, 2 * TOK])
        p_buf = sb("p_buf", [P, 3, 2 * TOK])
        pt_buf = sb("pt_buf", [P, 2, 2 * TOK])
        f_x = sb("f_x", [P, TOK])
        f_n = sb("f_n", [P, TOK])
        f_p = sb("f_p", [P, TOK])
        f_sum = sb("f_sum", [P, TOK])
        neg_fcum8 = sb("neg_fcum8", [P, TOK])

        bank = [ctx.enter_context(nc.psum_tensor(f"bank{b}", [P, 2 * TOK], f32)) for b in range(8)]

        consts_in = sem("consts_in")
        x_in = sem("x_in")
        mem_in = sem("mem_in")
        raw_in = [sem(f"raw_in{s}") for s in range(RING)]
        hi_ready = sem("hi_ready")
        lo_ready = sem("lo_ready")
        units_done = sem("units_done")
        tile_out = sem("tile_out")
        sq_done = sem("sq_done")
        sum_done = sem("sum_done")
        ms_done = sem("ms_done")
        rstd_ready = sem("rstd_ready")
        h_hi = sem("h_hi")
        h_lo = sem("h_lo")
        y_even = sem("y_even")
        y_odd = sem("y_odd")
        x_changed = sem("x_changed")
        dve_step = sem("dve_step")
        act_step = sem("act_step")
        pool_step = sem("pool_step")
        rot_in = [sem(f"rot_in{g}") for g in range(4)]
        roped = sem("roped")
        vt_done = sem("vt_done")
        vt_out = sem("vt_out")
        s_done = sem("s_done")
        s_out = sem("s_out")
        exp_done = sem("exp_done")
        arg_ready = sem("arg_ready")
        p_ready = sem("p_ready")
        t_done = sem("t_done")
        t_out = sem("t_out")
        o_done = sem("o_done")
        o_hi_out = sem("o_hi_out")
        o_out = sem("o_out")
        gelu_ready = sem("gelu_ready")
        tap2_ready = sem("tap2_ready")
        tap1_ready = sem("tap1_ready")
        m_ready = sem("m_ready")
        taps_done = sem("taps_done")
        prod_ready = sem("prod_ready")
        a_hi_ready = sem("a_hi_ready")
        a_ready = sem("a_ready")
        lam_ready = sem("lam_ready")
        sub_ready = sem("sub_ready")
        sub_ms = sem("sub_ms")
        sub_rstd = sem("sub_rstd")
        sub_hi = sem("sub_hi")
        wf_in = sem("wf_in")
        wf_split = sem("wf_split")
        f_logits = sem("f_logits")
        f_abs = sem("f_abs")
        f_log = sem("f_log")
        f_ready = sem("f_ready")
        out_done = sem("out_done")

        block = ctx.enter_context(nc.Block())

        OPERANDS = {"mem_a": (0, 1), "mem_b": (8, 1), "qk_a": (16, 1), "up_a": (24, 1), "q_b": (32, 2),
                    "kv_b": (33, 2), "up_b": (48, 1), "qkv_sb": (56, 1), "up_sb": (64, 1), "kv_fox": (72, 2),
                    "q_fox": (73, 2), "up_fox": (88, 1)}
        GAIN_OF = {"mem_a": "a_mem_norm", "mem_b": "b_mem_norm", "qk_a": "a_norm_attn", "up_a": "a_norm_mlp",
                   "q_b": "b_norm_attn", "kv_b": "kv_norm", "up_b": "b_norm_mlp", "qkv_sb": "sb_pre_g_2",
                   "up_sb": "ffn_pre_g_2.0", "kv_fox": "kv_norm_g_2", "q_fox": "fox_pre_g_2",
                   "up_fox": "ffn_pre_g_2.1"}
        NORMS = {n: i for i, n in enumerate(
            ["mem_a", "qk_a", "up_a", "q_b", "up_b", "final", "qkv_sb", "post_sb", "up_sb", "post_ffn_sb",
             "kv_fox", "post_fox", "up_fox", "post_ffn_fox"])}
        MS_AFTER = {"mem_a": 2, "qk_a": 1, "up_a": 1, "q_b": 1, "up_b": 1, "qkv_sb": 2, "up_sb": 2, "kv_fox": 2,
                    "up_fox": 2}

        def gain(name, k):
            return gains[:, GAINS.index(name), bass.ds(k, 1)]

        def operand_count(name, i, per, k):
            first, step = OPERANDS[name]
            return i * (per * step) + (first + step * k + 1)

        PRODUCTS = {"up_a": 0, "up_b": D_FF // P, "up_sb": 2 * D_FF // P, "up_fox": 2 * D_FF // P + D_FF2 // P}
        DOWN_OF = {"down_a": "up_a", "down_b": "up_b", "down_sb": "up_sb", "down_fox": "up_fox"}
        FIRST_TAP = {"up_sb": 0, "up_fox": 2 * D_FF2 // P}
        by_n = {u["n"]: u for units in heads.values() for u in units}
        DIFF_TILES = 6
        CONSTS = [(ones, "ones"), (ident, "ident"), (rope_c, "rope_c"), (rope_s, "rope_s"),
                  (mask_in, "mask_in"), (mask_ex, "mask_ex"), (subln, "subln"),
                  (conv, "conv"), (lam_in, "lam"), (b_f, "b_f")]

        def geometry(units):
            w0 = TOK if units[0]["kind"].startswith("mem") else P
            return w0, w0 + TOK

        @block.sync
        def _(sp):
            sp.dma_start(gains[:], ins["gains"]).then_inc(mem_in, 16)
            sp.dma_start(ZM[:], ins["mem"]).then_inc(mem_in, 16)

            def load(g, f, part, free, slot):
                at, k = sum(g["ks"][:part]), g["ks"][part]
                if free is not None:
                    sp.wait_ge(lo_ready, free)
                sp.dma_start(raw[:, slot, 0:k * P],
                             ins["w_" + g["name"]][f, :, at * P:(at + k) * P]).then_inc(raw_in[slot], 16)

            for name in order:
                g = plan[name]
                nk, body = len(g["ks"]), g["body"]
                if g["trips"] == 1:
                    for s in range(body):
                        load(g, s, 0, g["unit"] + s - RING + 1 if g["unit"] else None, s % RING)
                    if name == "mem_a":
                        sp.dma_start(X[:], ins["x"]).then_inc(x_in, 16)
                        for dst, const in CONSTS:
                            sp.dma_start(dst[:], ins[const]).then_inc(consts_in, 16)
                        sp.dma_start(H[:, 0:KT // 2, :].rearrange("p a (b c) -> p (a b) c", c=P),
                                     ins["w_f"]).then_inc(wf_in, 16)
                else:
                    with sp.Fori(0, g["trips"]) as i:
                        for s in range(body * nk):
                            load(g, i * body + s // nk, s % nk, i * (body * nk) + (g["unit"] + s - RING + 1),
                                 s % RING)
            sp.wait_ge(x_changed, 5 * KT)
            sp.dma_start(out, X[:]).then_inc(out_done, 16)
            sp.wait_ge(out_done, 16)

        @block.tensor
        def _(pe):
            n_ms, n_vt = [0], [0]

            def gemm(name, src_hi, src_lo):
                g = plan[name]
                nk, body = len(g["ks"]), g["body"]
                banks = RING if nk == 1 else 2

                def trip(i, first=False):
                    for s in range(body * nk):
                        part, b = s % nk, s // nk % banks
                        pe.wait_ge(lo_ready, i * (body * nk) + (g["unit"] + s + 1))
                        if part == 0 and g["tile"]:
                            pe.wait_ge(tile_out, i * body + (g["tile"] + s // nk - banks + 1))
                        at, slot, k_tiles = sum(g["ks"][:part]), s % RING, g["ks"][part]
                        if name in DOWN_OF:
                            pe.wait_ge(a_ready, RING + PRODUCTS[DOWN_OF[name]] + at + k_tiles)
                        for k in range(k_tiles):
                            w = slice(k * P, (k + 1) * P)
                            begin, end = part == 0 and k == 0, part == nk - 1 and k == k_tiles - 1
                            dst = bank[b][:, 0:TOK]
                            if first and s == 0:
                                pe.wait_ge(h_lo, operand_count(name, 0, 0, k))
                            nc.tensor.matmul(dst, w_hi[:, slot, w], src_hi[:, at + k, :], start=begin, stop=False)
                            nc.tensor.matmul(dst, w_hi[:, slot, w], src_lo[:, at + k, :], start=False, stop=False)
                            last = nc.tensor.matmul(dst, w_lo[:, slot, w], src_hi[:, at + k, :], start=False,
                                                    stop=end)
                        last.then_inc(units_done, 1)
                        if first and s == MS_AFTER.get(name):
                            mean_square()

                peeled = name in OPERANDS
                if peeled or g["trips"] == 1:
                    trip(0, peeled)
                if g["trips"] > 1:
                    with pe.Fori(1 if peeled else 0, g["trips"]) as i:
                        trip(i)

            def mean_square():
                pe.wait_ge(sum_done, KT * (n_ms[0] + 1))
                if n_ms[0]:
                    pe.wait_ge(rstd_ready, n_ms[0])
                nc.tensor.matmul(bank[7][:, 0:TOK], ones[:, 0:P], sumsq[:], start=True,
                                 stop=True).then_inc(ms_done, 1)
                n_ms[0] += 1

            def transpose_values(src, first, tiles):
                for j in range(first, first + tiles, 2):
                    if n_vt[0]:
                        pe.wait_ge(vt_out, n_vt[0])
                    for tt in range(2):
                        for jj in range(2):
                            last = nc.tensor.transpose(bank[6][:, tt * TOK + jj * P:tt * TOK + (jj + 1) * P],
                                                       src[:, j + jj, tt * P:(tt + 1) * P], ident[:])
                    last.then_inc(vt_done, 1)
                    n_vt[0] += 1

            def attention(units, q, k, v):
                w0, whole = geometry(units)
                mem = w0 == TOK

                def scores(u):
                    rows = slice(HEAD * u["half"], HEAD * (u["half"] + 1))
                    if u["n"] >= 2:
                        pe.wait_ge(s_out, u["n"] - 1)
                    forget = u["kind"] == "forget"
                    for qt in range(2):
                        width = w0 if qt == 0 else TOK
                        dst = bank[4 + u["n"] % 2][:, qt * w0:qt * w0 + width]
                        last = nc.tensor.matmul(dst, q(u["j"])[rows, qt * P:(qt + 1) * P],
                                                k(u["j"])[rows, 0:width], start=True, stop=not forget)
                        if forget:
                            c = HEAD * u["half"] + 2 * u["j"] + u["half"]
                            last = nc.tensor.matmul(dst, ident[rows, c:c + 1].broadcast_to([HEAD, P]),
                                                    neg_fcum8[rows, 0:width], start=False, stop=True)
                    last.then_inc(s_done, 1)

                def transposes(u):
                    if not u["emits"]:
                        return
                    pe.wait_ge(p_ready, u["n"] + 1)
                    pe.wait_ge(vt_out, n_vt[0])
                    if u["t"]:
                        pe.wait_ge(t_out, u["t"])
                    pieces = [(0, 0), (P, w0)] + ([(TOK, P), (TOK + P, TOK + P)] if mem else [(TOK, TOK)])
                    for dst, src in pieces:
                        last = nc.tensor.transpose(bank[6][:, dst:dst + P], p_buf[:, u["n"] % 3, src:src + P],
                                                   ident[:])
                    last.then_inc(t_done, 1)

                def outputs(u):
                    if not u["emits"]:
                        return
                    pe.wait_ge(t_out, u["t"] + 1)
                    diff = u["kind"] == "diff"
                    if (diff or u["half"] == 0) and u["tile"] >= 2:
                        pe.wait_ge(o_out, u["tile"] - 1)
                    rows = slice(0, P) if diff else slice(HEAD * u["half"], HEAD * (u["half"] + 1))
                    cols = slice(u["j"] * P + rows.start, u["j"] * P + rows.stop)
                    dst, pt = bank[(7, 3)[u["tile"] % 2]], pt_buf[:, u["t"] % 2, :]
                    nc.tensor.matmul(dst[rows, 0:TOK], v[:, 0, cols], pt[:, 0:TOK], start=True, stop=False)
                    last = nc.tensor.matmul(dst[rows, (0 if mem else P):TOK], v[:, 1, cols],
                                            pt[:, TOK:(2 * TOK if mem else TOK + P)], start=False, stop=True)
                    last.then_inc(o_done, 1)

                for i in range(len(units) + 3):
                    if i < len(units):
                        scores(units[i])
                    if 0 <= i - 2 < len(units):
                        transposes(units[i - 2])
                    if 0 <= i - 3 < len(units):
                        outputs(units[i - 3])

            def projected(name):
                g = plan[name]
                pe.wait_ge(tile_out, g["tile"] + g["tiles"])

            def attended(name):
                pe.wait_ge(o_out, heads[name][-1]["tile"] + 1)

            pe.wait_ge(consts_in, 16 * len(CONSTS))
            gemm("mem_a", h2_hi, h2_lo)
            gemm("mem_b", a_hi, a_lo)
            gemm("qk_a", h1_hi, h1_lo)
            transpose_values(ZM, 2, 2)
            transpose_values(ZM, 6, 2)
            gemm("vm_a", h1_hi, h1_lo)
            projected("vm_a")
            transpose_values(Z, 12, 6)
            pe.wait_ge(vt_out, n_vt[0])
            pe.wait_ge(roped, 2)
            attention(heads["diff"], lambda j: Z[:, j, :], lambda j: Z[:, 6 + j, :], v_tok)
            attention(heads["mem_a"], lambda j: Z[:, 18 + j, :], lambda j: ZM[:, j, :], mv_tok[:, 0])
            pe.wait_ge(sub_ready, 1)
            for j in range(DIFF_TILES):
                last = nc.tensor.matmul(bank[j // 2][:, j % 2 * TOK:(j % 2 + 1) * TOK], ones[:, 0:P],
                                        ROT[:, 6 + j, :], start=True, stop=True)
            last.then_inc(sub_ms, 1)
            attended("mem_a")
            pe.wait_ge(sub_ready, 3)
            gemm("out_a", h1_hi, h1_lo)
            gemm("up_a", h2_hi, h2_lo)
            gemm("down_a", a_hi, a_lo)
            gemm("q_b", h2_hi, h2_lo)
            gemm("kv_b", h1_hi, h1_lo)
            gemm("v_b", h1_hi, h1_lo)
            projected("v_b")
            transpose_values(Z, 14, 6)
            pe.wait_ge(vt_out, n_vt[0])
            pe.wait_ge(roped, 4)
            attention(heads["moba"], lambda j: Z[:, j, :], lambda j: Z[:, 8 + j, :], v_tok)
            attention(heads["mem_b"], lambda j: Z[:, 6 + j, :], lambda j: ZM[:, 4 + j, :], mv_tok[:, 1])
            attended("mem_b")
            gemm("out_b", h1_hi, h1_lo)
            gemm("up_b", h2_hi, h2_lo)
            gemm("down_b", a_hi, a_lo)
            mean_square()
            gemm("qkv_sb", h1_hi, h1_lo)
            projected("qkv_sb")
            transpose_values(Z, 16, 8)
            pe.wait_ge(vt_out, n_vt[0])
            attention(heads["stick"], lambda j: Z[:, j, :], lambda j: Z[:, 8 + j, :], v_tok)
            attended("stick")
            gemm("out_sb", h1_hi, h1_lo)
            mean_square()
            gemm("up_sb", h2_hi, h2_lo)
            gemm("down_sb", a_hi, a_lo)
            mean_square()
            gemm("kv_fox", h1_hi, h1_lo)
            pe.wait_ge(wf_split, 2)
            for k in range(KT):
                dst = bank[6][:, 0:TOK]
                nc.tensor.matmul(dst, wf_hi[:, k, :], h1_hi[:, k, :], start=k == 0, stop=False)
                nc.tensor.matmul(dst, wf_hi[:, k, :], h1_lo[:, k, :], start=False, stop=False)
                last = nc.tensor.matmul(dst, wf_lo[:, k, :], h1_hi[:, k, :], start=False, stop=k == KT - 1)
            last.then_inc(f_logits, 1)
            gemm("q_fox", h2_hi, h2_lo)
            projected("q_fox")
            pe.wait_ge(f_ready, 1)
            transpose_values(Z, 8, 8)
            pe.wait_ge(vt_out, n_vt[0])
            attention(heads["forget"], lambda j: Z[:, 16 + j, :], lambda j: Z[:, j, :], v_tok)
            attended("forget")
            gemm("out_fox", h1_hi, h1_lo)
            mean_square()
            gemm("up_fox", h2_hi, h2_lo)
            gemm("down_fox", a_hi, a_lo)
            mean_square()

        def run_projection(eng, name, lead, split, before=None, after=None, middle=None, peel=False):
            g = plan[name]
            nk, body = len(g["ks"]), g["body"]
            per = body * nk
            at = order.index(name)
            following = plan[order[at + 1]] if at + 1 < len(order) else None

            def trip(i, first, last):
                held = []
                for s in range(per):
                    ahead = s + lead
                    holds = first and middle is not None and s <= MS_AFTER[name]
                    finished = (i, i * per + (g["unit"] + s + 1), s // nk, first)
                    if before is not None and s % nk == nk - 1:
                        before(*finished)
                    if not last or ahead < per:
                        split(i, per, g["unit"] + ahead, g["ks"][ahead % nk])
                    elif following is not None:
                        split(i, per, g["unit"] + ahead, following["ks"][(ahead - per) % len(following["ks"])])
                    if after is not None and s % nk == nk - 1:
                        held.append(finished)
                    if holds and s == MS_AFTER[name]:
                        middle()
                    if not holds or s == MS_AFTER[name]:
                        for tile in held:
                            after(*tile)
                        held.clear()

            peel = peel or middle is not None
            if peel and g["trips"] > 1:
                trip(0, True, False)
            start = 1 if peel else 0
            if g["trips"] - 1 > start:
                with eng.Fori(start, g["trips"] - 1) as i:
                    trip(i, False, False)
            trip(g["trips"] - 1, g["trips"] == 1, True)

        @block.scalar
        def _(act):
            steps, n_norm, n_vt = [0], [0], [0]

            def link(instruction):
                steps[0] += 1
                instruction.then_inc(act_step, 1)
                act.wait_ge(act_step, steps[0])

            def split(i, per_trip, unit, k):
                slot = unit % RING
                act.wait_ge(raw_in[slot], i * (per_trip // RING * 16) + 16 * (unit // RING + 1))
                if unit >= RING:
                    act.wait_ge(units_done, i * per_trip + (unit - RING + 1))
                nc.scalar.copy(w_hi[:, slot, 0:k * P], raw[:, slot, 0:k * P]).then_inc(hi_ready, 1)

            def high(name, src, dst, i, per, k):
                nc.scalar.activation(dst[:, i * per + k, :], src[:, i * per + k, :], ACT.Identity,
                                     scale=gain(GAIN_OF[name], i * per + k)).then_inc(h_hi, 1)

            def squared(norm, src, i, per, k, signal=None):
                n = KT * NORMS[norm] + k
                if n >= 2:
                    act.wait_ge(sum_done, i * per + (n - 1))
                nc.scalar.activation(square[:, k % 2, :], src, ACT.Square).then_inc(sq_done, 1)

            def stream_tile(name, operands, norm):
                per = plan[name]["body"]

                def tile(i, done, b, first):
                    act.wait_ge(tile_out, i * per + (plan[name]["tile"] + b + 1))
                    for operand, dst in operands:
                        high(operand, X, dst, i, per, b)
                    at = i * (per * TOK) + b * TOK
                    squared(norm, X[:].rearrange("p k t -> p (k t)")[:, bass.ds(at, TOK)], i, per, b)
                return tile

            def output_tile(name, norm, g):
                per = plan[name]["body"]

                def tile(i, done, b, first):
                    act.wait_ge(units_done, done)
                    squared(norm, bank[b][:, 0:TOK], i, per, b)
                    nc.scalar.activation(H[:, i * per + b, :], bank[b][:, 0:TOK], ACT.Identity,
                                         scale=gain(g, i * per + b)).then_inc(tile_out, 1)
                return tile

            def relu(name):
                base, first_tile = PRODUCTS[name], plan[name]["tile"]

                def tile(i, done, b, first):
                    act.wait_ge(tile_out, i * 4 + (first_tile + b + 1))
                    nc.scalar.activation(a_hi[:, i * 4 + b, :], u_buf[:, b, :], ACT.Square).then_inc(a_hi_ready, 1)
                return tile

            def conv_high(name, i, b):
                pair = b // 2 - 1
                act.wait_ge(prod_ready, i * 2 + (PRODUCTS[name] + pair + 1))
                nc.scalar.copy(a_hi[:, i * 2 + pair, :], prod[:, pair % 2, :]).then_inc(a_hi_ready, 1)

            def conv_gelu(name):
                base, tap0, first_tile = PRODUCTS[name], FIRST_TAP[name], plan[name]["tile"]
                layer = 0 if name == "up_sb" else 1

                def tile(i, done, b, first):
                    pair = b // 2
                    act.wait_ge(tile_out, i * 4 + (first_tile + b + 1))
                    act.wait_ge(prod_ready, i * 2 + (base + pair - 1))
                    nc.scalar.activation(c_buf2[:, b, :], u_buf[:, b % 2, :], ACT.Identity,
                                         scale=conv[:, layer, 2, bass.ds(i * 4 + b, 1)],
                                         bias=conv[:, layer, 3, bass.ds(i * 4 + b, 1)]).then_inc(tap2_ready, 1)
                    if b % 2:
                        act.wait_ge(taps_done, i * 4 + (tap0 + b))
                        nc.scalar.activation(gate[:, pair, :], c_buf2[:, b - 1, :],
                                             ACT.Gelu_apprx_tanh).then_inc(gelu_ready, 1)
                    elif not (first and b == 0):
                        conv_high(name, i, b)
                return tile

            def project(name, before=None, after=None, middle=None, peel=False):
                run_projection(act, name, RING, split, before, after, middle, peel)

            def norm_scale():
                act.wait_ge(ms_done, n_norm[0] + 1)
                if n_norm[0] == NORMS["qk_a"]:
                    act.wait_ge(tile_out, plan["qk_a"]["tile"])
                link(nc.scalar.activation(log_ms[:], bank[7][:, 0:TOK], ACT.Ln, scale=1.0 / D, bias=eps_col[:]))
                nc.scalar.activation(rstd[:], log_ms[:], ACT.Exp, scale=-0.5).then_inc(rstd_ready, 1)
                n_norm[0] += 1

            def conv_scale():
                norm_scale()
                nc.scalar.preload_act_table(ACT.Gelu_apprx_tanh)

            def after_change(count, operands, norm):
                for k in range(KT):
                    act.wait_ge(x_changed, count + k + 1)
                    for operand, dst in operands:
                        high(operand, X, dst, 0, 0, k)
                for k in range(KT):
                    squared(norm, X[:, k, :], 0, 0, k)

            def rotate(g, first):
                for piece in range(4):
                    src, dst = 32 * (piece ^ 1), 32 * piece
                    act.dma_start(ROT[dst:dst + 32, 6 * (g % 2):6 * (g % 2) + 6, :],
                                  Z[src:src + 32, first:first + 6, :]).then_inc(rot_in[g], 16)

            def copy_values(dst, first, tiles):
                for j in range(0, tiles, 2):
                    act.wait_ge(vt_done, n_vt[0] + 1)
                    nc.scalar.copy(dst[:, :, (first + j) * P:(first + j + 2) * P],
                                   bank[6][:].rearrange("p (t c) -> p t c", t=2)).then_inc(vt_out, 1)
                    n_vt[0] += 1

            def attention(units):
                kind = units[0]["kind"]
                stick, diff, mem = kind == "stick", kind == "diff", kind.startswith("mem")
                w0, whole = geometry(units)

                def exps(u):
                    n = u["n"]
                    act.wait_ge(s_out, n + 1)
                    if stick:
                        nb = n_buf[:, n % 2, 0:whole]
                        link(nc.scalar.activation(nb, nb, ACT.Exp))
                        nc.scalar.activation(nb, nb, ACT.Ln, bias=1.0).then_inc(exp_done, 1)
                        return
                    free_probabilities(n)
                    for qt in range(2):
                        cols = slice(0, w0) if qt == 0 else slice(w0, whole)
                        last = nc.scalar.activation(p_buf[:, n % 3, cols], s_buf[:, n % 2, cols], ACT.Exp,
                                                    bias=unit_bias[:, n % 4, qt:qt + 1], scale=SCALE,
                                                    accum_out=unit_sum[:, n % 4, qt:qt + 1])
                    last.then_inc(exp_done, 1)

                def free_probabilities(n):
                    if n >= 3:
                        old = by_n[n - 3]
                        if old["emits"]:
                            act.wait_ge(t_done, old["t"] + 1)
                        else:
                            act.wait_ge(p_ready, n - 1)

                def weights(u):
                    n = u["n"]
                    act.wait_ge(arg_ready, n - units[0]["n"] + 1)
                    free_probabilities(n)
                    nc.scalar.activation(p_buf[:, n % 3, 0:whole], c_buf[:, n % 2, 0:whole],
                                         ACT.Exp).then_inc(p_ready, 1)

                def copies(u):
                    act.wait_ge(t_done, u["t"] + 1)
                    if u["t"] >= 2:
                        act.wait_ge(o_done, u["t"] - 1)
                    nc.scalar.copy(pt_buf[:, u["t"] % 2, 0:whole], bank[6][:, 0:whole]).then_inc(t_out, 1)

                def out_hi(u):
                    act.wait_ge(o_done, u["t"] + 1)
                    src = bank[(7, 3)[u["tile"] % 2]][:, 0:TOK]
                    if diff:
                        nc.scalar.copy(H[:, u["j"], :], src).then_inc(o_out, 1)
                    else:
                        j = u["j"] + (DIFF_TILES if mem else 0)
                        nc.scalar.copy(h1_hi[:, j, :], src).then_inc(o_hi_out, 1)

                for i in range(len(units) + 3):
                    if i < len(units):
                        exps(units[i])
                    if stick and 0 <= i - 1 < len(units):
                        weights(units[i - 1])
                    if 0 <= i - 2 < len(units) and units[i - 2]["emits"]:
                        copies(units[i - 2])
                    if 0 <= i - 3 < len(units) and units[i - 3]["half"]:
                        out_hi(units[i - 3])

            nc.scalar.preload_act_table_set("natural_log_exp_and_others")
            act.wait_ge(mem_in, 32)
            for k in range(KT):
                high("mem_a", ZM, h2_hi, 0, 0, k)
            for u in range(RING):
                split(0, RING, u, KT)
                for k in (2 * u, 2 * u + 1):
                    squared("mem_a", ZM[:, k, :], 0, 0, k)
            for k in range(KT):
                high("mem_b", ZM, a_hi, 0, 0, k)
            act.wait_ge(a_ready, RING)
            project("mem_a", middle=norm_scale)
            act.wait_ge(x_in, 16)
            for k in range(KT):
                high("qk_a", X, h1_hi, 0, 0, k)
            project("mem_b")
            for k in range(KT):
                squared("qk_a", X[:, k, :], 0, 0, k)
            project("qk_a", middle=norm_scale)
            act.wait_ge(tile_out, plan["vm_a"]["tile"])
            rotate(0, 0)
            rotate(1, 6)
            copy_values(mv_tok[:, 0], 0, 2)
            copy_values(mv_tok[:, 1], 0, 2)
            act.wait_ge(lam_ready, 1)
            nc.scalar.activation(lam_exp[:], lam_sum[:], ACT.Exp).then_inc(lam_ready, 1)
            act.wait_ge(wf_in, 16)
            nc.scalar.copy(wf_hi[:], H[:, 0:KT // 2, :].rearrange("p a (b c) -> p (a b) c", c=P)).then_inc(wf_split, 1)
            project("vm_a")
            copy_values(v_tok, 0, 6)
            attention(heads["diff"])
            attention(heads["mem_a"])
            act.wait_ge(sub_ms, 1)
            for b in range(3):
                last = nc.scalar.activation(ROT[:, 2 * b:2 * b + 2, :],
                                            bank[b][:].rearrange("p (t c) -> p t c", t=2), ACT.Ln,
                                            scale=1.0 / (2 * HEAD), bias=eps_col[:])
            link(last)
            nc.scalar.activation(ROT[:, 0:6, :], ROT[:, 0:6, :], ACT.Exp, scale=-0.5).then_inc(sub_rstd, 1)
            act.wait_ge(sub_ready, 2)
            nc.scalar.copy(h1_hi[:, 0:6, :], H[:, 0:6, :]).then_inc(sub_hi, 1)
            project("out_a", before=stream_tile("out_a", [("up_a", h2_hi)], "up_a"))
            project("up_a", after=relu("up_a"), middle=norm_scale)
            project("down_a", before=stream_tile("down_a", [("q_b", h2_hi), ("kv_b", h1_hi)], "q_b"))
            project("q_b", middle=norm_scale)
            act.wait_ge(tile_out, plan["kv_b"]["tile"])
            rotate(2, 0)
            project("kv_b")
            act.wait_ge(tile_out, plan["v_b"]["tile"])
            rotate(3, 8)
            project("v_b")
            copy_values(v_tok, 0, 6)
            attention(heads["moba"])
            attention(heads["mem_b"])
            project("out_b", before=stream_tile("out_b", [("up_b", h2_hi)], "up_b"))
            project("up_b", after=relu("up_b"), middle=norm_scale)
            project("down_b", before=stream_tile("down_b", [], "final"))
            norm_scale()
            after_change(0, [("qkv_sb", h1_hi)], "qkv_sb")
            project("qkv_sb", middle=norm_scale)
            copy_values(v_tok, 0, 8)
            attention(heads["stick"])
            project("out_sb", before=output_tile("out_sb", "post_sb", "sb_post_g_2"))
            norm_scale()
            after_change(KT, [("up_sb", h2_hi)], "up_sb")
            project("up_sb", after=conv_gelu("up_sb"), middle=conv_scale)
            conv_high("up_sb", plan["up_sb"]["trips"], 0)
            project("down_sb", before=output_tile("down_sb", "post_ffn_sb", "ffn_post_g_2.0"))
            norm_scale()
            after_change(2 * KT, [("kv_fox", h1_hi), ("q_fox", h2_hi)], "kv_fox")
            project("kv_fox", middle=norm_scale)
            act.wait_ge(f_abs, 1)
            link(nc.scalar.activation(f_n[:], f_n[:], ACT.Exp))
            nc.scalar.activation(f_n[:], f_n[:], ACT.Ln, bias=1.0).then_inc(f_log, 1)
            project("q_fox")
            copy_values(v_tok, 0, 8)
            attention(heads["forget"])
            project("out_fox", before=output_tile("out_fox", "post_fox", "fox_post_g_2"))
            norm_scale()
            after_change(3 * KT, [("up_fox", h2_hi)], "up_fox")
            project("up_fox", after=conv_gelu("up_fox"), middle=conv_scale)
            conv_high("up_fox", plan["up_fox"]["trips"], 0)
            project("down_fox", before=output_tile("down_fox", "post_ffn_fox", "ffn_post_g_2.1"))
            norm_scale()

        @block.vector
        def _(dve):
            steps, n_x = [0], [0]

            def link(instruction):
                steps[0] += 1
                instruction.then_inc(dve_step, 1)
                dve.wait_ge(dve_step, steps[0])

            def split(i, per_trip, unit, k):
                slot = unit % RING
                dve.wait_ge(hi_ready, i * per_trip + (unit + 1))
                nc.vector.tensor_tensor(w_lo[:, slot, 0:k * P], raw[:, slot, 0:k * P],
                                        w_hi[:, slot, 0:k * P].bitcast(f32), ALU.subtract).then_inc(lo_ready, 1)

            def take(name, norm, dst, shift=0):
                per = plan[name]["body"]

                def tile(i, done, b, first):
                    dve.wait_ge(units_done, done)
                    dve.wait_ge(rstd_ready, NORMS[norm] + 1)
                    nc.vector.tensor_tensor(dst[:, i * per + (shift + b), :], bank[b][:, 0:TOK], rstd[:],
                                            ALU.mult).then_inc(tile_out, 1)
                return tile

            def low(name, src, dst_hi, dst_lo, i, per, k):
                at = i * per + k
                dve.wait_ge(h_hi, operand_count(name, i, per, k))
                nc.vector.scalar_tensor_tensor(dst_lo[:, at, :], src[:, at, :], gain(GAIN_OF[name], at),
                                               dst_hi[:, at, :].bitcast(f32), ALU.mult,
                                               ALU.subtract).then_inc(h_lo, 1)

            def residual(name, operands):
                per = plan[name]["body"]

                def tile(i, done, b, first):
                    dve.wait_ge(units_done, done)
                    x = X[:, i * per + b, :]
                    nc.vector.tensor_tensor(x, bank[b][:, 0:TOK], x, ALU.add).then_inc(tile_out, 1)
                    for operand, hi, lo in operands:
                        low(operand, X, hi, lo, i, per, b)
                return tile

            def split_product(i, per, m, slot, dst):
                dve.wait_ge(prod_ready, i * per + (m + 1))
                dve.wait_ge(a_hi_ready, i * per + (m + 1))
                nc.vector.tensor_tensor(a_lo[:, dst, :], prod[:, slot, :], a_hi[:, dst, :].bitcast(f32),
                                        ALU.subtract).then_inc(a_ready, 1)

            def relu(name):
                base = PRODUCTS[name]

                def before(i, done, b, first):
                    dve.wait_ge(units_done, done)
                    dve.wait_ge(rstd_ready, NORMS[name] + 1)
                    dve.wait_ge(a_ready, i * 4 + (base + b + 1))
                    nc.vector.scalar_tensor_tensor(u_buf[:, b, :], bank[b][:, 0:TOK], 0.0, rstd[:], ALU.max,
                                                   ALU.mult).then_inc(tile_out, 1)

                def after(i, done, b, first):
                    split_product(i, 4, base + b, b % 2, i * 4 + b)
                return before, after

            def conv_low(name, i, b):
                pair = b // 2 - 1
                split_product(i, 2, PRODUCTS[name] + pair, pair % 2, i * 2 + pair)

            def conv_taps(name):
                tap0, first_tile = FIRST_TAP[name], plan[name]["tile"]
                layer = 0 if name == "up_sb" else 1

                def before(i, done, b, first):
                    dve.wait_ge(units_done, done)
                    dve.wait_ge(rstd_ready, NORMS[name] + 1)
                    if not first or b >= 2:
                        dve.wait_ge(m_ready, i * 4 + (tap0 + b - 1))
                        dve.wait_ge(tap1_ready, i * 4 + (tap0 + b - 1))
                    nc.vector.tensor_tensor(u_buf[:, b % 2, :], bank[b][:, 0:TOK], rstd[:],
                                            ALU.mult).then_inc(tile_out, 1)

                def after(i, done, b, first):
                    dve.wait_ge(tap2_ready, i * 4 + (tap0 + b + 1))
                    dve.wait_ge(tile_out, i * 4 + (first_tile + b + 1))
                    nc.vector.scalar_tensor_tensor(c_buf2[:, b, 1:TOK], u_buf[:, b % 2, 0:TOK - 1],
                                                   conv[:, layer, 1, bass.ds(i * 4 + b, 1)],
                                                   c_buf2[:, b, 1:TOK], ALU.mult, ALU.add).then_inc(tap1_ready, 1)
                    if b % 2 == 0 and not (first and b == 0):
                        conv_low(name, i, b)
                return before, after

            def project(name, before=None, after=None, peel=False):
                run_projection(dve, name, RING - 1, split, before, after, None, peel)

            def rstd_next(norm):
                dve.wait_ge(rstd_ready, NORMS[norm] + 1)

            def add_normed(norm, operands):
                rstd_next(norm)
                a = n_x[0]

                def lows(k):
                    for operand, hi, lo in operands:
                        low(operand, X, hi, lo, 0, 0, k)

                for k in range(KT):
                    if k % 2 == 0:
                        nc.vector.tensor_tensor(H[:, k, :], H[:, k, :], rstd[:], ALU.mult).then_inc(y_even, 1)
                        dve.wait_ge(y_even, (a - KT + k) // 2 + 1)
                    else:
                        dve.wait_ge(y_odd, (a - KT + k) // 2 + 1)
                    nc.vector.tensor_tensor(X[:, k, :], X[:, k, :], H[:, k, :], ALU.add).then_inc(x_changed, 1)
                    if k:
                        lows(k - 1)
                lows(KT - 1)
                n_x[0] += KT

            def attention(units):
                kind = units[0]["kind"]
                stick, diff, mem = kind == "stick", kind == "diff", kind.startswith("mem")
                w0, whole = geometry(units)
                query_tiles = (slice(0, w0), slice(w0, whole))
                no_mask = mask_in[:, P:2 * P].unsqueeze(1).broadcast_to([P, 2, P])

                def pieces(ap):
                    return ap.rearrange("p (a c) -> p a c", c=P) if mem else ap

                def masked(u):
                    n = u["n"]
                    b = bank[4 + n % 2]
                    dve.wait_ge(s_done, n + 1)
                    if n >= 2:
                        dve.wait_ge(exp_done, n - 1)
                    if stick:
                        if n - units[0]["n"] >= 2:
                            dve.wait_ge(arg_ready, n - units[0]["n"] - 1)
                        z = s_buf[:, n % 2, 0:whole]
                        link(nc.vector.scalar_tensor_tensor(z, b[:, 0:whole], SCALE, mask_ex[:], ALU.mult, ALU.add))
                        nc.vector.scalar_tensor_tensor(n_buf[:, n % 2, 0:whole], z, -1.0, z, ALU.mult,
                                                       ALU.min).then_inc(s_out, 1)
                        return
                    for qt, cols in enumerate(query_tiles):
                        last = nc.vector.tensor_tensor_reduce(
                            out=pieces(s_buf[:, n % 2, cols]), in0=pieces(b[:, cols]), in1=no_mask if mem else mask_in[:, cols],
                            scale=1.0, scalar=-3.0e38, op0=ALU.add, op1=ALU.max,
                            accum_out=unit_max[:, n % 4, qt:qt + 1])
                    link(last)
                    nc.vector.tensor_scalar(unit_bias[:, n % 4, :], unit_max[:, n % 4, :], -SCALE, None,
                                            ALU.mult).then_inc(s_out, 1)

                def normalised(u):
                    n = u["n"]
                    rcp = unit_rcp[:, n % 4, :]
                    dve.wait_ge(exp_done, n + 1)
                    link(nc.vector.reciprocal(rcp, unit_sum[:, n % 4, :]))
                    second = diff and u["half"]
                    if second:
                        link(nc.vector.tensor_scalar(rcp, rcp, neg_lam[:], None, ALU.mult))
                        dve.wait_ge(p_ready, n)
                    for qt, cols in enumerate(query_tiles):
                        p = p_buf[:, n % 3, cols]
                        if second:
                            last = nc.vector.scalar_tensor_tensor(p, p, rcp[:, qt:qt + 1],
                                                                  p_buf[:, (n - 1) % 3, cols], ALU.mult, ALU.add)
                        else:
                            last = nc.vector.tensor_scalar(p, p, rcp[:, qt:qt + 1], None, ALU.mult)
                    last.then_inc(p_ready, 1)

                def log_weights(u):
                    n = u["n"]
                    z, sp, c = s_buf[:, n % 2, 0:whole], n_buf[:, n % 2, 0:whole], c_buf[:, n % 2, 0:whole]
                    dve.wait_ge(exp_done, n + 1)
                    link(nc.vector.scalar_tensor_tensor(sp, z, 0.0, sp, ALU.max, ALU.add))
                    if n - units[0]["n"] >= 2:
                        dve.wait_ge(p_ready, n - 1)
                    for cols in query_tiles:
                        last = nc.vector.tensor_tensor_scan(c[:, cols][:, ::-1], ones[:, 0:cols.stop - cols.start],
                                                            sp[:, cols][:, ::-1], 0.0, ALU.mult, ALU.subtract)
                    link(last)
                    nc.vector.tensor_tensor(c, c, z, ALU.add).then_inc(arg_ready, 1)

                def out_lo(u):
                    dve.wait_ge(o_hi_out, u["tile"] - DIFF_TILES + 1)
                    j = u["j"] + (DIFF_TILES if mem else 0)
                    nc.vector.tensor_tensor(h1_lo[:, j, :], bank[(7, 3)[u["tile"] % 2]][:, 0:TOK],
                                            h1_hi[:, j, :].bitcast(f32), ALU.subtract).then_inc(o_out, 1)

                for i in range(len(units) + 4):
                    if i < len(units):
                        masked(units[i])
                    if 0 <= i - 1 < len(units):
                        log_weights(units[i - 1]) if stick else normalised(units[i - 1])
                    if 0 <= i - 4 < len(units) and units[i - 4]["half"] and not diff:
                        out_lo(units[i - 4])

            nc.vector.memset(eps_col[:], EPS).then_inc(a_ready, RING)
            for k in range(KT):
                low("mem_a", ZM, h2_hi, h2_lo, 0, 0, k)
            for u in range(RING - 1):
                split(0, RING, u, KT)
            for k in range(KT):
                low("mem_b", ZM, a_hi, a_lo, 0, 0, k)
            dve.wait_ge(h_lo, 2 * KT)
            project("mem_a", before=take("mem_a", "mem_a", ZM))
            for k in range(KT):
                low("qk_a", X, h1_hi, h1_lo, 0, 0, k)
            project("mem_b", before=take("mem_b", "mem_a", ZM, 4))
            project("qk_a", before=take("qk_a", "qk_a", Z), peel=True)
            dve.wait_ge(consts_in, 16 * len(CONSTS))
            nc.vector.tensor_scalar(subln_s[:], subln[:], 1.0 - LAM_INIT, None, ALU.mult)
            for pair in range(2):
                last = nc.vector.tensor_tensor(lam_prod[:, pair, :], lam_in[:, 2 * pair, :],
                                               lam_in[:, 2 * pair + 1, :], ALU.mult)
            link(last)
            nc.vector.tensor_reduce(lam_sum[:], lam_prod[:], AX.X, ALU.add).then_inc(lam_ready, 1)
            dve.wait_ge(lam_ready, 2)
            link(nc.vector.tensor_tensor(neg_lam[:], lam_exp[:, 1:2], lam_exp[:, 0:1], ALU.subtract))
            nc.vector.tensor_scalar(neg_lam[:], neg_lam[:], -LAM_INIT, None, ALU.add).then_inc(lam_ready, 1)
            dve.wait_ge(wf_split, 1)
            nc.vector.tensor_tensor(wf_lo[:], H[:, 0:KT // 2, :].rearrange("p a (b c) -> p (a b) c", c=P),
                                    wf_hi[:].bitcast(f32), ALU.subtract).then_inc(wf_split, 1)
            project("vm_a", before=take("vm_a", "qk_a", Z, 12))
            dve.wait_ge(lam_ready, 3)
            attention(heads["diff"])
            dve.wait_ge(o_out, DIFF_TILES)
            nc.vector.tensor_tensor(ROT[:, 6:12, :], H[:, 0:6, :], H[:, 0:6, :], ALU.mult).then_inc(sub_ready, 1)
            attention(heads["mem_a"])
            dve.wait_ge(sub_rstd, 1)
            dve.wait_ge(sub_ready, 1)
            nc.vector.scalar_tensor_tensor(H[:, 0:6, :], H[:, 0:6, :], subln_s[:], ROT[:, 0:6, :], ALU.mult,
                                           ALU.mult).then_inc(sub_ready, 1)
            dve.wait_ge(sub_ready, 2)
            dve.wait_ge(sub_hi, 1)
            nc.vector.tensor_tensor(h1_lo[:, 0:6, :], H[:, 0:6, :], h1_hi[:, 0:6, :].bitcast(f32),
                                    ALU.subtract).then_inc(sub_ready, 1)
            dve.wait_ge(sub_ready, 3)
            project("out_a", before=residual("out_a", [("up_a", h2_hi, h2_lo)]))
            project("up_a", *relu("up_a"))
            project("down_a", before=residual("down_a", [("q_b", h2_hi, h2_lo), ("kv_b", h1_hi, h1_lo)]))
            project("q_b", before=take("q_b", "q_b", Z))
            project("kv_b", before=take("kv_b", "q_b", Z, 8))
            project("v_b", before=take("v_b", "q_b", Z, 16))
            attention(heads["moba"])
            attention(heads["mem_b"])
            project("out_b", before=residual("out_b", [("up_b", h2_hi, h2_lo)]))
            project("up_b", *relu("up_b"))
            project("down_b", before=residual("down_b", []))
            rstd_next("final")
            for k in range(KT):
                nc.vector.scalar_tensor_tensor(X[:, k, :], X[:, k, :], gain("final_norm", k), rstd[:], ALU.mult,
                                               ALU.mult).then_inc(x_changed, 1)
                if k:
                    dve.wait_ge(x_changed, k)
                    low("qkv_sb", X, h1_hi, h1_lo, 0, 0, k - 1)
            dve.wait_ge(x_changed, KT)
            low("qkv_sb", X, h1_hi, h1_lo, 0, 0, KT - 1)
            n_x[0] += KT
            project("qkv_sb", before=take("qkv_sb", "qkv_sb", Z))
            attention(heads["stick"])
            project("out_sb")
            add_normed("post_sb", [("up_sb", h2_hi, h2_lo)])
            project("up_sb", *conv_taps("up_sb"), peel=True)
            conv_low("up_sb", plan["up_sb"]["trips"], 0)
            project("down_sb")
            add_normed("post_ffn_sb", [("kv_fox", h1_hi, h1_lo), ("q_fox", h2_hi, h2_lo)])
            project("kv_fox", before=take("kv_fox", "kv_fox", Z))
            dve.wait_ge(f_logits, 1)
            link(nc.vector.tensor_tensor(f_x[:], bank[6][:, 0:TOK], rstd[:], ALU.mult))
            link(nc.vector.tensor_scalar(f_x[:], f_x[:], b_f[:], -1.0, ALU.add, ALU.mult))
            nc.vector.scalar_tensor_tensor(f_n[:], f_x[:], -1.0, f_x[:], ALU.mult, ALU.min).then_inc(f_abs, 1)
            dve.wait_ge(f_log, 1)
            link(nc.vector.scalar_tensor_tensor(f_p[:], f_x[:], 0.0, f_n[:], ALU.max, ALU.add))
            link(nc.vector.tensor_tensor_scan(f_sum[:], ones[:], f_p[:], 0.0, ALU.mult, ALU.add))
            nc.vector.tensor_scalar(neg_fcum8[:], f_sum[:], 1.0 / SCALE, None, ALU.mult).then_inc(f_ready, 1)
            project("q_fox", before=take("q_fox", "kv_fox", Z, 16))
            attention(heads["forget"])
            project("out_fox")
            add_normed("post_fox", [("up_fox", h2_hi, h2_lo)])
            project("up_fox", *conv_taps("up_fox"), peel=True)
            conv_low("up_fox", plan["up_fox"]["trips"], 0)
            project("down_fox")
            add_normed("post_ffn_fox", [])

        @block.gpsimd
        def _(pool):
            steps, n_odd = [0], [0]

            def link(instruction):
                steps[0] += 1
                instruction.then_inc(pool_step, 1)
                pool.wait_ge(pool_step, steps[0])

            def sum_squares(norm):
                n = NORMS[norm]
                if n:
                    pool.wait_ge(ms_done, n)
                link(nc.gpsimd.memset(sumsq[:], 0.0))

                def add(i, b, first):
                    pool.wait_ge(sq_done, i * 2 + (KT * n + b + 1))
                    if n or not first:
                        pool.wait_ge(sum_done, i * 2 + (KT * n + b))
                    nc.gpsimd.tensor_tensor(sumsq[:], sumsq[:], square[:, b, :], ALU.add).then_inc(sum_done, 1)

                add(0, 0, True)
                add(0, 1, False)
                with pool.Fori(1, KT // 2) as i:
                    add(i, 0, False)
                    add(i, 1, False)

            def rope(g, first):
                z, rot = Z[:, first:first + 6, :], ROT[:, 6 * (g % 2):6 * (g % 2) + 6, :]
                pool.wait_ge(rot_in[g], 64)
                nc.gpsimd.tensor_tensor(z, z, rope_c[:].unsqueeze(1).broadcast_to([P, 6, TOK]),
                                        ALU.mult).then_inc(pool_step, 1)
                steps[0] += 1
                link(nc.gpsimd.tensor_tensor(rot, rot, rope_s[:].unsqueeze(1).broadcast_to([P, 6, TOK]), ALU.mult))
                nc.gpsimd.tensor_tensor(z, z, rot, ALU.add).then_inc(roped, 1)

            def scale_odd(norm):
                pool.wait_ge(rstd_ready, NORMS[norm] + 1)
                for k in range(1, KT, 2):
                    nc.gpsimd.tensor_tensor(H[:, k, :], H[:, k, :], rstd[:], ALU.mult).then_inc(y_odd, 1)

            def relu(name):
                base, first_tile = PRODUCTS[name], plan[name]["tile"]
                with pool.Fori(0, plan[name]["trips"]) as i:
                    for b in range(4):
                        pool.wait_ge(tile_out, i * 4 + (first_tile + b + 1))
                        pool.wait_ge(a_ready, i * 4 + (base + b + RING - 1))
                        nc.gpsimd.tensor_tensor(prod[:, b % 2, :], u_buf[:, b, :], u_buf[:, b, :],
                                                ALU.mult).then_inc(prod_ready, 1)

            def conv_products(name):
                base, tap0, first_tile = PRODUCTS[name], FIRST_TAP[name], plan[name]["tile"]
                layer = 0 if name == "up_sb" else 1

                def trip(i, first):
                    for b in range(4):
                        pair = base + b // 2
                        pool.wait_ge(tile_out, i * 4 + (first_tile + b + 1))
                        if not (first and b < 2):
                            pool.wait_ge(taps_done, i * 4 + (tap0 + b - 1))
                        nc.gpsimd.tensor_tensor(m_buf[:, b % 2, :], u_buf[:, b % 2, :],
                                                conv[:, layer, 0, bass.ds(i * 4 + b, 1)].broadcast_to([P, TOK]),
                                                ALU.mult).then_inc(m_ready, 1)
                        pool.wait_ge(m_ready, i * 4 + (tap0 + b + 1))
                        pool.wait_ge(tap1_ready, i * 4 + (tap0 + b + 1))
                        c = c_buf2[:, b, 2:TOK]
                        nc.gpsimd.tensor_tensor(c, c, m_buf[:, b % 2, 0:TOK - 2], ALU.add).then_inc(taps_done, 1)
                        if b % 2:
                            pool.wait_ge(taps_done, i * 4 + (tap0 + b + 1))
                            pool.wait_ge(gelu_ready, i * 2 + (pair - PRODUCTS["up_sb"] + 1))
                            pool.wait_ge(a_ready, i * 2 + (pair + RING - 1))
                            nc.gpsimd.tensor_tensor(prod[:, b // 2, :], gate[:, b // 2, :], c_buf2[:, b, :],
                                                    ALU.mult).then_inc(prod_ready, 1)

                trip(0, True)
                with pool.Fori(1, plan[name]["trips"]) as i:
                    trip(i, False)

            sum_squares("mem_a")
            sum_squares("qk_a")
            rope(0, 0)
            rope(1, 6)
            sum_squares("up_a")
            relu("up_a")
            sum_squares("q_b")
            rope(2, 0)
            rope(3, 8)
            sum_squares("up_b")
            relu("up_b")
            sum_squares("final")
            sum_squares("qkv_sb")
            sum_squares("post_sb")
            scale_odd("post_sb")
            sum_squares("up_sb")
            conv_products("up_sb")
            sum_squares("post_ffn_sb")
            scale_odd("post_ffn_sb")
            sum_squares("kv_fox")
            sum_squares("post_fox")
            scale_odd("post_fox")
            sum_squares("up_fox")
            conv_products("up_fox")
            sum_squares("post_ffn_fox")
            scale_odd("post_ffn_fox")


def tiles_of(w):
    k, n = w.shape
    return np.ascontiguousarray(w.reshape(k // P, P, n // P, P).transpose(2, 1, 0, 3).reshape(n // P, P, k))


def feature_major(t):
    return np.ascontiguousarray(t.T.reshape(KT, P, TOK).transpose(1, 0, 2))


def shape_constants():
    half = HEAD // 2
    inv = (1.0 / (np.float32(10000.0) ** (np.arange(half, dtype=np.float32) / np.float32(half)))).astype(np.float32)
    angle = (np.arange(TOK, dtype=np.float32)[:, None] * inv[None, :]).T
    cos, sin = np.cos(angle).astype(np.float32), np.sin(angle).astype(np.float32)
    q, k = np.arange(P)[:, None], np.arange(P)[None, :]
    inclusive = np.where(k <= q, 0.0, NEG).astype(np.float32)
    strict = np.where(k < q, 0.0, NEG).astype(np.float32)
    seen = np.zeros((P, P), np.float32)
    return {"ones": np.ones((P, TOK), np.float32),
            "ident": np.eye(P, dtype=np.float32), "rope_c": np.concatenate([cos] * 4),
            "rope_s": np.concatenate([-sin, sin] * 2),
            "mask_in": np.concatenate([inclusive, seen, inclusive], axis=1),
            "mask_ex": np.concatenate([strict, seen, strict], axis=1)}


def kernel(**inputs):
    import concourse.bacc as bacc
    from concourse.bass_utils import run_bass_kernel_spmd

    a = {k: np.asarray(v) for k, v in inputs.items()}
    up2 = [a["w_up_2"][i].reshape(D, 2, D_FF2 // P, P).transpose(0, 2, 1, 3).reshape(D, 2 * D_FF2)
           for i in range(2)]
    qkv = a["w_kvf_2"]
    weights = {"mem_a": a["a_w_mem_kv"][0], "mem_b": a["b_w_mem_kv"][0],
               "qk_a": a["a_w_in"][0][:, :2 * SELF_W], "vm_a": a["a_w_in"][0][:, 2 * SELF_W:],
               "out_a": a["a_w_out"][0], "up_a": a["a_w_up"][0], "down_a": a["a_w_down"][0],
               "q_b": a["b_w_in"][0], "kv_b": a["w_kv"][:, :D], "v_b": a["w_kv"][:, D:],
               "out_b": a["b_w_out"][0], "up_b": a["b_w_up"][0],
               "down_b": a["b_w_down"][0], "qkv_sb": a["sb_w_qkv_2"][0], "out_sb": a["sb_w_o_2"][0],
               "up_sb": up2[0], "down_sb": a["w_down_2"][0], "kv_fox": qkv[:, :2 * D], "q_fox": a["fox_w_q_2"][0],
               "out_fox": a["fox_w_o_2"][0], "up_fox": up2[1], "down_fox": a["w_down_2"][1]}
    arrays = {"w_" + name: tiles_of(w) for name, w in weights.items()}
    arrays["x"] = feature_major(a["x"][0])
    arrays["mem"] = feature_major(a["mem"][0])

    def row(name):
        base, _, at = name.partition(".")
        return a[base][int(at)] if at else a[base].reshape(D)

    arrays["gains"] = np.ascontiguousarray(np.stack([row(n) for n in GAINS]).reshape(len(GAINS), KT, P)
                                           .transpose(2, 0, 1))
    arrays["subln"] = np.ascontiguousarray(a["a_subln"].reshape(P, 1))
    taps = np.concatenate([a["conv_w_2"], a["conv_b_2"][:, None, :]], axis=1)
    arrays["conv"] = np.ascontiguousarray(taps.reshape(2, 4, 2, D_FF2 // P, P).transpose(4, 0, 1, 3, 2)
                                          .reshape(P, 2, 4, 2 * D_FF2 // P))
    arrays["lam"] = np.ascontiguousarray(np.broadcast_to(a["a_lambda"][0], (P, 4, HEAD)))
    w_f, b_f = np.zeros((D, P), np.float32), np.zeros((P, 1), np.float32)
    for at in (0, HEAD):
        w_f[:, at:at + HEADS2] = qkv[:, 2 * D:]
        b_f[at:at + HEADS2, 0] = a["b_f_2"]
    arrays["w_f"] = np.ascontiguousarray(w_f.reshape(KT, P, P).transpose(1, 0, 2))
    arrays["b_f"] = b_f
    arrays.update(shape_constants())

    nc = bacc.Bacc("TRN2", target_bir_lowering=False, num_devices=1)
    ins = {name: nc.dram_tensor("in_" + name, v.shape, mybir.dt.from_np(v.dtype), kind="ExternalInput").ap()
           for name, v in arrays.items()}
    out = nc.dram_tensor("out_x", (P, KT, TOK), mybir.dt.float32, kind="ExternalOutput").ap()
    build_program(nc, ins, out)
    r = run_bass_kernel_spmd(nc, [{"in_" + name: v for name, v in arrays.items()}], core_ids=[0])
    got = np.asarray(r.results[0]["out_x"])
    return np.ascontiguousarray(got.transpose(1, 0, 2).reshape(D, TOK).T).reshape(1, TOK, D)
```

```python
import math
from contextlib import ExitStack

import numpy as np

import concourse.bass as bass
from concourse import mybir

P = 128
D = 1024
TOK = 256
KT = D // P
HEAD = 64
SELF_W = 3 * D // 4
MEM_W = D - SELF_W
D_FF = 4 * D
D_FF2 = ((8 * D // 3 + 127) // 128) * 128
HEADS2 = D // HEAD
NEG = -1e30
EPS = 1e-6
LAM_INIT = 0.8 - 0.6 * math.exp(-0.3 * 0)
RING = 4
SCALE = HEAD ** -0.5

GAINS = ["a_norm_attn", "a_mem_norm", "b_mem_norm", "a_norm_mlp", "kv_norm", "b_norm_attn", "b_norm_mlp",
         "final_norm", "sb_pre_g_2", "sb_post_g_2", "kv_norm_g_2", "fox_pre_g_2", "fox_post_g_2",
         "ffn_pre_g_2.0", "ffn_pre_g_2.1", "ffn_post_g_2.0", "ffn_post_g_2.1"]

ALL_K = (8,)
DOWN_K = (8, 8, 8, 8)
DOWN2_K = (6, 6, 5, 5)

GEMMS = [("mem_a", 4, ALL_K), ("mem_b", 4, ALL_K),
         ("in_a", 20, ALL_K), ("out_a", 8, ALL_K), ("up_a", 32, ALL_K), ("down_a", 8, DOWN_K),
         ("in_b", 20, ALL_K), ("out_b", 8, ALL_K), ("up_b", 32, ALL_K), ("down_b", 8, DOWN_K),
         ("in_sb", 24, ALL_K), ("out_sb", 8, ALL_K), ("up_sb", 44, ALL_K), ("down_sb", 8, DOWN2_K),
         ("in_fox", 24, ALL_K), ("out_fox", 8, ALL_K), ("up_fox", 44, ALL_K), ("down_fox", 8, DOWN2_K)]

VALUE_GROUPS = {"in_a": (512, 256), "in_b": (512, 256), "in_sb": (512, 512), "in_fox": (512, 512)}


def stream_plan():
    plan, unit, tile = {}, 0, 0
    for name, tiles, ks in GEMMS:
        body = RING if len(ks) == 1 else 2
        values = sum(VALUE_GROUPS.get(name, ())) // P
        plan[name] = dict(name=name, tiles=tiles, ks=ks, unit=unit, tile=tile, body=body, trips=tiles // body,
                          units=tiles * len(ks), values=values)
        unit += tiles * len(ks)
        tile += tiles - values
    return plan


def value_units(name):
    units, first = [], 0
    for group, width in enumerate(VALUE_GROUPS[name]):
        per = D // width
        units += [(group, first, width, range(k, k + per)) for k in range(0, KT, per)]
        first += width
    return units


ATTENTIONS = {"mem_a": 4, "diff": 12, "mem_b": 4, "moba": 12, "stick": 16, "forget": 16}
FUSED = {"in_a": ("mem_a", "diff"), "in_b": ("mem_b", "moba"), "in_sb": ("stick",), "in_fox": ("forget",)}
LAG = {"in_a": 2, "in_b": 2, "in_sb": 3, "in_fox": 3}


def attention_plan():
    plan, n, t, tiles, plain = {}, 0, 0, 0, 0
    for name, units in ATTENTIONS.items():
        rows = []
        for u in range(units):
            half = u % 2
            diff = name == "diff"
            emits = not diff or half == 1
            rows.append(dict(n=n, j=u // 2, half=half, emits=emits, t=t, tile=tiles, plain=plain, diff=diff,
                             mem=name.startswith("mem"), stick=name == "stick", kind=name,
                             first=n - u))
            n += 1
            t += emits
            tiles += half
            plain += half and not diff
        plan[name] = rows
    return plan


def build_program(nc, ins, out):
    f32, f32r = mybir.dt.float32, mybir.dt.float32r
    ALU, ACT, AX = mybir.AluOpType, mybir.ActivationFunctionType, mybir.AxisListType
    plan, heads = stream_plan(), attention_plan()
    order = [g[0] for g in GEMMS]

    ctx = ExitStack()
    with ctx:
        def sb(name, shape, dt=f32):
            return ctx.enter_context(nc.sbuf_tensor(name, shape, dt))

        def sem(name):
            return ctx.enter_context(nc.semaphore(name))

        raw = sb("raw", [P, RING, KT * P])
        w_hi = sb("w_hi", [P, RING, KT * P], f32r)
        w_lo = sb("w_lo", [P, RING, KT * P], f32r)
        X = sb("X", [P, KT, TOK])
        h1_hi = sb("h1_hi", [P, KT, TOK], f32r)
        h1_lo = sb("h1_lo", [P, KT, TOK], f32r)
        h2_hi = sb("h2_hi", [P, KT, TOK], f32r)
        h2_lo = sb("h2_lo", [P, KT, TOK], f32r)
        H = sb("H", [P, KT, TOK])
        ZM = sb("ZM", [P, KT, TOK])
        mv_tok = sb("mv_tok", [P, 2, 2, MEM_W])
        wf_hi = sb("wf_hi", [P, KT, P], f32r)
        wf_lo = sb("wf_lo", [P, KT, P], f32r)
        ident = sb("ident_sb", [P, P])
        ones = sb("ones_sb", [P, TOK])
        rope_c = sb("rope_c_sb", [P, TOK])
        rope_s = sb("rope_s_sb", [P, TOK])
        mask_in = sb("mask_in_sb", [P, 3 * P])
        mask_ex = sb("mask_ex_sb", [P, 3 * P])
        gains = sb("gains_sb", [P, len(GAINS), KT])
        subln = sb("subln_sb", [P, 1])
        subln_s = sb("subln_s", [P, 1])
        conv = sb("conv_sb", [P, 2, 4, 2 * D_FF2 // P])
        lam_in = sb("lam_in_sb", [P, 4, HEAD])
        lam_prod = sb("lam_prod", [P, 2, HEAD])
        lam_sum = sb("lam_sum", [P, 2])
        lam_exp = sb("lam_exp", [P, 2])
        neg_lam = sb("neg_lam", [P, 1])
        b_f = sb("b_f_sb", [P, 1])
        eps_col = sb("eps_col", [P, 1])
        log_ms_col = sb("log_ms_col", [P, 2])
        rstd_col = sb("rstd_col", [P, 2])
        sumsq = sb("sumsq", [P, TOK])
        square = sb("square", [P, 2, TOK])
        log_ms = sb("log_ms", [P, TOK])
        rstd = sb("rstd", [P, TOK])
        unit_max = sb("unit_max", [P, 4, 2])
        unit_bias = sb("unit_bias", [P, 4, 2])
        unit_sum = sb("unit_sum", [P, 4, 2])
        unit_rcp = sb("unit_rcp", [P, 4, 2])

        with ExitStack() as mlp:
            def mlp_sb(name, shape, dt=f32):
                return mlp.enter_context(nc.sbuf_tensor(name, shape, dt))

            a_hi = mlp_sb("a_hi", [P, D_FF // P, TOK], f32r)
            a_lo = mlp_sb("a_lo", [P, D_FF // P, TOK], f32r)
            c_buf2 = mlp_sb("conv_buf", [P, 4, TOK])
            prod = mlp_sb("prod", [P, 2, TOK])
        u_buf = H[:, 0:4, :]
        m_buf = H[:, 4:6, :]
        gate = H[:, 6:8, :]
        Z = sb("Z", [P, 16, TOK])
        ROT = sb("ROT", [P, 4, TOK])
        o_hi = sb("o_hi", [P, KT, TOK], f32r)
        o_lo = sb("o_lo", [P, KT, TOK], f32r)
        v_tok = sb("v_tok", [P, 2, D])
        s_buf = sb("s_buf", [P, 2, 2 * TOK])
        n_buf = sb("n_buf", [P, 2, 2 * TOK])
        c_buf = sb("c_buf", [P, 2, 2 * TOK])
        p_buf = sb("p_buf", [P, 3, 2 * TOK])
        sub_rms = n_buf[:, :, 0:TOK]
        pt_buf = sb("pt_buf", [P, 2, 2 * TOK])
        f_x = sb("f_x", [P, TOK])
        f_n = sb("f_n", [P, TOK])
        f_p = sb("f_p", [P, TOK])
        f_sum = sb("f_sum", [P, TOK])
        neg_fcum8 = sb("neg_fcum8", [P, TOK])

        bank = [ctx.enter_context(nc.psum_tensor(f"bank{b}", [P, 2 * TOK], f32)) for b in range(8)]

        consts_in = sem("consts_in")
        x_in = sem("x_in")
        mem_in = sem("mem_in")
        raw_in = [sem(f"raw_in{s}") for s in range(RING)]
        hi_ready = sem("hi_ready")
        lo_ready = sem("lo_ready")
        units_done = sem("units_done")
        tile_out = sem("tile_out")
        sq_done = sem("sq_done")
        sum_done = sem("sum_done")
        ms_done = sem("ms_done")
        rstd_ready = sem("rstd_ready")
        col_ready = sem("col_ready")
        h_hi = sem("h_hi")
        h_lo = sem("h_lo")
        y_even = sem("y_even")
        y_odd = sem("y_odd")
        x_changed = sem("x_changed")
        dve_step = sem("dve_step")
        act_step = sem("act_step")
        pool_step = sem("pool_step")
        rot_in = [sem(f"rot_in{b}") for b in range(2)]
        roped = sem("roped")
        vt_done = sem("vt_done")
        vt_out = sem("vt_out")
        v_out = sem("v_out")
        s_done = sem("s_done")
        s_out = sem("s_out")
        exp_done = sem("exp_done")
        arg_ready = sem("arg_ready")
        p_ready = sem("p_ready")
        t_done = sem("t_done")
        t_out = sem("t_out")
        o_done = sem("o_done")
        o_hi_out = sem("o_hi_out")
        o_out = sem("o_out")
        gelu_ready = sem("gelu_ready")
        tap2_ready = sem("tap2_ready")
        tap1_ready = sem("tap1_ready")
        m_ready = sem("m_ready")
        taps_done = sem("taps_done")
        prod_ready = sem("prod_ready")
        a_hi_ready = sem("a_hi_ready")
        a_ready = sem("a_ready")
        lam_ready = sem("lam_ready")
        sub_copied = sem("sub_copied")
        sub_out = sem("sub_out")
        sub_ms = sem("sub_ms")
        sub_rstd = sem("sub_rstd")
        sub_scaled = sem("sub_scaled")
        sub_hi = sem("sub_hi")
        sub_lo = sem("sub_lo")
        wf_in = sem("wf_in")
        wf_split = sem("wf_split")
        f_logits = sem("f_logits")
        f_abs = sem("f_abs")
        f_log = sem("f_log")
        f_ready = sem("f_ready")
        out_done = sem("out_done")

        block = ctx.enter_context(nc.Block())

        OPERANDS = {"mem_a": (0, 1), "mem_b": (8, 1), "in_a": (16, 1), "up_a": (24, 1), "in_b": (32, 2),
                    "q_b": (33, 2), "up_b": (48, 1), "in_sb": (56, 1), "up_sb": (64, 1), "in_fox": (72, 2),
                    "q_fox": (73, 2), "up_fox": (88, 1)}
        GAIN_OF = {"mem_a": "a_mem_norm", "mem_b": "b_mem_norm", "in_a": "a_norm_attn", "up_a": "a_norm_mlp",
                   "q_b": "b_norm_attn", "in_b": "kv_norm", "up_b": "b_norm_mlp", "in_sb": "sb_pre_g_2",
                   "up_sb": "ffn_pre_g_2.0", "in_fox": "kv_norm_g_2", "q_fox": "fox_pre_g_2",
                   "up_fox": "ffn_pre_g_2.1"}
        NORMS = {n: i for i, n in enumerate(
            ["mem_a", "in_a", "up_a", "in_b", "up_b", "final", "in_sb", "post_sb", "up_sb", "post_ffn_sb",
             "in_fox", "post_fox", "up_fox", "post_ffn_fox"])}
        MS_AFTER = {"mem_a": 2, "in_a": 2, "up_a": 1, "in_b": 2, "up_b": 1, "in_sb": 2, "up_sb": 2, "in_fox": 2,
                    "up_fox": 2}
        VALUE_PIECES = 4
        ROPE_PAIRS = SELF_W // P

        def gain(name, k):
            return gains[:, GAINS.index(name), bass.ds(k, 1)]

        def operand_count(name, i, per, k):
            first, step = OPERANDS[name]
            return i * (per * step) + (first + step * k + 1)

        PRODUCTS = {"up_a": 0, "up_b": D_FF // P, "up_sb": 2 * D_FF // P, "up_fox": 2 * D_FF // P + D_FF2 // P}
        DOWN_OF = {"down_a": "up_a", "down_b": "up_b", "down_sb": "up_sb", "down_fox": "up_fox"}
        FIRST_TAP = {"up_sb": 0, "up_fox": 2 * D_FF2 // P}
        by_n = {u["n"]: u for units in heads.values() for u in units}
        DIFF_TILES = 6
        CONSTS = [(ones, "ones"), (ident, "ident"), (rope_c, "rope_c"), (rope_s, "rope_s"),
                  (mask_in, "mask_in"), (mask_ex, "mask_ex"), (subln, "subln"),
                  (conv, "conv"), (lam_in, "lam"), (b_f, "b_f")]

        def geometry(u):
            w0 = TOK if u["mem"] else P
            return w0, w0 + TOK

        def output_feature_tile(u):
            return u["j"] + (SELF_W // P if u["mem"] else 0)

        def attention_units(name):
            return [u for kind in FUSED[name] for u in heads[kind]]

        by_tile = {u["tile"]: u for u in by_n.values()}

        def left_bank(tile):
            u = by_tile[tile]
            return (sub_out, u["j"] + 1) if u["diff"] else (o_out, u["plain"] + 1)

        def values_before(name):
            return VALUE_PIECES * list(FUSED).index(name)

        def fused(name, tile, step, lags):
            tiles, units = plan[name]["tiles"] - plan[name]["values"], attention_units(name)
            for s in range(LAG[name] + len(units) + lags):
                if s < tiles:
                    tile(s)
                if s >= LAG[name]:
                    step(s - LAG[name])

        @block.sync
        def _(sp):
            sp.dma_start(gains[:], ins["gains"]).then_inc(mem_in, 16)
            sp.dma_start(ZM[:], ins["mem"]).then_inc(mem_in, 16)

            def load(g, f, part, free, slot):
                at, k = sum(g["ks"][:part]), g["ks"][part]
                if free is not None:
                    sp.wait_ge(lo_ready, free)
                sp.dma_start(raw[:, slot, 0:k * P],
                             ins["w_" + g["name"]][f, :, at * P:(at + k) * P]).then_inc(raw_in[slot], 16)

            for name in order:
                g = plan[name]
                nk, body = len(g["ks"]), g["body"]
                if g["trips"] == 1:
                    for s in range(body):
                        load(g, s, 0, g["unit"] + s - RING + 1 if g["unit"] else None, s % RING)
                    if name == "mem_a":
                        sp.dma_start(X[:], ins["x"]).then_inc(x_in, 16)
                        for dst, const in CONSTS:
                            sp.dma_start(dst[:], ins[const]).then_inc(consts_in, 16)
                        sp.dma_start(H[:, 0:KT // 2, :].rearrange("p a (b c) -> p (a b) c", c=P),
                                     ins["w_f"]).then_inc(wf_in, 16)
                else:
                    with sp.Fori(0, g["trips"]) as i:
                        for s in range(body * nk):
                            load(g, i * body + s // nk, s % nk, i * (body * nk) + (g["unit"] + s - RING + 1),
                                 s % RING)
            sp.wait_ge(x_changed, 5 * KT)
            sp.dma_start(out, X[:]).then_inc(out_done, 16)
            sp.wait_ge(out_done, 16)

        @block.tensor
        def _(pe):
            n_ms, n_vt = [0], [0]

            def values(name):
                g = plan[name]
                pe.wait_ge(tile_out, g["tile"])
                for s, (group, _, width, k_tiles) in enumerate(value_units(name)):
                    pe.wait_ge(lo_ready, g["unit"] + s + 1)
                    slot = (g["unit"] + s) % RING
                    for at, k in enumerate(k_tiles):
                        if group == 0:
                            pe.wait_ge(h_lo, operand_count(name, 0, 0, k))
                        w = slice(at * width, (at + 1) * width)
                        for tt in range(2):
                            dst, tokens = bank[2 * group + tt][:, 0:width], slice(tt * P, (tt + 1) * P)
                            nc.tensor.matmul(dst, h1_hi[:, k, tokens], w_hi[:, slot, w], start=k == 0, stop=False)
                            nc.tensor.matmul(dst, h1_hi[:, k, tokens], w_lo[:, slot, w], start=False, stop=False)
                            last = nc.tensor.matmul(dst, h1_lo[:, k, tokens], w_hi[:, slot, w], start=False,
                                                    stop=k == KT - 1)
                    last.then_inc(units_done, 1)
                    if s == MS_AFTER[name]:
                        mean_square(columns=True)

            def query_key_tile(name, s, src_hi, src_lo):
                g = plan[name]
                unit = g["unit"] + g["values"] + s
                pe.wait_ge(lo_ready, unit + 1)
                if s < 2:
                    pe.wait_ge(v_out, values_before(name) + 2)
                else:
                    pe.wait_ge(tile_out, g["tile"] + s - 1)
                for k in range(KT):
                    w = slice(k * P, (k + 1) * P)
                    dst, slot = bank[s % 2][:, 0:TOK], unit % RING
                    nc.tensor.matmul(dst, w_hi[:, slot, w], src_hi[:, k, :], start=k == 0, stop=False)
                    nc.tensor.matmul(dst, w_hi[:, slot, w], src_lo[:, k, :], start=False, stop=False)
                    last = nc.tensor.matmul(dst, w_lo[:, slot, w], src_hi[:, k, :], start=False, stop=k == KT - 1)
                last.then_inc(units_done, 1)

            def gemm(name, src_hi, src_lo, operand_tile=None):
                g = plan[name]
                nk, body = len(g["ks"]), g["body"]
                banks = RING if nk == 1 else 2

                def trip(i, first=False):
                    for s in range(body * nk):
                        part, b = s % nk, s // nk % banks
                        pe.wait_ge(lo_ready, i * (body * nk) + (g["unit"] + s + 1))
                        if part == 0 and g["tile"]:
                            pe.wait_ge(tile_out, i * body + (g["tile"] + s // nk - banks + 1))
                        at, slot, k_tiles = sum(g["ks"][:part]), s % RING, g["ks"][part]
                        if name in DOWN_OF:
                            pe.wait_ge(a_ready, RING + PRODUCTS[DOWN_OF[name]] + at + k_tiles)
                        for k in range(k_tiles):
                            w = slice(k * P, (k + 1) * P)
                            begin, end = part == 0 and k == 0, part == nk - 1 and k == k_tiles - 1
                            dst = bank[b][:, 0:TOK]
                            if s == 0 and operand_tile is not None:
                                pe.wait_ge(*operand_tile(k))
                            if first and s == 0:
                                pe.wait_ge(h_lo, operand_count(name, 0, 0, k))
                            nc.tensor.matmul(dst, w_hi[:, slot, w], src_hi[:, at + k, :], start=begin, stop=False)
                            nc.tensor.matmul(dst, w_hi[:, slot, w], src_lo[:, at + k, :], start=False, stop=False)
                            last = nc.tensor.matmul(dst, w_lo[:, slot, w], src_hi[:, at + k, :], start=False,
                                                    stop=end)
                        last.then_inc(units_done, 1)
                        if first and s == MS_AFTER.get(name):
                            mean_square()

                peeled = name in OPERANDS
                if peeled or g["trips"] == 1:
                    trip(0, peeled)
                if g["trips"] > 1:
                    with pe.Fori(1 if peeled else 0, g["trips"]) as i:
                        trip(i)

            def mean_square(columns=False):
                pe.wait_ge(sum_done, KT * (n_ms[0] + 1))
                if n_ms[0]:
                    pe.wait_ge(rstd_ready, n_ms[0])
                last = nc.tensor.matmul(bank[7][:, 0:TOK], ones[:, 0:P], sumsq[:], start=True, stop=True)
                for tt in range(2 if columns else 0):
                    last = nc.tensor.matmul(bank[7][:, TOK + tt:TOK + tt + 1], sumsq[:, tt * P:(tt + 1) * P],
                                            ones[:, 0:1], start=True, stop=True)
                last.then_inc(ms_done, 1)
                n_ms[0] += 1

            def transpose_values(src, first, tiles):
                for j in range(first, first + tiles, 2):
                    if n_vt[0]:
                        pe.wait_ge(vt_out, n_vt[0])
                    for tt in range(2):
                        for jj in range(2):
                            last = nc.tensor.transpose(bank[6][:, tt * TOK + jj * P:tt * TOK + (jj + 1) * P],
                                                       src[:, j + jj, tt * P:(tt + 1) * P], ident[:])
                    last.then_inc(vt_done, 1)
                    n_vt[0] += 1

            def attention(name):
                units = attention_units(name)
                layer = list(FUSED).index(name)
                rope = "mem_" in FUSED[name][0]

                def operands(u):
                    j = u["j"]
                    if u["mem"]:
                        return (Z[:, j, :], ZM[:, 4 * layer + j, :], mv_tok[:, layer],
                                (tile_out, plan[name]["tile"] + j + 1))
                    if rope:
                        return (Z[:, 2 + 2 * j, :], Z[:, 3 + 2 * j, :], v_tok,
                                (roped, ROPE_PAIRS * layer + j + 1))
                    return Z[:, 2 * j, :], Z[:, 2 * j + 1, :], v_tok, (tile_out, plan[name]["tile"] + 2 * j + 2)

                def scores(u):
                    w0, _ = geometry(u)
                    q, k, _, ready = operands(u)
                    pe.wait_ge(*ready)
                    rows = slice(HEAD * u["half"], HEAD * (u["half"] + 1))
                    if u["n"] >= 2:
                        pe.wait_ge(s_out, u["n"] - 1)
                    forget = u["kind"] == "forget"
                    if forget:
                        pe.wait_ge(f_ready, 1)
                    for qt in range(2):
                        width = w0 if qt == 0 else TOK
                        dst = bank[4 + u["n"] % 2][:, qt * w0:qt * w0 + width]
                        last = nc.tensor.matmul(dst, q[rows, qt * P:(qt + 1) * P], k[rows, 0:width], start=True,
                                                stop=not forget)
                        if forget:
                            c = HEAD * u["half"] + 2 * u["j"] + u["half"]
                            last = nc.tensor.matmul(dst, ident[rows, c:c + 1].broadcast_to([HEAD, P]),
                                                    neg_fcum8[rows, 0:width], start=False, stop=True)
                    last.then_inc(s_done, 1)

                def transposes(u):
                    if not u["emits"]:
                        return
                    w0, _ = geometry(u)
                    pe.wait_ge(p_ready, u["n"] + 1)
                    pe.wait_ge(vt_out, n_vt[0])
                    if u["t"]:
                        pe.wait_ge(t_out, u["t"])
                    pieces = [(0, 0), (P, w0)] + ([(TOK, P), (TOK + P, TOK + P)] if u["mem"] else [(TOK, TOK)])
                    for dst, src in pieces:
                        last = nc.tensor.transpose(bank[6][:, dst:dst + P], p_buf[:, u["n"] % 3, src:src + P],
                                                   ident[:])
                    last.then_inc(t_done, 1)

                def outputs(u):
                    if not u["emits"]:
                        return
                    pe.wait_ge(t_out, u["t"] + 1)
                    diff, mem, v = u["diff"], u["mem"], operands(u)[2]
                    if u["n"] == units[0]["n"]:
                        pe.wait_ge(v_out, values_before(name) + VALUE_PIECES)
                    if (diff or u["half"] == 0) and u["tile"] >= 2:
                        pe.wait_ge(*left_bank(u["tile"] - 2))
                    rows = slice(0, P) if diff else slice(HEAD * u["half"], HEAD * (u["half"] + 1))
                    cols = slice(u["j"] * P + rows.start, u["j"] * P + rows.stop)
                    dst, pt = bank[(7, 3)[u["tile"] % 2]], pt_buf[:, u["t"] % 2, :]
                    nc.tensor.matmul(dst[rows, 0:TOK], v[:, 0, cols], pt[:, 0:TOK], start=True, stop=False)
                    last = nc.tensor.matmul(dst[rows, (0 if mem else P):TOK], v[:, 1, cols],
                                            pt[:, TOK:(2 * TOK if mem else TOK + P)], start=False, stop=True)
                    last.then_inc(o_done, 1)

                def sub_square(u):
                    j = u["j"]
                    if not (u["diff"] and u["half"]):
                        return
                    pe.wait_ge(sub_out, j + 1)
                    if j:
                        pe.wait_ge(sub_rstd, j)
                    nc.tensor.matmul(bank[2][:, j % 2 * TOK:(j % 2 + 1) * TOK], ones[:, 0:P], square[:, j % 2, :],
                                     start=True, stop=True).then_inc(sub_ms, 1)

                def step(i):
                    if i < len(units):
                        scores(units[i])
                    if 0 <= i - 2 < len(units):
                        transposes(units[i - 2])
                    if 0 <= i - 3 < len(units):
                        outputs(units[i - 3])
                    if 0 <= i - 4 < len(units):
                        sub_square(units[i - 4])
                return step

            def attended(name):
                by_feature = {output_feature_tile(u): u for u in attention_units(name)}

                def wait(k):
                    u = by_feature[k]
                    return (sub_lo, u["j"] + 1) if u["diff"] else (o_out, u["plain"] + 1)
                return wait

            pe.wait_ge(consts_in, 16 * len(CONSTS))
            gemm("mem_a", h2_hi, h2_lo)
            gemm("mem_b", a_hi, a_lo)
            values("in_a")
            transpose_values(ZM, 2, 2)
            transpose_values(ZM, 6, 2)
            fused("in_a", lambda s: query_key_tile("in_a", s, h1_hi, h1_lo), attention("in_a"), 4)
            gemm("out_a", o_hi, o_lo, attended("in_a"))
            gemm("up_a", h2_hi, h2_lo)
            gemm("down_a", a_hi, a_lo)
            values("in_b")
            pe.wait_ge(h_lo, operand_count("q_b", 0, 0, KT - 1))
            fused("in_b", lambda s: query_key_tile("in_b", s, *((h1_hi, h1_lo) if s > 2 and s % 2
                                                                else (h2_hi, h2_lo))), attention("in_b"), 3)
            gemm("out_b", o_hi, o_lo, attended("in_b"))
            gemm("up_b", h2_hi, h2_lo)
            gemm("down_b", a_hi, a_lo)
            mean_square()
            values("in_sb")
            fused("in_sb", lambda s: query_key_tile("in_sb", s, h1_hi, h1_lo), attention("in_sb"), 3)
            gemm("out_sb", o_hi, o_lo, attended("in_sb"))
            mean_square()
            gemm("up_sb", h2_hi, h2_lo)
            gemm("down_sb", a_hi, a_lo)
            mean_square()
            values("in_fox")
            pe.wait_ge(wf_split, 2)
            for k in range(KT):
                dst = bank[6][:, 0:TOK]
                nc.tensor.matmul(dst, wf_hi[:, k, :], h1_hi[:, k, :], start=k == 0, stop=False)
                nc.tensor.matmul(dst, wf_hi[:, k, :], h1_lo[:, k, :], start=False, stop=False)
                last = nc.tensor.matmul(dst, wf_lo[:, k, :], h1_hi[:, k, :], start=False, stop=k == KT - 1)
            last.then_inc(f_logits, 1)
            pe.wait_ge(h_lo, operand_count("q_fox", 0, 0, KT - 1))
            fused("in_fox", lambda s: query_key_tile("in_fox", s, *((h1_hi, h1_lo) if s % 2 else (h2_hi, h2_lo))),
                  attention("in_fox"), 3)
            gemm("out_fox", o_hi, o_lo, attended("in_fox"))
            mean_square()
            gemm("up_fox", h2_hi, h2_lo)
            gemm("down_fox", a_hi, a_lo)
            mean_square()

        def run_projection(eng, name, lead, split, before=None, after=None, middle=None, peel=False):
            g = plan[name]
            nk, body = len(g["ks"]), g["body"]
            per = body * nk
            at = order.index(name)
            following = plan[order[at + 1]] if at + 1 < len(order) else None

            def trip(i, first, last):
                held = []
                for s in range(per):
                    ahead = s + lead
                    holds = first and middle is not None and s <= MS_AFTER[name]
                    finished = (i, i * per + (g["unit"] + s + 1), s // nk, first)
                    if before is not None and s % nk == nk - 1:
                        before(*finished)
                    if not last or ahead < per:
                        split(i, per, g["unit"] + ahead, g["ks"][ahead % nk])
                    elif following is not None:
                        split(i, per, g["unit"] + ahead, following["ks"][(ahead - per) % len(following["ks"])])
                    if after is not None and s % nk == nk - 1:
                        held.append(finished)
                    if holds and s == MS_AFTER[name]:
                        middle()
                    if not holds or s == MS_AFTER[name]:
                        for tile in held:
                            after(*tile)
                        held.clear()

            peel = peel or middle is not None
            if peel and g["trips"] > 1:
                trip(0, True, False)
            start = 1 if peel else 0
            if g["trips"] - 1 > start:
                with eng.Fori(start, g["trips"] - 1) as i:
                    trip(i, False, False)
            trip(g["trips"] - 1, g["trips"] == 1, True)

        @block.scalar
        def _(act):
            steps, n_norm, n_vt, n_columns = [0], [0], [0], [0]

            def link(instruction):
                steps[0] += 1
                instruction.then_inc(act_step, 1)
                act.wait_ge(act_step, steps[0])

            def split(i, per_trip, unit, k):
                slot = unit % RING
                act.wait_ge(raw_in[slot], i * (per_trip // RING * 16) + 16 * (unit // RING + 1))
                if unit >= RING:
                    act.wait_ge(units_done, i * per_trip + (unit - RING + 1))
                nc.scalar.copy(w_hi[:, slot, 0:k * P], raw[:, slot, 0:k * P]).then_inc(hi_ready, 1)

            def high(name, src, dst, i, per, k):
                nc.scalar.activation(dst[:, i * per + k, :], src[:, i * per + k, :], ACT.Identity,
                                     scale=gain(GAIN_OF[name], i * per + k)).then_inc(h_hi, 1)

            def squared(norm, src, i, per, k, signal=None):
                n = KT * NORMS[norm] + k
                if n >= 2:
                    act.wait_ge(sum_done, i * per + (n - 1))
                nc.scalar.activation(square[:, k % 2, :], src, ACT.Square).then_inc(sq_done, 1)

            def stream_tile(name, operands, norm):
                per = plan[name]["body"]

                def tile(i, done, b, first):
                    act.wait_ge(tile_out, i * per + (plan[name]["tile"] + b + 1))
                    for operand, dst in operands:
                        high(operand, X, dst, i, per, b)
                    at = i * (per * TOK) + b * TOK
                    squared(norm, X[:].rearrange("p k t -> p (k t)")[:, bass.ds(at, TOK)], i, per, b)
                return tile

            def output_tile(name, norm, g):
                per = plan[name]["body"]

                def tile(i, done, b, first):
                    act.wait_ge(units_done, done)
                    squared(norm, bank[b][:, 0:TOK], i, per, b)
                    nc.scalar.activation(H[:, i * per + b, :], bank[b][:, 0:TOK], ACT.Identity,
                                         scale=gain(g, i * per + b)).then_inc(tile_out, 1)
                return tile

            def relu(name):
                base, first_tile = PRODUCTS[name], plan[name]["tile"]

                def tile(i, done, b, first):
                    act.wait_ge(tile_out, i * 4 + (first_tile + b + 1))
                    nc.scalar.activation(a_hi[:, i * 4 + b, :], u_buf[:, b, :], ACT.Square).then_inc(a_hi_ready, 1)
                return tile

            def conv_high(name, i, b):
                pair = b // 2 - 1
                act.wait_ge(prod_ready, i * 2 + (PRODUCTS[name] + pair + 1))
                nc.scalar.copy(a_hi[:, i * 2 + pair, :], prod[:, pair % 2, :]).then_inc(a_hi_ready, 1)

            def conv_gelu(name):
                base, tap0, first_tile = PRODUCTS[name], FIRST_TAP[name], plan[name]["tile"]
                layer = 0 if name == "up_sb" else 1

                def tile(i, done, b, first):
                    pair = b // 2
                    act.wait_ge(tile_out, i * 4 + (first_tile + b + 1))
                    act.wait_ge(prod_ready, i * 2 + (base + pair - 1))
                    nc.scalar.activation(c_buf2[:, b, :], u_buf[:, b % 2, :], ACT.Identity,
                                         scale=conv[:, layer, 2, bass.ds(i * 4 + b, 1)],
                                         bias=conv[:, layer, 3, bass.ds(i * 4 + b, 1)]).then_inc(tap2_ready, 1)
                    if b % 2:
                        act.wait_ge(taps_done, i * 4 + (tap0 + b))
                        nc.scalar.activation(gate[:, pair, :], c_buf2[:, b - 1, :],
                                             ACT.Gelu_apprx_tanh).then_inc(gelu_ready, 1)
                    elif not (first and b == 0):
                        conv_high(name, i, b)
                return tile

            def project(name, before=None, after=None, middle=None, peel=False):
                run_projection(act, name, RING, split, before, after, middle, peel)

            def norm_scale(columns=False):
                act.wait_ge(ms_done, n_norm[0] + 1)
                if n_norm[0] == NORMS["in_a"]:
                    act.wait_ge(tile_out, plan["in_a"]["tile"])
                if columns:
                    act.wait_ge(v_out, VALUE_PIECES * n_columns[0])
                    n_columns[0] += 1
                    link(nc.scalar.activation(log_ms_col[:], bank[7][:, TOK:TOK + 2], ACT.Ln, scale=1.0 / D,
                                              bias=eps_col[:]))
                    nc.scalar.activation(rstd_col[:], log_ms_col[:], ACT.Exp, scale=-0.5).then_inc(col_ready, 1)
                link(nc.scalar.activation(log_ms[:], bank[7][:, 0:TOK], ACT.Ln, scale=1.0 / D, bias=eps_col[:]))
                nc.scalar.activation(rstd[:], log_ms[:], ACT.Exp, scale=-0.5).then_inc(rstd_ready, 1)
                n_norm[0] += 1

            def conv_scale():
                norm_scale()
                nc.scalar.preload_act_table(ACT.Gelu_apprx_tanh)

            def after_change(count, operands, norm):
                for k in range(KT):
                    act.wait_ge(x_changed, count + k + 1)
                    for operand, dst in operands:
                        high(operand, X, dst, 0, 0, k)
                for k in range(KT):
                    squared(norm, X[:, k, :], 0, 0, k)

            def rotate(name, j):
                pair = ROPE_PAIRS * list(FUSED).index(name) + j
                act.wait_ge(tile_out, plan[name]["tile"] + 2 * j + 4)
                if pair >= 2:
                    act.wait_ge(roped, pair - 1)
                at = 2 * (pair % 2)
                for piece in range(4):
                    src, dst = 32 * (piece ^ 1), 32 * piece
                    act.dma_start(ROT[dst:dst + 32, at:at + 2, :],
                                  Z[src:src + 32, 2 + 2 * j:4 + 2 * j, :]).then_inc(rot_in[pair % 2], 16)

            def values(name, middle=None):
                g = plan[name]
                units = value_units(name)
                for s, (group, first, width, k_tiles) in enumerate(units):
                    split(0, RING, g["unit"] + s + RING, KT)
                    if s == MS_AFTER[name]:
                        norm_scale(columns=True)
                    if k_tiles.stop == KT:
                        act.wait_ge(units_done, g["unit"] + s + 1)
                        act.wait_ge(col_ready, n_columns[0])
                        for tt in range(2):
                            nc.scalar.activation(v_tok[:, tt, first:first + width],
                                                 bank[2 * group + tt][:, 0:width], ACT.Identity,
                                                 scale=rstd_col[:, tt:tt + 1]).then_inc(v_out, 1)

            def query_key_tile(name, s):
                g = plan[name]
                split(0, RING, g["unit"] + g["values"] + s + RING, KT)

            def copy_values(dst, first, tiles):
                for j in range(0, tiles, 2):
                    act.wait_ge(vt_done, n_vt[0] + 1)
                    nc.scalar.copy(dst[:, :, (first + j) * P:(first + j + 2) * P],
                                   bank[6][:].rearrange("p (t c) -> p t c", t=2)).then_inc(vt_out, 1)
                    n_vt[0] += 1

            def attention(name):
                units = attention_units(name)
                stick = name == "in_sb"

                def exps(u):
                    n = u["n"]
                    w0, whole = geometry(u)
                    act.wait_ge(s_out, n + 1)
                    if stick:
                        nb = n_buf[:, n % 2, 0:whole]
                        link(nc.scalar.activation(nb, nb, ACT.Exp))
                        nc.scalar.activation(nb, nb, ACT.Ln, bias=1.0).then_inc(exp_done, 1)
                        return
                    free_probabilities(n)
                    for qt in range(2):
                        cols = slice(0, w0) if qt == 0 else slice(w0, whole)
                        last = nc.scalar.activation(p_buf[:, n % 3, cols], s_buf[:, n % 2, cols], ACT.Exp,
                                                    bias=unit_bias[:, n % 4, qt:qt + 1], scale=SCALE,
                                                    accum_out=unit_sum[:, n % 4, qt:qt + 1])
                    last.then_inc(exp_done, 1)

                def free_probabilities(n):
                    if n >= 3:
                        old = by_n[n - 3]
                        if old["emits"]:
                            act.wait_ge(t_done, old["t"] + 1)
                        else:
                            act.wait_ge(p_ready, n - 1)

                def weights(u):
                    n = u["n"]
                    _, whole = geometry(u)
                    act.wait_ge(arg_ready, n - units[0]["n"] + 1)
                    free_probabilities(n)
                    nc.scalar.activation(p_buf[:, n % 3, 0:whole], c_buf[:, n % 2, 0:whole],
                                         ACT.Exp).then_inc(p_ready, 1)

                def copies(u):
                    _, whole = geometry(u)
                    act.wait_ge(t_done, u["t"] + 1)
                    if u["t"] >= 2:
                        act.wait_ge(o_done, u["t"] - 1)
                    nc.scalar.copy(pt_buf[:, u["t"] % 2, 0:whole], bank[6][:, 0:whole]).then_inc(t_out, 1)

                def out_hi(u):
                    j = u["j"]
                    act.wait_ge(o_done, u["t"] + 1)
                    src = bank[(7, 3)[u["tile"] % 2]][:, 0:TOK]
                    if u["diff"]:
                        nc.scalar.copy(H[:, j, :], src).then_inc(sub_copied, 1)
                        if j >= 2:
                            act.wait_ge(sub_ms, j - 1)
                        nc.scalar.activation(square[:, j % 2, :], src, ACT.Square).then_inc(sub_out, 1)
                    else:
                        nc.scalar.copy(o_hi[:, output_feature_tile(u), :], src).then_inc(o_hi_out, 1)

                def sub_scale(u):
                    j = u["j"]
                    act.wait_ge(sub_ms, j + 1)
                    if j:
                        act.wait_ge(sub_rstd, j)
                    link(nc.scalar.activation(log_ms[:], bank[2][:, j % 2 * TOK:(j % 2 + 1) * TOK], ACT.Ln,
                                              scale=1.0 / (2 * HEAD), bias=eps_col[:]))
                    if j >= 2:
                        act.wait_ge(sub_scaled, j - 1)
                    nc.scalar.activation(sub_rms[:, j % 2, :], log_ms[:], ACT.Exp, scale=-0.5).then_inc(sub_rstd, 1)

                def sub_high(u):
                    j = u["j"]
                    act.wait_ge(sub_scaled, j + 1)
                    nc.scalar.copy(o_hi[:, j, :], H[:, j, :]).then_inc(sub_hi, 1)

                def step(i):
                    if i < len(units):
                        exps(units[i])
                    if stick and 0 <= i - 1 < len(units):
                        weights(units[i - 1])
                    if 0 <= i - 2 < len(units) and units[i - 2]["emits"]:
                        copies(units[i - 2])
                    if 0 <= i - 3 < len(units) and units[i - 3]["half"]:
                        out_hi(units[i - 3])
                    if 0 <= i - 5 < len(units) and units[i - 5]["diff"] and units[i - 5]["half"]:
                        sub_scale(units[i - 5])
                    if 0 <= i - 6 < len(units) and units[i - 6]["diff"] and units[i - 6]["half"]:
                        sub_high(units[i - 6])
                    j, odd = divmod(i + LAG[name] - 3, 2)
                    if "mem_" in FUSED[name][0] and odd == 0 and 0 <= j < ROPE_PAIRS:
                        rotate(name, j)
                return step

            nc.scalar.preload_act_table_set("natural_log_exp_and_others")
            act.wait_ge(mem_in, 32)
            for k in range(KT):
                high("mem_a", ZM, h2_hi, 0, 0, k)
            for u in range(RING):
                split(0, RING, u, KT)
                for k in (2 * u, 2 * u + 1):
                    squared("mem_a", ZM[:, k, :], 0, 0, k)
            for k in range(KT):
                high("mem_b", ZM, a_hi, 0, 0, k)
            act.wait_ge(a_ready, RING)
            project("mem_a", middle=norm_scale)
            act.wait_ge(x_in, 16)
            for k in range(KT):
                high("in_a", X, h1_hi, 0, 0, k)
            project("mem_b")
            for k in range(KT):
                squared("in_a", X[:, k, :], 0, 0, k)
            values("in_a")
            copy_values(mv_tok[:, 0], 0, 2)
            copy_values(mv_tok[:, 1], 0, 2)
            act.wait_ge(lam_ready, 1)
            nc.scalar.activation(lam_exp[:], lam_sum[:], ACT.Exp).then_inc(lam_ready, 1)
            act.wait_ge(wf_in, 16)
            nc.scalar.copy(wf_hi[:], H[:, 0:KT // 2, :].rearrange("p a (b c) -> p (a b) c", c=P)).then_inc(wf_split, 1)
            fused("in_a", lambda s: query_key_tile("in_a", s), attention("in_a"), 6)
            project("out_a", before=stream_tile("out_a", [("up_a", h2_hi)], "up_a"))
            project("up_a", after=relu("up_a"), middle=norm_scale)
            project("down_a", before=stream_tile("down_a", [("in_b", h1_hi), ("q_b", h2_hi)], "in_b"))
            values("in_b")
            fused("in_b", lambda s: query_key_tile("in_b", s), attention("in_b"), 3)
            project("out_b", before=stream_tile("out_b", [("up_b", h2_hi)], "up_b"))
            project("up_b", after=relu("up_b"), middle=norm_scale)
            project("down_b", before=stream_tile("down_b", [], "final"))
            norm_scale()
            after_change(0, [("in_sb", h1_hi)], "in_sb")
            values("in_sb")
            fused("in_sb", lambda s: query_key_tile("in_sb", s), attention("in_sb"), 3)
            project("out_sb", before=output_tile("out_sb", "post_sb", "sb_post_g_2"))
            norm_scale()
            after_change(KT, [("up_sb", h2_hi)], "up_sb")
            project("up_sb", after=conv_gelu("up_sb"), middle=conv_scale)
            conv_high("up_sb", plan["up_sb"]["trips"], 0)
            project("down_sb", before=output_tile("down_sb", "post_ffn_sb", "ffn_post_g_2.0"))
            norm_scale()
            after_change(2 * KT, [("in_fox", h1_hi), ("q_fox", h2_hi)], "in_fox")
            values("in_fox")
            act.wait_ge(f_abs, 1)
            link(nc.scalar.activation(f_n[:], f_n[:], ACT.Exp))
            nc.scalar.activation(f_n[:], f_n[:], ACT.Ln, bias=1.0).then_inc(f_log, 1)
            fused("in_fox", lambda s: query_key_tile("in_fox", s), attention("in_fox"), 3)
            project("out_fox", before=output_tile("out_fox", "post_fox", "fox_post_g_2"))
            norm_scale()
            after_change(3 * KT, [("up_fox", h2_hi)], "up_fox")
            project("up_fox", after=conv_gelu("up_fox"), middle=conv_scale)
            conv_high("up_fox", plan["up_fox"]["trips"], 0)
            project("down_fox", before=output_tile("down_fox", "post_ffn_fox", "ffn_post_g_2.1"))
            norm_scale()

        @block.vector
        def _(dve):
            steps, n_x = [0], [0]

            def link(instruction):
                steps[0] += 1
                instruction.then_inc(dve_step, 1)
                dve.wait_ge(dve_step, steps[0])

            def split(i, per_trip, unit, k):
                slot = unit % RING
                dve.wait_ge(hi_ready, i * per_trip + (unit + 1))
                nc.vector.tensor_tensor(w_lo[:, slot, 0:k * P], raw[:, slot, 0:k * P],
                                        w_hi[:, slot, 0:k * P].bitcast(f32), ALU.subtract).then_inc(lo_ready, 1)

            def query_key_tile(name, s):
                g = plan[name]
                unit = g["unit"] + g["values"] + s
                dve.wait_ge(units_done, unit + 1)
                dve.wait_ge(rstd_ready, NORMS[name] + 1)
                nc.vector.tensor_tensor(Z[:, s, :], bank[s % 2][:, 0:TOK], rstd[:], ALU.mult).then_inc(tile_out, 1)
                split(0, RING, unit + RING - 1, KT)

            def values(name):
                g = plan[name]
                for s in range(g["values"]):
                    split(0, RING, g["unit"] + s + RING - 1, KT)

            def take(name, norm, dst, shift=0):
                per = plan[name]["body"]

                def tile(i, done, b, first):
                    dve.wait_ge(units_done, done)
                    dve.wait_ge(rstd_ready, NORMS[norm] + 1)
                    nc.vector.tensor_tensor(dst[:, i * per + (shift + b), :], bank[b][:, 0:TOK], rstd[:],
                                            ALU.mult).then_inc(tile_out, 1)
                return tile

            def low(name, src, dst_hi, dst_lo, i, per, k):
                at = i * per + k
                dve.wait_ge(h_hi, operand_count(name, i, per, k))
                nc.vector.scalar_tensor_tensor(dst_lo[:, at, :], src[:, at, :], gain(GAIN_OF[name], at),
                                               dst_hi[:, at, :].bitcast(f32), ALU.mult,
                                               ALU.subtract).then_inc(h_lo, 1)

            def residual(name, operands):
                per = plan[name]["body"]

                def tile(i, done, b, first):
                    dve.wait_ge(units_done, done)
                    x = X[:, i * per + b, :]
                    nc.vector.tensor_tensor(x, bank[b][:, 0:TOK], x, ALU.add).then_inc(tile_out, 1)
                    for operand, hi, lo in operands:
                        low(operand, X, hi, lo, i, per, b)
                return tile

            def split_product(i, per, m, slot, dst):
                dve.wait_ge(prod_ready, i * per + (m + 1))
                dve.wait_ge(a_hi_ready, i * per + (m + 1))
                nc.vector.tensor_tensor(a_lo[:, dst, :], prod[:, slot, :], a_hi[:, dst, :].bitcast(f32),
                                        ALU.subtract).then_inc(a_ready, 1)

            def relu(name):
                base = PRODUCTS[name]

                def before(i, done, b, first):
                    dve.wait_ge(units_done, done)
                    dve.wait_ge(rstd_ready, NORMS[name] + 1)
                    dve.wait_ge(a_ready, i * 4 + (base + b + 1))
                    nc.vector.scalar_tensor_tensor(u_buf[:, b, :], bank[b][:, 0:TOK], 0.0, rstd[:], ALU.max,
                                                   ALU.mult).then_inc(tile_out, 1)

                def after(i, done, b, first):
                    split_product(i, 4, base + b, b % 2, i * 4 + b)
                return before, after

            def conv_low(name, i, b):
                pair = b // 2 - 1
                split_product(i, 2, PRODUCTS[name] + pair, pair % 2, i * 2 + pair)

            def conv_taps(name):
                tap0, first_tile = FIRST_TAP[name], plan[name]["tile"]
                layer = 0 if name == "up_sb" else 1

                def before(i, done, b, first):
                    dve.wait_ge(units_done, done)
                    dve.wait_ge(rstd_ready, NORMS[name] + 1)
                    if not first or b >= 2:
                        dve.wait_ge(m_ready, i * 4 + (tap0 + b - 1))
                        dve.wait_ge(tap1_ready, i * 4 + (tap0 + b - 1))
                    nc.vector.tensor_tensor(u_buf[:, b % 2, :], bank[b][:, 0:TOK], rstd[:],
                                            ALU.mult).then_inc(tile_out, 1)

                def after(i, done, b, first):
                    dve.wait_ge(tap2_ready, i * 4 + (tap0 + b + 1))
                    dve.wait_ge(tile_out, i * 4 + (first_tile + b + 1))
                    nc.vector.scalar_tensor_tensor(c_buf2[:, b, 1:TOK], u_buf[:, b % 2, 0:TOK - 1],
                                                   conv[:, layer, 1, bass.ds(i * 4 + b, 1)],
                                                   c_buf2[:, b, 1:TOK], ALU.mult, ALU.add).then_inc(tap1_ready, 1)
                    if b % 2 == 0 and not (first and b == 0):
                        conv_low(name, i, b)
                return before, after

            def project(name, before=None, after=None, peel=False):
                run_projection(dve, name, RING - 1, split, before, after, None, peel)

            def rstd_next(norm):
                dve.wait_ge(rstd_ready, NORMS[norm] + 1)

            def add_normed(norm, operands):
                rstd_next(norm)
                a = n_x[0]

                def lows(k):
                    for operand, hi, lo in operands:
                        low(operand, X, hi, lo, 0, 0, k)

                for k in range(KT):
                    if k % 2 == 0:
                        nc.vector.tensor_tensor(H[:, k, :], H[:, k, :], rstd[:], ALU.mult).then_inc(y_even, 1)
                        dve.wait_ge(y_even, (a - KT + k) // 2 + 1)
                    else:
                        dve.wait_ge(y_odd, (a - KT + k) // 2 + 1)
                    nc.vector.tensor_tensor(X[:, k, :], X[:, k, :], H[:, k, :], ALU.add).then_inc(x_changed, 1)
                    if k:
                        lows(k - 1)
                lows(KT - 1)
                n_x[0] += KT

            def attention(name):
                units = attention_units(name)
                stick = name == "in_sb"
                no_mask = mask_in[:, P:2 * P].unsqueeze(1).broadcast_to([P, 2, P])

                def query_tiles(u):
                    w0, whole = geometry(u)
                    return slice(0, w0), slice(w0, whole)

                def masked(u):
                    n, mem = u["n"], u["mem"]
                    _, whole = geometry(u)

                    def pieces(ap):
                        return ap.rearrange("p (a c) -> p a c", c=P) if mem else ap
                    b = bank[4 + n % 2]
                    dve.wait_ge(s_done, n + 1)
                    if n >= 2:
                        dve.wait_ge(exp_done, n - 1)
                    if stick:
                        if n - units[0]["n"] >= 2:
                            dve.wait_ge(arg_ready, n - units[0]["n"] - 1)
                        z = s_buf[:, n % 2, 0:whole]
                        link(nc.vector.scalar_tensor_tensor(z, b[:, 0:whole], SCALE, mask_ex[:], ALU.mult, ALU.add))
                        nc.vector.scalar_tensor_tensor(n_buf[:, n % 2, 0:whole], z, -1.0, z, ALU.mult,
                                                       ALU.min).then_inc(s_out, 1)
                        return
                    for qt, cols in enumerate(query_tiles(u)):
                        last = nc.vector.tensor_tensor_reduce(
                            out=pieces(s_buf[:, n % 2, cols]), in0=pieces(b[:, cols]), in1=no_mask if mem else mask_in[:, cols],
                            scale=1.0, scalar=-3.0e38, op0=ALU.add, op1=ALU.max,
                            accum_out=unit_max[:, n % 4, qt:qt + 1])
                    link(last)
                    nc.vector.tensor_scalar(unit_bias[:, n % 4, :], unit_max[:, n % 4, :], -SCALE, None,
                                            ALU.mult).then_inc(s_out, 1)

                def normalised(u):
                    n = u["n"]
                    rcp = unit_rcp[:, n % 4, :]
                    dve.wait_ge(exp_done, n + 1)
                    link(nc.vector.reciprocal(rcp, unit_sum[:, n % 4, :]))
                    second = u["diff"] and u["half"]
                    if second:
                        link(nc.vector.tensor_scalar(rcp, rcp, neg_lam[:], None, ALU.mult))
                        dve.wait_ge(p_ready, n)
                    for qt, cols in enumerate(query_tiles(u)):
                        p = p_buf[:, n % 3, cols]
                        if second:
                            last = nc.vector.scalar_tensor_tensor(p, p, rcp[:, qt:qt + 1],
                                                                  p_buf[:, (n - 1) % 3, cols], ALU.mult, ALU.add)
                        else:
                            last = nc.vector.tensor_scalar(p, p, rcp[:, qt:qt + 1], None, ALU.mult)
                    last.then_inc(p_ready, 1)

                def log_weights(u):
                    n = u["n"]
                    _, whole = geometry(u)
                    z, sp, c = s_buf[:, n % 2, 0:whole], n_buf[:, n % 2, 0:whole], c_buf[:, n % 2, 0:whole]
                    dve.wait_ge(exp_done, n + 1)
                    link(nc.vector.scalar_tensor_tensor(sp, z, 0.0, sp, ALU.max, ALU.add))
                    if n - units[0]["n"] >= 2:
                        dve.wait_ge(p_ready, n - 1)
                    for cols in query_tiles(u):
                        last = nc.vector.tensor_tensor_scan(c[:, cols][:, ::-1], ones[:, 0:cols.stop - cols.start],
                                                            sp[:, cols][:, ::-1], 0.0, ALU.mult, ALU.subtract)
                    link(last)
                    nc.vector.tensor_tensor(c, c, z, ALU.add).then_inc(arg_ready, 1)

                def out_lo(u):
                    dve.wait_ge(o_hi_out, u["plain"] + 1)
                    j = output_feature_tile(u)
                    nc.vector.tensor_tensor(o_lo[:, j, :], bank[(7, 3)[u["tile"] % 2]][:, 0:TOK],
                                            o_hi[:, j, :].bitcast(f32), ALU.subtract).then_inc(o_out, 1)

                def sub_scale(u):
                    j = u["j"]
                    dve.wait_ge(sub_rstd, j + 1)
                    nc.vector.scalar_tensor_tensor(H[:, j, :], H[:, j, :], subln_s[:], sub_rms[:, j % 2, :],
                                                   ALU.mult, ALU.mult).then_inc(sub_scaled, 1)

                def sub_low(u):
                    j = u["j"]
                    dve.wait_ge(sub_hi, j + 1)
                    nc.vector.tensor_tensor(o_lo[:, j, :], H[:, j, :], o_hi[:, j, :].bitcast(f32),
                                            ALU.subtract).then_inc(sub_lo, 1)

                def step(i):
                    if i < len(units):
                        masked(units[i])
                    if 0 <= i - 1 < len(units):
                        log_weights(units[i - 1]) if stick else normalised(units[i - 1])
                    if 0 <= i - 4 < len(units) and units[i - 4]["half"] and not units[i - 4]["diff"]:
                        out_lo(units[i - 4])
                    if 0 <= i - 5 < len(units) and units[i - 5]["half"] and units[i - 5]["diff"]:
                        sub_scale(units[i - 5])
                    if 0 <= i - 6 < len(units) and units[i - 6]["half"] and units[i - 6]["diff"]:
                        sub_low(units[i - 6])
                return step

            nc.vector.memset(eps_col[:], EPS).then_inc(a_ready, RING)
            for k in range(KT):
                low("mem_a", ZM, h2_hi, h2_lo, 0, 0, k)
            for u in range(RING - 1):
                split(0, RING, u, KT)
            for k in range(KT):
                low("mem_b", ZM, a_hi, a_lo, 0, 0, k)
            dve.wait_ge(h_lo, 2 * KT)
            project("mem_a", before=take("mem_a", "mem_a", ZM))
            for k in range(KT):
                low("in_a", X, h1_hi, h1_lo, 0, 0, k)
            project("mem_b", before=take("mem_b", "mem_a", ZM, 4))
            values("in_a")
            dve.wait_ge(consts_in, 16 * len(CONSTS))
            nc.vector.tensor_scalar(subln_s[:], subln[:], 1.0 - LAM_INIT, None, ALU.mult)
            for pair in range(2):
                last = nc.vector.tensor_tensor(lam_prod[:, pair, :], lam_in[:, 2 * pair, :],
                                               lam_in[:, 2 * pair + 1, :], ALU.mult)
            link(last)
            nc.vector.tensor_reduce(lam_sum[:], lam_prod[:], AX.X, ALU.add).then_inc(lam_ready, 1)
            dve.wait_ge(lam_ready, 2)
            link(nc.vector.tensor_tensor(neg_lam[:], lam_exp[:, 1:2], lam_exp[:, 0:1], ALU.subtract))
            nc.vector.tensor_scalar(neg_lam[:], neg_lam[:], -LAM_INIT, None, ALU.add).then_inc(lam_ready, 1)
            dve.wait_ge(wf_split, 1)
            nc.vector.tensor_tensor(wf_lo[:], H[:, 0:KT // 2, :].rearrange("p a (b c) -> p (a b) c", c=P),
                                    wf_hi[:].bitcast(f32), ALU.subtract).then_inc(wf_split, 1)
            dve.wait_ge(lam_ready, 3)
            fused("in_a", lambda s: query_key_tile("in_a", s), attention("in_a"), 6)
            project("out_a", before=residual("out_a", [("up_a", h2_hi, h2_lo)]))
            project("up_a", *relu("up_a"))
            project("down_a", before=residual("down_a", [("in_b", h1_hi, h1_lo), ("q_b", h2_hi, h2_lo)]))
            values("in_b")
            fused("in_b", lambda s: query_key_tile("in_b", s), attention("in_b"), 4)
            project("out_b", before=residual("out_b", [("up_b", h2_hi, h2_lo)]))
            project("up_b", *relu("up_b"))
            project("down_b", before=residual("down_b", []))
            rstd_next("final")
            for k in range(KT):
                nc.vector.scalar_tensor_tensor(X[:, k, :], X[:, k, :], gain("final_norm", k), rstd[:], ALU.mult,
                                               ALU.mult).then_inc(x_changed, 1)
                if k:
                    dve.wait_ge(x_changed, k)
                    low("in_sb", X, h1_hi, h1_lo, 0, 0, k - 1)
            dve.wait_ge(x_changed, KT)
            low("in_sb", X, h1_hi, h1_lo, 0, 0, KT - 1)
            n_x[0] += KT
            values("in_sb")
            fused("in_sb", lambda s: query_key_tile("in_sb", s), attention("in_sb"), 4)
            project("out_sb")
            add_normed("post_sb", [("up_sb", h2_hi, h2_lo)])
            project("up_sb", *conv_taps("up_sb"), peel=True)
            conv_low("up_sb", plan["up_sb"]["trips"], 0)
            project("down_sb")
            add_normed("post_ffn_sb", [("in_fox", h1_hi, h1_lo), ("q_fox", h2_hi, h2_lo)])
            values("in_fox")
            dve.wait_ge(f_logits, 1)
            dve.wait_ge(rstd_ready, NORMS["in_fox"] + 1)
            link(nc.vector.tensor_tensor(f_x[:], bank[6][:, 0:TOK], rstd[:], ALU.mult))
            link(nc.vector.tensor_scalar(f_x[:], f_x[:], b_f[:], -1.0, ALU.add, ALU.mult))
            nc.vector.scalar_tensor_tensor(f_n[:], f_x[:], -1.0, f_x[:], ALU.mult, ALU.min).then_inc(f_abs, 1)
            dve.wait_ge(f_log, 1)
            link(nc.vector.scalar_tensor_tensor(f_p[:], f_x[:], 0.0, f_n[:], ALU.max, ALU.add))
            link(nc.vector.tensor_tensor_scan(f_sum[:], ones[:], f_p[:], 0.0, ALU.mult, ALU.add))
            nc.vector.tensor_scalar(neg_fcum8[:], f_sum[:], 1.0 / SCALE, None, ALU.mult).then_inc(f_ready, 1)
            fused("in_fox", lambda s: query_key_tile("in_fox", s), attention("in_fox"), 4)
            project("out_fox")
            add_normed("post_fox", [("up_fox", h2_hi, h2_lo)])
            project("up_fox", *conv_taps("up_fox"), peel=True)
            conv_low("up_fox", plan["up_fox"]["trips"], 0)
            project("down_fox")
            add_normed("post_ffn_fox", [])

        @block.gpsimd
        def _(pool):
            steps, n_odd = [0], [0]

            def link(instruction):
                steps[0] += 1
                instruction.then_inc(pool_step, 1)
                pool.wait_ge(pool_step, steps[0])

            def sum_squares(norm):
                n = NORMS[norm]
                if n:
                    pool.wait_ge(ms_done, n)
                link(nc.gpsimd.memset(sumsq[:], 0.0))

                def add(i, b, first):
                    pool.wait_ge(sq_done, i * 2 + (KT * n + b + 1))
                    if n or not first:
                        pool.wait_ge(sum_done, i * 2 + (KT * n + b))
                    nc.gpsimd.tensor_tensor(sumsq[:], sumsq[:], square[:, b, :], ALU.add).then_inc(sum_done, 1)

                add(0, 0, True)
                add(0, 1, False)
                with pool.Fori(1, KT // 2) as i:
                    add(i, 0, False)
                    add(i, 1, False)

            def rope(layer):
                for j in range(ROPE_PAIRS):
                    pair = ROPE_PAIRS * layer + j
                    at = 2 * (pair % 2)
                    z, rot = Z[:, 2 + 2 * j:4 + 2 * j, :], ROT[:, at:at + 2, :]
                    pool.wait_ge(rot_in[pair % 2], 64 * (pair // 2 + 1))
                    nc.gpsimd.tensor_tensor(z, z, rope_c[:].unsqueeze(1).broadcast_to([P, 2, TOK]),
                                            ALU.mult).then_inc(pool_step, 1)
                    steps[0] += 1
                    link(nc.gpsimd.tensor_tensor(rot, rot, rope_s[:].unsqueeze(1).broadcast_to([P, 2, TOK]),
                                                 ALU.mult))
                    nc.gpsimd.tensor_tensor(z, z, rot, ALU.add).then_inc(roped, 1)

            def scale_odd(norm):
                pool.wait_ge(rstd_ready, NORMS[norm] + 1)
                for k in range(1, KT, 2):
                    nc.gpsimd.tensor_tensor(H[:, k, :], H[:, k, :], rstd[:], ALU.mult).then_inc(y_odd, 1)

            def relu(name):
                base, first_tile = PRODUCTS[name], plan[name]["tile"]
                with pool.Fori(0, plan[name]["trips"]) as i:
                    for b in range(4):
                        pool.wait_ge(tile_out, i * 4 + (first_tile + b + 1))
                        pool.wait_ge(a_ready, i * 4 + (base + b + RING - 1))
                        nc.gpsimd.tensor_tensor(prod[:, b % 2, :], u_buf[:, b, :], u_buf[:, b, :],
                                                ALU.mult).then_inc(prod_ready, 1)

            def conv_products(name):
                base, tap0, first_tile = PRODUCTS[name], FIRST_TAP[name], plan[name]["tile"]
                layer = 0 if name == "up_sb" else 1

                def trip(i, first):
                    for b in range(4):
                        pair = base + b // 2
                        pool.wait_ge(tile_out, i * 4 + (first_tile + b + 1))
                        if not (first and b < 2):
                            pool.wait_ge(taps_done, i * 4 + (tap0 + b - 1))
                        nc.gpsimd.tensor_tensor(m_buf[:, b % 2, :], u_buf[:, b % 2, :],
                                                conv[:, layer, 0, bass.ds(i * 4 + b, 1)].broadcast_to([P, TOK]),
                                                ALU.mult).then_inc(m_ready, 1)
                        pool.wait_ge(m_ready, i * 4 + (tap0 + b + 1))
                        pool.wait_ge(tap1_ready, i * 4 + (tap0 + b + 1))
                        c = c_buf2[:, b, 2:TOK]
                        nc.gpsimd.tensor_tensor(c, c, m_buf[:, b % 2, 0:TOK - 2], ALU.add).then_inc(taps_done, 1)
                        if b % 2:
                            pool.wait_ge(taps_done, i * 4 + (tap0 + b + 1))
                            pool.wait_ge(gelu_ready, i * 2 + (pair - PRODUCTS["up_sb"] + 1))
                            pool.wait_ge(a_ready, i * 2 + (pair + RING - 1))
                            nc.gpsimd.tensor_tensor(prod[:, b // 2, :], gate[:, b // 2, :], c_buf2[:, b, :],
                                                    ALU.mult).then_inc(prod_ready, 1)

                trip(0, True)
                with pool.Fori(1, plan[name]["trips"]) as i:
                    trip(i, False)

            sum_squares("mem_a")
            sum_squares("in_a")
            pool.wait_ge(consts_in, 16 * len(CONSTS))
            rope(0)
            sum_squares("up_a")
            relu("up_a")
            sum_squares("in_b")
            rope(1)
            sum_squares("up_b")
            relu("up_b")
            sum_squares("final")
            sum_squares("in_sb")
            sum_squares("post_sb")
            scale_odd("post_sb")
            sum_squares("up_sb")
            conv_products("up_sb")
            sum_squares("post_ffn_sb")
            scale_odd("post_ffn_sb")
            sum_squares("in_fox")
            sum_squares("post_fox")
            scale_odd("post_fox")
            sum_squares("up_fox")
            conv_products("up_fox")
            sum_squares("post_ffn_fox")
            scale_odd("post_ffn_fox")


def tiles_of(w):
    k, n = w.shape
    return np.ascontiguousarray(w.reshape(k // P, P, n // P, P).transpose(2, 1, 0, 3).reshape(n // P, P, k))


def in_units(name, v, q, k, q_mem=None):
    values = [np.concatenate([v[P * kt:P * (kt + 1), first:first + width] for kt in k_tiles], axis=1)[None]
              for _, first, width, k_tiles in value_units(name)]
    n = q.shape[1] // P
    pairs = np.stack([tiles_of(q), tiles_of(k)], axis=1).reshape(2 * n, P, D)
    return np.concatenate(values + ([] if q_mem is None else [tiles_of(q_mem)]) + [pairs])


def feature_major(t):
    return np.ascontiguousarray(t.T.reshape(KT, P, TOK).transpose(1, 0, 2))


def shape_constants():
    half = HEAD // 2
    inv = (1.0 / (np.float32(10000.0) ** (np.arange(half, dtype=np.float32) / np.float32(half)))).astype(np.float32)
    angle = (np.arange(TOK, dtype=np.float32)[:, None] * inv[None, :]).T
    cos, sin = np.cos(angle).astype(np.float32), np.sin(angle).astype(np.float32)
    q, k = np.arange(P)[:, None], np.arange(P)[None, :]
    inclusive = np.where(k <= q, 0.0, NEG).astype(np.float32)
    strict = np.where(k < q, 0.0, NEG).astype(np.float32)
    seen = np.zeros((P, P), np.float32)
    return {"ones": np.ones((P, TOK), np.float32),
            "ident": np.eye(P, dtype=np.float32), "rope_c": np.concatenate([cos] * 4),
            "rope_s": np.concatenate([-sin, sin] * 2),
            "mask_in": np.concatenate([inclusive, seen, inclusive], axis=1),
            "mask_ex": np.concatenate([strict, seen, strict], axis=1)}


def kernel(**inputs):
    import concourse.bacc as bacc
    from concourse.bass_utils import run_bass_kernel_spmd

    a = {k: np.asarray(v) for k, v in inputs.items()}
    up2 = [a["w_up_2"][i].reshape(D, 2, D_FF2 // P, P).transpose(0, 2, 1, 3).reshape(D, 2 * D_FF2)
           for i in range(2)]
    qkv = a["w_kvf_2"]
    weights = {"mem_a": a["a_w_mem_kv"][0], "mem_b": a["b_w_mem_kv"][0],
               "out_a": a["a_w_out"][0], "up_a": a["a_w_up"][0], "down_a": a["a_w_down"][0],
               "out_b": a["b_w_out"][0], "up_b": a["b_w_up"][0],
               "down_b": a["b_w_down"][0], "out_sb": a["sb_w_o_2"][0],
               "up_sb": up2[0], "down_sb": a["w_down_2"][0],
               "out_fox": a["fox_w_o_2"][0], "up_fox": up2[1], "down_fox": a["w_down_2"][1]}
    arrays = {"w_" + name: tiles_of(w) for name, w in weights.items()}
    a_in, b_in, sb_in = a["a_w_in"][0], a["b_w_in"][0], a["sb_w_qkv_2"][0]
    s = SELF_W
    arrays["w_in_a"] = in_units("in_a", a_in[:, 2 * s:3 * s], a_in[:, :s], a_in[:, s:2 * s], a_in[:, 3 * s:])
    arrays["w_in_b"] = in_units("in_b", a["w_kv"][:, s:], b_in[:, :s], a["w_kv"][:, :s], b_in[:, s:])
    arrays["w_in_sb"] = in_units("in_sb", sb_in[:, 2 * D:], sb_in[:, :D], sb_in[:, D:2 * D])
    arrays["w_in_fox"] = in_units("in_fox", qkv[:, D:2 * D], a["fox_w_q_2"][0], qkv[:, :D])
    arrays["x"] = feature_major(a["x"][0])
    arrays["mem"] = feature_major(a["mem"][0])

    def row(name):
        base, _, at = name.partition(".")
        return a[base][int(at)] if at else a[base].reshape(D)

    arrays["gains"] = np.ascontiguousarray(np.stack([row(n) for n in GAINS]).reshape(len(GAINS), KT, P)
                                           .transpose(2, 0, 1))
    arrays["subln"] = np.ascontiguousarray(a["a_subln"].reshape(P, 1))
    taps = np.concatenate([a["conv_w_2"], a["conv_b_2"][:, None, :]], axis=1)
    arrays["conv"] = np.ascontiguousarray(taps.reshape(2, 4, 2, D_FF2 // P, P).transpose(4, 0, 1, 3, 2)
                                          .reshape(P, 2, 4, 2 * D_FF2 // P))
    arrays["lam"] = np.ascontiguousarray(np.broadcast_to(a["a_lambda"][0], (P, 4, HEAD)))
    w_f, b_f = np.zeros((D, P), np.float32), np.zeros((P, 1), np.float32)
    for at in (0, HEAD):
        w_f[:, at:at + HEADS2] = qkv[:, 2 * D:]
        b_f[at:at + HEADS2, 0] = a["b_f_2"]
    arrays["w_f"] = np.ascontiguousarray(w_f.reshape(KT, P, P).transpose(1, 0, 2))
    arrays["b_f"] = b_f
    arrays.update(shape_constants())

    nc = bacc.Bacc("TRN2", target_bir_lowering=False, num_devices=1)
    ins = {name: nc.dram_tensor("in_" + name, v.shape, mybir.dt.from_np(v.dtype), kind="ExternalInput").ap()
           for name, v in arrays.items()}
    out = nc.dram_tensor("out_x", (P, KT, TOK), mybir.dt.float32, kind="ExternalOutput").ap()
    build_program(nc, ins, out)
    r = run_bass_kernel_spmd(nc, [{"in_" + name: v for name, v in arrays.items()}], core_ids=[0])
    got = np.asarray(r.results[0]["out_x"])
    return np.ascontiguousarray(got.transpose(1, 0, 2).reshape(D, TOK).T).reshape(1, TOK, D)
```

```python
import math
from contextlib import ExitStack

import numpy as np

import concourse.bass as bass
from concourse import mybir

P = 128
D = 1024
TOK = 256
KT = D // P
HEAD = 64
SELF_W = 3 * D // 4
MEM_W = D - SELF_W
D_FF = 4 * D
D_FF2 = ((8 * D // 3 + 127) // 128) * 128
HEADS2 = D // HEAD
NEG = -1e30
EPS = 1e-6
LAM_INIT = 0.8 - 0.6 * math.exp(-0.3 * 0)
RING = 4
SCALE = HEAD ** -0.5

GAINS = ["a_norm_attn", "a_mem_norm", "b_mem_norm", "a_norm_mlp", "kv_norm", "b_norm_attn", "b_norm_mlp",
         "final_norm", "sb_pre_g_2", "sb_post_g_2", "kv_norm_g_2", "fox_pre_g_2", "fox_post_g_2",
         "ffn_pre_g_2.0", "ffn_pre_g_2.1", "ffn_post_g_2.0", "ffn_post_g_2.1"]

ALL_K = (8,)
DOWN_K = (8, 8, 8, 8)
DOWN2_K = (6, 6, 5, 5)

GEMMS = [("mem_a", 4, ALL_K), ("in_a", 20, ALL_K), ("mem_b", 4, ALL_K), ("out_a", 8, ALL_K), ("up_a", 32, ALL_K), ("down_a", 8, DOWN_K),
         ("in_b", 20, ALL_K), ("out_b", 8, ALL_K), ("up_b", 32, ALL_K), ("down_b", 8, DOWN_K),
         ("in_sb", 24, ALL_K), ("out_sb", 8, ALL_K), ("up_sb", 44, ALL_K), ("down_sb", 8, DOWN2_K),
         ("in_fox", 24, ALL_K), ("out_fox", 8, ALL_K), ("up_fox", 44, ALL_K), ("down_fox", 8, DOWN2_K)]

VALUE_GROUPS = {"in_a": (512, 256), "in_b": (512, 256), "in_sb": (512, 512), "in_fox": (512, 512)}


def stream_plan():
    plan, unit, tile = {}, 0, 0
    for name, tiles, ks in GEMMS:
        body = RING if len(ks) == 1 else 2
        values = sum(VALUE_GROUPS.get(name, ())) // P
        plan[name] = dict(name=name, tiles=tiles, ks=ks, unit=unit, tile=tile, body=body, trips=tiles // body,
                          units=tiles * len(ks), values=values)
        unit += tiles * len(ks)
        tile += tiles - values
    return plan


def value_units(name):
    units, first = [], 0
    for group, width in enumerate(VALUE_GROUPS[name]):
        per = D // width
        units += [(group, first, width, range(k, k + per)) for k in range(0, KT, per)]
        first += width
    return units


ATTENTIONS = {"mem_a": 4, "diff": 12, "mem_b": 4, "moba": 12, "stick": 16, "forget": 16}
FUSED = {"in_a": ("mem_a", "diff"), "in_b": ("mem_b", "moba"), "in_sb": ("stick",), "in_fox": ("forget",)}
LAG = {"in_a": 2, "in_b": 2, "in_sb": 3, "in_fox": 3}
AHEAD = {"in_a": 2, "in_b": 2, "in_sb": 3, "in_fox": 2}


def attention_plan():
    plan, n, t, tiles, plain = {}, 0, 0, 0, 0
    for name, units in ATTENTIONS.items():
        rows = []
        for u in range(units):
            half = u % 2
            diff = name == "diff"
            emits = not diff or half == 1
            rows.append(dict(n=n, j=u // 2, half=half, emits=emits, t=t, tile=tiles, plain=plain, diff=diff,
                             mem=name.startswith("mem"), stick=name == "stick", kind=name,
                             first=n - u))
            n += 1
            t += emits
            tiles += half
            plain += half and not diff
        plan[name] = rows
    return plan


def build_program(nc, ins, out):
    f32, f32r = mybir.dt.float32, mybir.dt.float32r
    ALU, ACT, AX = mybir.AluOpType, mybir.ActivationFunctionType, mybir.AxisListType
    plan, heads = stream_plan(), attention_plan()
    order = [g[0] for g in GEMMS]

    ctx = ExitStack()
    with ctx:
        def sb(name, shape, dt=f32):
            return ctx.enter_context(nc.sbuf_tensor(name, shape, dt))

        def sem(name):
            return ctx.enter_context(nc.semaphore(name))

        raw = sb("raw", [P, RING, KT * P])
        w_hi = sb("w_hi", [P, RING, KT * P], f32r)
        w_lo = sb("w_lo", [P, RING, KT * P], f32r)
        X = sb("X", [P, KT, TOK])
        h1_hi = sb("h1_hi", [P, KT, TOK], f32r)
        h1_lo = sb("h1_lo", [P, KT, TOK], f32r)
        h2_hi = sb("h2_hi", [P, KT, TOK], f32r)
        h2_lo = sb("h2_lo", [P, KT, TOK], f32r)
        H = sb("H", [P, KT, TOK])
        ZM = sb("ZM", [P, KT, TOK])
        mv_tok = sb("mv_tok", [P, 2, 2, MEM_W])
        wf_hi = sb("wf_hi", [P, KT, P], f32r)
        wf_lo = sb("wf_lo", [P, KT, P], f32r)
        ident = sb("ident_sb", [P, P])
        ones = sb("ones_sb", [P, TOK])
        rope_c = sb("rope_c_sb", [P, TOK])
        rope_s = sb("rope_s_sb", [P, TOK])
        mask_in = sb("mask_in_sb", [P, 3 * P])
        mask_ex = sb("mask_ex_sb", [P, 3 * P])
        gains = sb("gains_sb", [P, len(GAINS), KT])
        subln = sb("subln_sb", [P, 1])
        subln_s = sb("subln_s", [P, 1])
        conv = sb("conv_sb", [P, 2, 4, 2 * D_FF2 // P])
        lam_in = sb("lam_in_sb", [P, 4, HEAD])
        lam_prod = sb("lam_prod", [P, 2, HEAD])
        lam_sum = sb("lam_sum", [P, 2])
        lam_exp = sb("lam_exp", [P, 2])
        neg_lam = sb("neg_lam", [P, 1])
        b_f = sb("b_f_sb", [P, 1])
        eps_col = sb("eps_col", [P, 1])
        log_ms_col = sb("log_ms_col", [P, 2])
        rstd_col = sb("rstd_col", [P, 2])
        sumsq = sb("sumsq", [P, TOK])
        square = sb("square", [P, 2, TOK])
        log_ms = sb("log_ms", [P, TOK])
        rstd = sb("rstd", [P, TOK])
        rstd_mem = sb("rstd_mem", [P, TOK])
        unit_max = sb("unit_max", [P, 4, 2])
        unit_bias = sb("unit_bias", [P, 4, 2])
        unit_sum = sb("unit_sum", [P, 4, 2])
        unit_rcp = sb("unit_rcp", [P, 4, 2])

        with ExitStack() as mlp:
            def mlp_sb(name, shape, dt=f32):
                return mlp.enter_context(nc.sbuf_tensor(name, shape, dt))

            a_hi = mlp_sb("a_hi", [P, D_FF // P, TOK], f32r)
            a_lo = mlp_sb("a_lo", [P, D_FF // P, TOK], f32r)
            c_buf2 = mlp_sb("conv_buf", [P, 4, TOK])
            prod = mlp_sb("prod", [P, 2, TOK])
        u_buf = H[:, 0:4, :]
        m_buf = H[:, 4:6, :]
        gate = H[:, 6:8, :]
        Z = sb("Z", [P, 16, TOK])
        ROT = sb("ROT", [P, 4, TOK])
        o_hi = sb("o_hi", [P, KT, TOK], f32r)
        o_lo = sb("o_lo", [P, KT, TOK], f32r)
        v_tok = sb("v_tok", [P, 2, D])
        s_buf = sb("s_buf", [P, 3, 2 * TOK])
        n_buf = sb("n_buf", [P, 2, 2 * TOK])
        c_buf = sb("c_buf", [P, 2, 2 * TOK])
        p_buf = sb("p_buf", [P, 3, 2 * TOK])
        sub_rms = n_buf[:, :, 0:TOK]
        pt_buf = sb("pt_buf", [P, 2, 2 * TOK])
        f_x = sb("f_x", [P, TOK])
        f_n = sb("f_n", [P, TOK])
        f_p = sb("f_p", [P, TOK])
        f_sum = sb("f_sum", [P, TOK])
        fcum_hi = sb("fcum_hi", [P, TOK], f32r)
        fcum_lo = sb("fcum_lo", [P, TOK], f32r)
        ident_r = sb("ident_r", [P, P], f32r)

        bank = [ctx.enter_context(nc.psum_tensor(f"bank{b}", [P, 2 * TOK], f32)) for b in range(8)]

        consts_in = sem("consts_in")
        warm_ready = sem("warm_ready")
        ones_in = sem("ones_in")
        x_in = sem("x_in")
        mem_in = sem("mem_in")
        raw_in = [sem(f"raw_in{s}") for s in range(RING)]
        hi_ready = sem("hi_ready")
        lo_ready = sem("lo_ready")
        units_done = sem("units_done")
        tile_out = sem("tile_out")
        sq_done = sem("sq_done")
        sum_done = sem("sum_done")
        ms_done = sem("ms_done")
        rstd_ready = sem("rstd_ready")
        rstd_kept = sem("rstd_kept")
        col_ready = sem("col_ready")
        h_hi = sem("h_hi")
        h_lo = sem("h_lo")
        y_even = sem("y_even")
        y_odd = sem("y_odd")
        x_changed = sem("x_changed")
        dve_step = sem("dve_step")
        act_step = sem("act_step")
        pool_step = sem("pool_step")
        rot_in = [sem(f"rot_in{b}") for b in range(2)]
        sin_done = sem("sin_done")
        roped = sem("roped")
        vt_done = sem("vt_done")
        vt_out = sem("vt_out")
        v_out = sem("v_out")
        s_done = sem("s_done")
        s_out = sem("s_out")
        exp_done = sem("exp_done")
        scanned = sem("scanned")
        arg_ready = sem("arg_ready")
        p_ready = sem("p_ready")
        t_done = sem("t_done")
        t_out = sem("t_out")
        o_done = sem("o_done")
        o_hi_out = sem("o_hi_out")
        o_out = sem("o_out")
        gelu_ready = sem("gelu_ready")
        tap2_ready = sem("tap2_ready")
        tap1_ready = sem("tap1_ready")
        m_ready = sem("m_ready")
        taps_done = sem("taps_done")
        prod_ready = sem("prod_ready")
        a_hi_ready = sem("a_hi_ready")
        a_ready = sem("a_ready")
        lam_ready = sem("lam_ready")
        sub_copied = sem("sub_copied")
        sub_out = sem("sub_out")
        sub_ms = sem("sub_ms")
        sub_rstd = sem("sub_rstd")
        sub_scaled = sem("sub_scaled")
        sub_hi = sem("sub_hi")
        sub_lo = sem("sub_lo")
        wf_in = sem("wf_in")
        wf_split = sem("wf_split")
        f_logits = sem("f_logits")
        f_abs = sem("f_abs")
        f_log = sem("f_log")
        f_cum = sem("f_cum")
        f_high = sem("f_high")
        f_ready = sem("f_ready")
        out_done = sem("out_done")

        block = ctx.enter_context(nc.Block())

        OPERANDS = {"mem_a": (0, 1), "mem_b": (8, 1), "in_a": (16, 1), "up_a": (24, 1), "in_b": (32, 2),
                    "q_b": (33, 2), "up_b": (48, 1), "in_sb": (56, 1), "up_sb": (64, 1), "in_fox": (72, 2),
                    "q_fox": (73, 2), "up_fox": (88, 1)}
        GAIN_OF = {"mem_a": "a_mem_norm", "mem_b": "b_mem_norm", "in_a": "a_norm_attn", "up_a": "a_norm_mlp",
                   "q_b": "b_norm_attn", "in_b": "kv_norm", "up_b": "b_norm_mlp", "in_sb": "sb_pre_g_2",
                   "up_sb": "ffn_pre_g_2.0", "in_fox": "kv_norm_g_2", "q_fox": "fox_pre_g_2",
                   "up_fox": "ffn_pre_g_2.1"}
        NORMS = {n: i for i, n in enumerate(
            ["mem_a", "in_a", "up_a", "in_b", "up_b", "final", "in_sb", "post_sb", "up_sb", "post_ffn_sb",
             "in_fox", "post_fox", "up_fox", "post_ffn_fox"])}
        MS_AFTER = {"mem_a": 2, "in_a": 2, "up_a": 1, "in_b": 2, "up_b": 1, "in_sb": 3, "up_sb": 2, "in_fox": 3,
                    "up_fox": 2}
        TOGETHER = ("up_sb", "up_fox")
        DIRECT = ("final", "post_sb", "post_ffn_sb", "post_fox", "post_ffn_fox")
        VALUE_PIECES = 4
        ROPE_PAIRS = SELF_W // P

        def gain(name, k):
            return gains[:, GAINS.index(name), bass.ds(k, 1)]

        def operand_count(name, i, per, k):
            first, step = OPERANDS[name]
            return i * (per * step) + (first + step * k + 1)

        PRODUCTS = {"up_a": 0, "up_b": D_FF // P, "up_sb": 2 * D_FF // P, "up_fox": 2 * D_FF // P + D_FF2 // P}
        DOWN_OF = {"down_a": "up_a", "down_b": "up_b", "down_sb": "up_sb", "down_fox": "up_fox"}
        FIRST_TAP = {"up_sb": 0, "up_fox": 2 * D_FF2 // P}
        by_n = {u["n"]: u for units in heads.values() for u in units}
        CONSTS = [(ident, "ident"), (rope_c, "rope_c"), (rope_s, "rope_s"),
                  (mask_in, "mask_in"), (mask_ex, "mask_ex"), (subln, "subln"),
                  (conv, "conv"), (lam_in, "lam"), (b_f, "b_f")]

        def geometry(u):
            w0 = TOK if u["mem"] else P
            return w0, w0 + TOK

        def output_feature_tile(u):
            return u["j"] + (SELF_W // P if u["mem"] else 0)

        def attention_units(name):
            return [u for kind in FUSED[name] for u in heads[kind]]

        by_tile = {u["tile"]: u for u in by_n.values()}

        def left_bank(tile):
            u = by_tile[tile]
            return (sub_out, u["j"] + 1) if u["diff"] else (o_out, u["plain"] + 1)

        def values_before(name):
            return VALUE_PIECES * list(FUSED).index(name)

        def fused_tiles(name):
            return plan[name]["tiles"] - plan[name]["values"] + (plan["mem_b"]["tiles"] if name == "in_a" else 0)

        def fused(name, tile, step, lags):
            tiles, units = fused_tiles(name), attention_units(name)
            for s in range(LAG[name] + len(units) + lags):
                if s < tiles:
                    tile(s)
                if s >= LAG[name]:
                    step(s - LAG[name])

        @block.sync
        def _(sp):
            sp.dma_start(gains[:], ins["gains"]).then_inc(mem_in, 16)
            sp.dma_start(ZM[:], ins["mem"]).then_inc(mem_in, 16)

            def load(g, f, part, free, slot):
                at, k = sum(g["ks"][:part]), g["ks"][part]
                if free is not None:
                    sp.wait_ge(lo_ready, free)
                sp.dma_start(raw[:, slot, 0:k * P],
                             ins["w_" + g["name"]][f, :, at * P:(at + k) * P]).then_inc(raw_in[slot], 16)

            for name in order:
                g = plan[name]
                nk, body = len(g["ks"]), g["body"]
                if g["trips"] == 1:
                    for s in range(body):
                        load(g, s, 0, g["unit"] + s - RING + 1 if g["unit"] else None, s % RING)
                    if name == "mem_a":
                        sp.dma_start(ones[:], ins["ones"]).then_inc(ones_in, 16)
                        sp.dma_start(X[:], ins["x"]).then_inc(x_in, 16)
                        for dst, const in CONSTS:
                            sp.dma_start(dst[:], ins[const]).then_inc(consts_in, 16)
                        sp.dma_start(H[:, 0:KT // 2, :].rearrange("p a (b c) -> p (a b) c", c=P),
                                     ins["w_f"]).then_inc(wf_in, 16)
                else:
                    with sp.Fori(0, g["trips"]) as i:
                        for s in range(body * nk):
                            load(g, i * body + s // nk, s % nk, i * (body * nk) + (g["unit"] + s - RING + 1),
                                 s % RING)
            sp.wait_ge(x_changed, 5 * KT)
            sp.dma_start(out, X[:]).then_inc(out_done, 16)
            sp.wait_ge(out_done, 16)

        @block.tensor
        def _(pe):
            n_ms, n_vt = [0], [0]

            def values(name):
                g = plan[name]
                pe.wait_ge(tile_out, g["tile"])
                for s, (group, _, width, k_tiles) in enumerate(value_units(name)):
                    pe.wait_ge(lo_ready, g["unit"] + s + 1)
                    slot = (g["unit"] + s) % RING
                    for at, k in enumerate(k_tiles):
                        if group == 0:
                            pe.wait_ge(h_lo, operand_count(name, 0, 0, k))
                        w = slice(at * width, (at + 1) * width)
                        for tt in range(2):
                            dst, tokens = bank[2 * group + tt][:, 0:width], slice(tt * P, (tt + 1) * P)
                            nc.tensor.matmul(dst, h1_hi[:, k, tokens], w_hi[:, slot, w], start=k == 0, stop=False)
                            nc.tensor.matmul(dst, h1_hi[:, k, tokens], w_lo[:, slot, w], start=False, stop=False)
                            last = nc.tensor.matmul(dst, h1_lo[:, k, tokens], w_hi[:, slot, w], start=False,
                                                    stop=k == KT - 1)
                    last.then_inc(units_done, 1)
                    if s == MS_AFTER[name]:
                        mean_square(columns=True)

            def query_key_tile(name, s, src_hi, src_lo):
                g = plan[name]
                unit = g["unit"] + g["values"] + s
                pe.wait_ge(lo_ready, unit + 1)
                if s < 2:
                    pe.wait_ge(v_out, values_before(name) + 2)
                else:
                    pe.wait_ge(tile_out, g["tile"] + s - 1)
                for k in range(KT):
                    w = slice(k * P, (k + 1) * P)
                    dst, slot = bank[s % 2][:, 0:TOK], unit % RING
                    nc.tensor.matmul(dst, w_hi[:, slot, w], src_hi[:, k, :], start=k == 0, stop=False)
                    nc.tensor.matmul(dst, w_hi[:, slot, w], src_lo[:, k, :], start=False, stop=False)
                    last = nc.tensor.matmul(dst, w_lo[:, slot, w], src_hi[:, k, :], start=False, stop=k == KT - 1)
                last.then_inc(units_done, 1)

            def gemm(name, src_hi, src_lo, operand_tile=None):
                g = plan[name]
                nk, body = len(g["ks"]), g["body"]
                banks = RING if nk == 1 else 2

                def trip(i, first=False, done=0):
                    for s in range(done, body * nk):
                        part, b = s % nk, s // nk % banks
                        pe.wait_ge(lo_ready, i * (body * nk) + (g["unit"] + s + 1))
                        if part == 0 and g["tile"]:
                            pe.wait_ge(tile_out, i * body + (g["tile"] + s // nk - banks + 1))
                        at, slot, k_tiles = sum(g["ks"][:part]), s % RING, g["ks"][part]
                        if name in DOWN_OF:
                            pe.wait_ge(a_ready, RING + PRODUCTS[DOWN_OF[name]] + at + k_tiles)
                        for k in range(k_tiles):
                            w = slice(k * P, (k + 1) * P)
                            begin, end = part == 0 and k == 0, part == nk - 1 and k == k_tiles - 1
                            dst = bank[b][:, 0:TOK]
                            if s == 0 and operand_tile is not None:
                                pe.wait_ge(*operand_tile(k))
                            if first and s == 0:
                                pe.wait_ge(h_lo, operand_count(name, 0, 0, k))
                            nc.tensor.matmul(dst, w_hi[:, slot, w], src_hi[:, at + k, :], start=begin, stop=False)
                            nc.tensor.matmul(dst, w_hi[:, slot, w], src_lo[:, at + k, :], start=False, stop=False)
                            last = nc.tensor.matmul(dst, w_lo[:, slot, w], src_hi[:, at + k, :], start=False,
                                                    stop=end)
                        last.then_inc(units_done, 1)
                        if first and s == MS_AFTER.get(name):
                            mean_square()

                def together():
                    units = MS_AFTER[name] + 1
                    for k in range(KT):
                        pe.wait_ge(h_lo, operand_count(name, 0, 0, k))
                        w = slice(k * P, (k + 1) * P)
                        for s in range(units):
                            if k == 0:
                                pe.wait_ge(lo_ready, g["unit"] + s + 1)
                                pe.wait_ge(tile_out, g["tile"] + s - banks + 1)
                            dst, slot = bank[s][:, 0:TOK], s % RING
                            nc.tensor.matmul(dst, w_hi[:, slot, w], src_hi[:, k, :], start=k == 0, stop=False)
                            nc.tensor.matmul(dst, w_hi[:, slot, w], src_lo[:, k, :], start=False, stop=False)
                            last = nc.tensor.matmul(dst, w_lo[:, slot, w], src_hi[:, k, :], start=False,
                                                    stop=k == KT - 1)
                            if k == KT - 1:
                                last.then_inc(units_done, 1)
                    mean_square()
                    trip(0, done=units)

                peeled = name in OPERANDS
                if name in TOGETHER:
                    together()
                elif peeled or g["trips"] == 1:
                    trip(0, peeled)
                if g["trips"] > 1:
                    with pe.Fori(1 if peeled else 0, g["trips"]) as i:
                        trip(i)

            def mean_square(columns=False):
                direct = list(NORMS)[n_ms[0]] in DIRECT
                pe.wait_ge(sum_done, KT * (n_ms[0] + 1) - direct)
                if n_ms[0]:
                    pe.wait_ge(rstd_ready, n_ms[0])
                else:
                    pe.wait_ge(ones_in, 16)
                last = nc.tensor.matmul(bank[7][:, 0:TOK], ones[:, 0:P], sumsq[:], start=True, stop=not direct)
                if direct:
                    pe.wait_ge(sq_done, KT * (n_ms[0] + 1))
                    last = nc.tensor.matmul(bank[7][:, 0:TOK], ones[:, 0:P], square[:, (KT - 1) % 2, :],
                                            start=False, stop=True)
                for tt in range(2 if columns else 0):
                    last = nc.tensor.matmul(bank[7][:, TOK + tt:TOK + tt + 1], sumsq[:, tt * P:(tt + 1) * P],
                                            ones[:, 0:1], start=True, stop=True)
                last.then_inc(ms_done, 1)
                n_ms[0] += 1

            def keep_warm(src, count):
                for _ in range(count):
                    nc.tensor.matmul(bank[6][:, 0:TOK], src[:, 0:P], src[:], start=True, stop=True)

            def transpose_values(src, first, tiles):
                for j in range(first, first + tiles, 2):
                    if n_vt[0]:
                        pe.wait_ge(vt_out, n_vt[0])
                    for tt in range(2):
                        for jj in range(2):
                            last = nc.tensor.transpose(bank[6][:, tt * TOK + jj * P:tt * TOK + (jj + 1) * P],
                                                       src[:, j + jj, tt * P:(tt + 1) * P], ident[:])
                    last.then_inc(vt_done, 1)
                    n_vt[0] += 1

            def attention(name):
                units, ahead = attention_units(name), AHEAD[name]
                layer = list(FUSED).index(name)
                rope = "mem_" in FUSED[name][0]

                def operands(u):
                    j = u["j"]
                    if u["mem"]:
                        return (Z[:, j, :], ZM[:, 4 * layer + j, :], mv_tok[:, layer],
                                (tile_out, plan[name]["tile"] + j + 1))
                    if rope:
                        return (Z[:, 2 + 2 * j, :], Z[:, 3 + 2 * j, :], v_tok,
                                (roped, ROPE_PAIRS * layer + j + 1))
                    return Z[:, 2 * j, :], Z[:, 2 * j + 1, :], v_tok, (tile_out, plan[name]["tile"] + 2 * j + 2)

                def scores(u):
                    w0, _ = geometry(u)
                    q, k, _, ready = operands(u)
                    pe.wait_ge(*ready)
                    rows = slice(HEAD * u["half"], HEAD * (u["half"] + 1))
                    if u["n"] >= 2:
                        pe.wait_ge(s_out, u["n"] - 1)
                    forget = u["kind"] == "forget"
                    if forget:
                        pe.wait_ge(f_ready, 1)
                    for qt in range(2):
                        width = w0 if qt == 0 else TOK
                        dst = bank[4 + u["n"] % 2][:, qt * w0:qt * w0 + width]
                        last = nc.tensor.matmul(dst, q[rows, qt * P:(qt + 1) * P], k[rows, 0:width], start=True,
                                                stop=not forget)
                        if forget:
                            c = HEAD * u["half"] + 2 * u["j"] + u["half"]
                            pick = ident_r[rows, c:c + 1].broadcast_to([HEAD, P])
                            nc.tensor.matmul(dst, pick, fcum_hi[rows, 0:width], start=False, stop=False)
                            last = nc.tensor.matmul(dst, pick, fcum_lo[rows, 0:width], start=False, stop=True)
                    last.then_inc(s_done, 1)

                def transposes(u):
                    if not u["emits"]:
                        return
                    w0, _ = geometry(u)
                    pe.wait_ge(p_ready, u["n"] + 1)
                    pe.wait_ge(vt_out, n_vt[0])
                    if u["t"]:
                        pe.wait_ge(t_out, u["t"])
                    pieces = [(0, 0), (P, w0)] + ([(TOK, P), (TOK + P, TOK + P)] if u["mem"] else [(TOK, TOK)])
                    for dst, src in pieces:
                        last = nc.tensor.transpose(bank[6][:, dst:dst + P], p_buf[:, u["n"] % 3, src:src + P],
                                                   ident[:])
                    last.then_inc(t_done, 1)

                def outputs(u):
                    if not u["emits"]:
                        return
                    pe.wait_ge(t_out, u["t"] + 1)
                    diff, mem, v = u["diff"], u["mem"], operands(u)[2]
                    if u["n"] == units[0]["n"]:
                        pe.wait_ge(v_out, values_before(name) + VALUE_PIECES)
                    if (diff or u["half"] == 0) and u["tile"] >= 2:
                        pe.wait_ge(*left_bank(u["tile"] - 2))
                    rows = slice(0, P) if diff else slice(HEAD * u["half"], HEAD * (u["half"] + 1))
                    cols = slice(u["j"] * P + rows.start, u["j"] * P + rows.stop)
                    dst, pt = bank[(7, 3)[u["tile"] % 2]], pt_buf[:, u["t"] % 2, :]
                    nc.tensor.matmul(dst[rows, 0:TOK], v[:, 0, cols], pt[:, 0:TOK], start=True, stop=False)
                    last = nc.tensor.matmul(dst[rows, (0 if mem else P):TOK], v[:, 1, cols],
                                            pt[:, TOK:(2 * TOK if mem else TOK + P)], start=False, stop=True)
                    last.then_inc(o_done, 1)

                def sub_square(u):
                    j = u["j"]
                    if not (u["diff"] and u["half"]):
                        return
                    pe.wait_ge(sub_out, j + 1)
                    if j:
                        pe.wait_ge(sub_rstd, j)
                    nc.tensor.matmul(bank[2][:, j % 2 * TOK:(j % 2 + 1) * TOK], ones[:, 0:P], square[:, j % 2, :],
                                     start=True, stop=True).then_inc(sub_ms, 1)

                def step(i):
                    if i < len(units):
                        scores(units[i])
                    if 0 <= i - ahead < len(units):
                        transposes(units[i - ahead])
                    if 0 <= i - ahead - 1 < len(units):
                        outputs(units[i - ahead - 1])
                    if 0 <= i - 4 < len(units):
                        sub_square(units[i - 4])
                return step

            def attended(name):
                by_feature = {output_feature_tile(u): u for u in attention_units(name)}

                def wait(k):
                    u = by_feature[k]
                    return (sub_lo, u["j"] + 1) if u["diff"] else (o_out, u["plain"] + 1)
                return wait

            pe.wait_ge(warm_ready, 1)
            keep_warm(log_ms, 20)
            gemm("mem_a", a_hi, a_lo)
            pe.wait_ge(consts_in, 16 * len(CONSTS))
            values("in_a")
            transpose_values(ZM, 2, 2)
            fused("in_a", lambda s: query_key_tile("in_a", s, *((h1_hi, h1_lo) if s < 2 + 2 * ROPE_PAIRS
                                                                else (h2_hi, h2_lo))), attention("in_a"), 4)
            gemm("out_a", o_hi, o_lo, attended("in_a"))
            gemm("up_a", h2_hi, h2_lo)
            gemm("down_a", a_hi, a_lo)
            values("in_b")
            transpose_values(ZM, 6, 2)
            pe.wait_ge(h_lo, operand_count("q_b", 0, 0, KT - 1))
            fused("in_b", lambda s: query_key_tile("in_b", s, *((h1_hi, h1_lo) if s > 2 and s % 2
                                                                else (h2_hi, h2_lo))), attention("in_b"), 3)
            gemm("out_b", o_hi, o_lo, attended("in_b"))
            gemm("up_b", h2_hi, h2_lo)
            gemm("down_b", a_hi, a_lo)
            mean_square()
            keep_warm(ones, 7)
            values("in_sb")
            fused("in_sb", lambda s: query_key_tile("in_sb", s, h1_hi, h1_lo), attention("in_sb"), 4)
            gemm("out_sb", o_hi, o_lo, attended("in_sb"))
            mean_square()
            keep_warm(ones, 7)
            gemm("up_sb", h2_hi, h2_lo)
            gemm("down_sb", a_hi, a_lo)
            mean_square()
            keep_warm(ones, 7)
            values("in_fox")
            pe.wait_ge(wf_split, 2)
            for k in range(KT):
                dst = bank[6][:, 0:TOK]
                nc.tensor.matmul(dst, wf_hi[:, k, :], h1_hi[:, k, :], start=k == 0, stop=False)
                nc.tensor.matmul(dst, wf_hi[:, k, :], h1_lo[:, k, :], start=False, stop=False)
                last = nc.tensor.matmul(dst, wf_lo[:, k, :], h1_hi[:, k, :], start=False, stop=k == KT - 1)
            last.then_inc(f_logits, 1)
            pe.wait_ge(h_lo, operand_count("q_fox", 0, 0, KT - 1))
            fused("in_fox", lambda s: query_key_tile("in_fox", s, *((h1_hi, h1_lo) if s % 2 else (h2_hi, h2_lo))),
                  attention("in_fox"), 3)
            gemm("out_fox", o_hi, o_lo, attended("in_fox"))
            mean_square()
            keep_warm(ones, 7)
            gemm("up_fox", h2_hi, h2_lo)
            gemm("down_fox", a_hi, a_lo)
            mean_square()

        def run_projection(eng, name, lead, split, before=None, after=None, middle=None, opening=()):
            g = plan[name]
            nk, body = len(g["ks"]), g["body"]
            per = body * nk
            at = order.index(name)
            following = plan[order[at + 1]] if at + 1 < len(order) else None

            def trip(i, first, last):
                held = []
                start = 0
                if first and name in TOGETHER:
                    for what, s in opening:
                        if what == "split":
                            split(i, per, g["unit"] + s + lead, g["ks"][0])
                        elif what == "middle":
                            middle[s]()
                        else:
                            {"before": before, "after": after}[what](i, g["unit"] + s + 1, s, first)
                    start = MS_AFTER[name] + 1
                for s in range(start, per):
                    ahead = s + lead
                    holds = first and name in MS_AFTER and s <= MS_AFTER[name]
                    finished = (i, i * per + (g["unit"] + s + 1), s // nk, first)
                    if before is not None and s % nk == nk - 1 and not holds:
                        before(*finished)
                    if not last or ahead < per:
                        split(i, per, g["unit"] + ahead, g["ks"][ahead % nk])
                    elif following is not None:
                        split(i, per, g["unit"] + ahead, following["ks"][(ahead - per) % len(following["ks"])])
                    if holds:
                        held.append(finished)
                    elif after is not None and s % nk == nk - 1:
                        after(*finished)
                    if holds and s == MS_AFTER[name]:
                        if middle is not None:
                            middle()
                        for tile in held:
                            for work in (before, after):
                                if work is not None:
                                    work(*tile)

            peel = name in MS_AFTER
            if peel and g["trips"] > 1:
                trip(0, True, False)
            start = 1 if peel else 0
            if g["trips"] - 1 > start:
                with eng.Fori(start, g["trips"] - 1) as i:
                    trip(i, False, False)
            trip(g["trips"] - 1, g["trips"] == 1, True)

        @block.scalar
        def _(act):
            steps, n_norm, n_vt, n_columns = [0], [0], [0], [0]

            def link(instruction):
                steps[0] += 1
                instruction.then_inc(act_step, 1)
                act.wait_ge(act_step, steps[0])

            def split(i, per_trip, unit, k):
                slot = unit % RING
                act.wait_ge(raw_in[slot], i * (per_trip // RING * 16) + 16 * (unit // RING + 1))
                if unit >= RING:
                    act.wait_ge(units_done, i * per_trip + (unit - RING + 1))
                nc.scalar.copy(w_hi[:, slot, 0:k * P], raw[:, slot, 0:k * P]).then_inc(hi_ready, 1)

            def high(name, src, dst, i, per, k):
                nc.scalar.activation(dst[:, i * per + k, :], src[:, i * per + k, :], ACT.Identity,
                                     scale=gain(GAIN_OF[name], i * per + k)).then_inc(h_hi, 1)

            def squared(norm, src, i, per, k, signal=None):
                n = KT * NORMS[norm] + k
                if n >= 2:
                    act.wait_ge(sum_done, i * per + (n - 1))
                nc.scalar.activation(square[:, k % 2, :], src, ACT.Square).then_inc(sq_done, 1)

            def stream_tile(name, operands, norm):
                per = plan[name]["body"]

                def tile(i, done, b, first):
                    act.wait_ge(tile_out, i * per + (plan[name]["tile"] + b + 1))
                    for operand, dst in operands:
                        high(operand, X, dst, i, per, b)
                    at = i * (per * TOK) + b * TOK
                    squared(norm, X[:].rearrange("p k t -> p (k t)")[:, bass.ds(at, TOK)], i, per, b)
                return tile

            def output_tile(name, norm, g):
                per = plan[name]["body"]

                def tile(i, done, b, first):
                    act.wait_ge(units_done, done)
                    squared(norm, bank[b][:, 0:TOK], i, per, b)
                    nc.scalar.activation(H[:, i * per + b, :], bank[b][:, 0:TOK], ACT.Identity,
                                         scale=gain(g, i * per + b)).then_inc(tile_out, 1)
                return tile

            def relu(name):
                base, first_tile = PRODUCTS[name], plan[name]["tile"]

                def tile(i, done, b, first):
                    act.wait_ge(tile_out, i * 4 + (first_tile + b + 1))
                    nc.scalar.activation(a_hi[:, i * 4 + b, :], u_buf[:, b, :], ACT.Square).then_inc(a_hi_ready, 1)
                return tile

            def conv_high(name, i, b):
                pair = b // 2 - 1
                act.wait_ge(prod_ready, i * 2 + (PRODUCTS[name] + pair + 1))
                nc.scalar.copy(a_hi[:, i * 2 + pair, :], prod[:, pair % 2, :]).then_inc(a_hi_ready, 1)

            def conv_gelu(name):
                base, tap0, first_tile = PRODUCTS[name], FIRST_TAP[name], plan[name]["tile"]
                layer = 0 if name == "up_sb" else 1

                def tile(i, done, b, first):
                    pair = b // 2
                    act.wait_ge(tile_out, i * 4 + (first_tile + b + 1))
                    act.wait_ge(prod_ready, i * 2 + (base + pair - 1))
                    nc.scalar.activation(c_buf2[:, b, :], u_buf[:, b % 2, :], ACT.Identity,
                                         scale=conv[:, layer, 2, bass.ds(i * 4 + b, 1)],
                                         bias=conv[:, layer, 3, bass.ds(i * 4 + b, 1)]).then_inc(tap2_ready, 1)
                    if b % 2:
                        act.wait_ge(taps_done, i * 4 + (tap0 + b))
                        nc.scalar.activation(gate[:, pair, :], c_buf2[:, b - 1, :],
                                             ACT.Gelu_apprx_tanh).then_inc(gelu_ready, 1)
                    elif not (first and b == 0):
                        conv_high(name, i, b)
                return tile

            def project(name, before=None, after=None, middle=None):
                run_projection(act, name, RING, split, before, after, middle,
                               [("split", 0), ("middle", 0), ("split", 1), ("middle", 1), ("after", 0),
                                ("split", 2), ("after", 1), ("after", 2)])

            def norm_scale(columns=False):
                act.wait_ge(ms_done, n_norm[0] + 1)
                if n_norm[0] == NORMS["in_a"]:
                    act.wait_ge(tile_out, plan["in_a"]["tile"])
                    act.wait_ge(rstd_kept, 1)
                if columns:
                    act.wait_ge(v_out, VALUE_PIECES * n_columns[0])
                    n_columns[0] += 1
                    link(nc.scalar.activation(log_ms_col[:], bank[7][:, TOK:TOK + 2], ACT.Ln, scale=1.0 / D,
                                              bias=eps_col[:]))
                    nc.scalar.activation(rstd_col[:], log_ms_col[:], ACT.Exp, scale=-0.5).then_inc(col_ready, 1)
                link(nc.scalar.activation(log_ms[:], bank[7][:, 0:TOK], ACT.Ln, scale=1.0 / D, bias=eps_col[:]))
                nc.scalar.activation(rstd[:], log_ms[:], ACT.Exp, scale=-0.5).then_inc(rstd_ready, 1)
                n_norm[0] += 1

            def load_gelu():
                nc.scalar.preload_act_table(ACT.Gelu_apprx_tanh)

            def after_change(count, operands, norm):
                for k in range(KT):
                    act.wait_ge(x_changed, count + k + 1)
                    for operand, dst in operands:
                        high(operand, X, dst, 0, 0, k)
                    squared(norm, X[:, k, :], 0, 0, k)

            def rotate(name, j):
                pair = ROPE_PAIRS * list(FUSED).index(name) + j
                act.wait_ge(tile_out, plan[name]["tile"] + 2 * j + 4)
                if pair >= 2:
                    act.wait_ge(roped, pair - 1)
                at = 2 * (pair % 2)
                for piece in range(4):
                    src, dst = 32 * (piece ^ 1), 32 * piece
                    act.dma_start(ROT[dst:dst + 32, at:at + 2, :],
                                  Z[src:src + 32, 2 + 2 * j:4 + 2 * j, :]).then_inc(rot_in[pair % 2], 16)

            def values(name, middle=None):
                g = plan[name]
                units = value_units(name)
                for s, (group, first, width, k_tiles) in enumerate(units):
                    split(0, RING, g["unit"] + s + RING, KT)
                    if s == MS_AFTER[name]:
                        norm_scale(columns=True)
                    if k_tiles.stop == KT:
                        act.wait_ge(units_done, g["unit"] + s + 1)
                        act.wait_ge(col_ready, n_columns[0])
                        for tt in range(2):
                            nc.scalar.activation(v_tok[:, tt, first:first + width],
                                                 bank[2 * group + tt][:, 0:width], ACT.Identity,
                                                 scale=rstd_col[:, tt:tt + 1]).then_inc(v_out, 1)

            def query_key_tile(name, s):
                g = plan[name]
                split(0, RING, g["unit"] + g["values"] + s + RING, KT)

            def copy_values(dst, first, tiles):
                for j in range(0, tiles, 2):
                    act.wait_ge(vt_done, n_vt[0] + 1)
                    nc.scalar.copy(dst[:, :, (first + j) * P:(first + j + 2) * P],
                                   bank[6][:].rearrange("p (t c) -> p t c", t=2)).then_inc(vt_out, 1)
                    n_vt[0] += 1

            def attention(name):
                units, ahead = attention_units(name), AHEAD[name]
                stick = name == "in_sb"

                def exps(u):
                    n = u["n"]
                    w0, whole = geometry(u)
                    act.wait_ge(s_out, n + 1)
                    if stick:
                        nb = n_buf[:, n % 2, 0:whole]
                        link(nc.scalar.activation(nb, nb, ACT.Exp))
                        nc.scalar.activation(nb, nb, ACT.Ln, bias=1.0).then_inc(exp_done, 1)
                        return
                    free_probabilities(n)
                    for qt in range(2):
                        cols = slice(0, w0) if qt == 0 else slice(w0, whole)
                        last = nc.scalar.activation(p_buf[:, n % 3, cols], s_buf[:, n % 3, cols], ACT.Exp,
                                                    bias=unit_bias[:, n % 4, qt:qt + 1], scale=SCALE,
                                                    accum_out=unit_sum[:, n % 4, qt:qt + 1])
                    last.then_inc(exp_done, 1)

                def free_probabilities(n):
                    if n >= 3:
                        old = by_n[n - 3]
                        if old["emits"]:
                            act.wait_ge(t_done, old["t"] + 1)
                        else:
                            act.wait_ge(p_ready, n - 1)

                def weights(u):
                    n = u["n"]
                    _, whole = geometry(u)
                    act.wait_ge(arg_ready, n - units[0]["n"] + 1)
                    free_probabilities(n)
                    nc.scalar.activation(p_buf[:, n % 3, 0:whole], c_buf[:, n % 2, 0:whole],
                                         ACT.Exp).then_inc(p_ready, 1)

                def copies(u):
                    _, whole = geometry(u)
                    act.wait_ge(t_done, u["t"] + 1)
                    if u["t"] >= 2:
                        act.wait_ge(o_done, u["t"] - 1)
                    nc.scalar.copy(pt_buf[:, u["t"] % 2, 0:whole], bank[6][:, 0:whole]).then_inc(t_out, 1)

                def out_hi(u):
                    j = u["j"]
                    act.wait_ge(o_done, u["t"] + 1)
                    src = bank[(7, 3)[u["tile"] % 2]][:, 0:TOK]
                    if u["diff"]:
                        nc.scalar.copy(H[:, j, :], src).then_inc(sub_copied, 1)
                        if j >= 2:
                            act.wait_ge(sub_ms, j - 1)
                        nc.scalar.activation(square[:, j % 2, :], src, ACT.Square).then_inc(sub_out, 1)
                    else:
                        nc.scalar.copy(o_hi[:, output_feature_tile(u), :], src).then_inc(o_hi_out, 1)

                def sub_scale(u):
                    j = u["j"]
                    act.wait_ge(sub_ms, j + 1)
                    if j:
                        act.wait_ge(sub_rstd, j)
                    link(nc.scalar.activation(log_ms[:], bank[2][:, j % 2 * TOK:(j % 2 + 1) * TOK], ACT.Ln,
                                              scale=1.0 / (2 * HEAD), bias=eps_col[:]))
                    if j >= 2:
                        act.wait_ge(sub_scaled, j - 1)
                    nc.scalar.activation(sub_rms[:, j % 2, :], log_ms[:], ACT.Exp, scale=-0.5).then_inc(sub_rstd, 1)

                def sub_high(u):
                    j = u["j"]
                    act.wait_ge(sub_scaled, j + 1)
                    nc.scalar.copy(o_hi[:, j, :], H[:, j, :]).then_inc(sub_hi, 1)

                def leave_psum(i):
                    if 0 <= i - ahead < len(units) and units[i - ahead]["emits"]:
                        copies(units[i - ahead])
                    if 0 <= i - ahead - 1 < len(units) and units[i - ahead - 1]["half"]:
                        out_hi(units[i - ahead - 1])

                def step(i):
                    alone = fused_tiles(name) - LAG[name]
                    if i > alone:
                        leave_psum(i - 1)
                    if i < len(units):
                        exps(units[i])
                    if stick and 0 <= i - 2 < len(units):
                        weights(units[i - 2])
                    if i < alone:
                        leave_psum(i)
                    if 0 <= i - 5 < len(units) and units[i - 5]["diff"] and units[i - 5]["half"]:
                        sub_scale(units[i - 5])
                    if 0 <= i - 6 < len(units) and units[i - 6]["diff"] and units[i - 6]["half"]:
                        sub_high(units[i - 6])
                    j, odd = divmod(i + LAG[name] - 3, 2)
                    if "mem_" in FUSED[name][0] and odd == 0 and 0 <= j < ROPE_PAIRS:
                        rotate(name, j)
                return step

            nc.scalar.preload_act_table_set("natural_log_exp_and_others")
            act.wait_ge(mem_in, 32)
            for k in range(KT):
                high("mem_a", ZM, a_hi, 0, 0, k)
            for u in range(RING):
                split(0, RING, u, KT)
                for k in (2 * u, 2 * u + 1):
                    squared("mem_a", ZM[:, k, :], 0, 0, k)
                    high("mem_b", ZM, h2_hi, 0, 0, k)
            act.wait_ge(x_in, 16)
            for k in range(KT):
                high("in_a", X, h1_hi, 0, 0, k)
            act.wait_ge(a_ready, RING)
            project("mem_a", middle=norm_scale)
            for k in range(KT):
                squared("in_a", X[:, k, :], 0, 0, k)
            values("in_a")
            copy_values(mv_tok[:, 0], 0, 2)
            act.wait_ge(lam_ready, 1)
            nc.scalar.activation(lam_exp[:], lam_sum[:], ACT.Exp).then_inc(lam_ready, 1)
            act.wait_ge(wf_in, 16)
            nc.scalar.copy(wf_hi[:], H[:, 0:KT // 2, :].rearrange("p a (b c) -> p (a b) c", c=P)).then_inc(wf_split, 1)
            fused("in_a", lambda s: query_key_tile("in_a", s), attention("in_a"), 6)
            project("out_a", before=stream_tile("out_a", [("up_a", h2_hi)], "up_a"))
            project("up_a", after=relu("up_a"), middle=norm_scale)
            project("down_a", before=stream_tile("down_a", [("in_b", h1_hi), ("q_b", h2_hi)], "in_b"))
            values("in_b")
            copy_values(mv_tok[:, 1], 0, 2)
            fused("in_b", lambda s: query_key_tile("in_b", s), attention("in_b"), 4)
            project("out_b", before=stream_tile("out_b", [("up_b", h2_hi)], "up_b"))
            project("up_b", after=relu("up_b"), middle=norm_scale)
            project("down_b", before=stream_tile("down_b", [], "final"))
            norm_scale()
            after_change(0, [("in_sb", h1_hi)], "in_sb")
            values("in_sb")
            fused("in_sb", lambda s: query_key_tile("in_sb", s), attention("in_sb"), 5)
            project("out_sb", before=output_tile("out_sb", "post_sb", "sb_post_g_2"))
            norm_scale()
            after_change(KT, [("up_sb", h2_hi)], "up_sb")
            project("up_sb", after=conv_gelu("up_sb"), middle=(norm_scale, load_gelu))
            conv_high("up_sb", plan["up_sb"]["trips"], 0)
            nc.scalar.preload_act_table_set("natural_log_exp_and_others")
            project("down_sb", before=output_tile("down_sb", "post_ffn_sb", "ffn_post_g_2.0"))
            norm_scale()
            after_change(2 * KT, [("in_fox", h1_hi), ("q_fox", h2_hi)], "in_fox")
            values("in_fox")
            act.wait_ge(f_abs, 1)
            link(nc.scalar.activation(f_n[:], f_n[:], ACT.Exp))
            nc.scalar.activation(f_n[:], f_n[:], ACT.Ln, bias=1.0).then_inc(f_log, 1)
            nc.scalar.copy(ident_r[:], ident[:])
            act.wait_ge(f_cum, 1)
            nc.scalar.copy(fcum_hi[:], f_x[:]).then_inc(f_high, 1)
            fused("in_fox", lambda s: query_key_tile("in_fox", s), attention("in_fox"), 4)
            project("out_fox", before=output_tile("out_fox", "post_fox", "fox_post_g_2"))
            norm_scale()
            after_change(3 * KT, [("up_fox", h2_hi)], "up_fox")
            project("up_fox", after=conv_gelu("up_fox"), middle=(norm_scale, load_gelu))
            conv_high("up_fox", plan["up_fox"]["trips"], 0)
            nc.scalar.preload_act_table_set("natural_log_exp_and_others")
            project("down_fox", before=output_tile("down_fox", "post_ffn_fox", "ffn_post_g_2.1"))
            norm_scale()

        @block.vector
        def _(dve):
            steps, n_x, early = [0], [0], set()

            def link(instruction):
                steps[0] += 1
                instruction.then_inc(dve_step, 1)
                dve.wait_ge(dve_step, steps[0])

            def split(i, per_trip, unit, k):
                slot = unit % RING
                if unit in early:
                    early.remove(unit)
                    return
                dve.wait_ge(hi_ready, i * per_trip + (unit + 1))
                nc.vector.tensor_tensor(w_lo[:, slot, 0:k * P], raw[:, slot, 0:k * P],
                                        w_hi[:, slot, 0:k * P].bitcast(f32), ALU.subtract).then_inc(lo_ready, 1)

            def split_early(name):
                unit = plan[name]["unit"] + RING - 1
                split(0, RING, unit, KT)
                early.add(unit)

            def query_key_tile(name, s):
                g = plan[name]
                unit = g["unit"] + g["values"] + s
                dve.wait_ge(units_done, unit + 1)
                dve.wait_ge(rstd_ready, NORMS[name] + 1)
                dst, scale = (Z[:, s, :] if s < 16 else None), rstd
                memory = s - (g["tiles"] - g["values"])
                if memory >= 0:
                    dve.wait_ge(rstd_kept, 1)
                    dst, scale = ZM[:, 4 + memory, :], rstd_mem
                nc.vector.tensor_tensor(dst, bank[s % 2][:, 0:TOK], scale[:], ALU.mult).then_inc(tile_out, 1)
                split(0, RING, unit + RING - 1, KT)

            def values(name):
                g = plan[name]
                for s in range(g["values"]):
                    split(0, RING, g["unit"] + s + RING - 1, KT)

            def take(name, norm, dst, shift=0):
                per = plan[name]["body"]

                def tile(i, done, b, first):
                    dve.wait_ge(units_done, done)
                    dve.wait_ge(rstd_ready, NORMS[norm] + 1)
                    nc.vector.tensor_tensor(dst[:, i * per + (shift + b), :], bank[b][:, 0:TOK], rstd[:],
                                            ALU.mult).then_inc(tile_out, 1)
                return tile

            def low(name, src, dst_hi, dst_lo, i, per, k):
                at = i * per + k
                dve.wait_ge(h_hi, operand_count(name, i, per, k))
                nc.vector.scalar_tensor_tensor(dst_lo[:, at, :], src[:, at, :], gain(GAIN_OF[name], at),
                                               dst_hi[:, at, :].bitcast(f32), ALU.mult,
                                               ALU.subtract).then_inc(h_lo, 1)

            def residual(name, operands):
                per = plan[name]["body"]

                def tile(i, done, b, first):
                    dve.wait_ge(units_done, done)
                    x = X[:, i * per + b, :]
                    nc.vector.tensor_tensor(x, bank[b][:, 0:TOK], x, ALU.add).then_inc(tile_out, 1)
                    for operand, hi, lo in operands:
                        low(operand, X, hi, lo, i, per, b)
                return tile

            def split_product(i, per, m, slot, dst):
                dve.wait_ge(prod_ready, i * per + (m + 1))
                dve.wait_ge(a_hi_ready, i * per + (m + 1))
                nc.vector.tensor_tensor(a_lo[:, dst, :], prod[:, slot, :], a_hi[:, dst, :].bitcast(f32),
                                        ALU.subtract).then_inc(a_ready, 1)

            def relu(name):
                base = PRODUCTS[name]

                def before(i, done, b, first):
                    dve.wait_ge(units_done, done)
                    dve.wait_ge(rstd_ready, NORMS[name] + 1)
                    dve.wait_ge(a_ready, i * 4 + (base + b + 1))
                    nc.vector.scalar_tensor_tensor(u_buf[:, b, :], bank[b][:, 0:TOK], 0.0, rstd[:], ALU.max,
                                                   ALU.mult).then_inc(tile_out, 1)

                def after(i, done, b, first):
                    split_product(i, 4, base + b, b % 2, i * 4 + b)
                return before, after

            def conv_low(name, i, b):
                pair = b // 2 - 1
                split_product(i, 2, PRODUCTS[name] + pair, pair % 2, i * 2 + pair)

            def conv_taps(name):
                tap0, first_tile = FIRST_TAP[name], plan[name]["tile"]
                layer = 0 if name == "up_sb" else 1

                def before(i, done, b, first):
                    dve.wait_ge(units_done, done)
                    dve.wait_ge(rstd_ready, NORMS[name] + 1)
                    if not first or b >= 2:
                        dve.wait_ge(m_ready, i * 4 + (tap0 + b - 1))
                        dve.wait_ge(tap1_ready, i * 4 + (tap0 + b - 1))
                    nc.vector.tensor_tensor(u_buf[:, b % 2, :], bank[b][:, 0:TOK], rstd[:],
                                            ALU.mult).then_inc(tile_out, 1)

                def after(i, done, b, first):
                    dve.wait_ge(tap2_ready, i * 4 + (tap0 + b + 1))
                    dve.wait_ge(tile_out, i * 4 + (first_tile + b + 1))
                    nc.vector.scalar_tensor_tensor(c_buf2[:, b, 1:TOK], u_buf[:, b % 2, 0:TOK - 1],
                                                   conv[:, layer, 1, bass.ds(i * 4 + b, 1)],
                                                   c_buf2[:, b, 1:TOK], ALU.mult, ALU.add).then_inc(tap1_ready, 1)
                    if b % 2 == 0 and not (first and b == 0):
                        conv_low(name, i, b)
                return before, after

            def project(name, before=None, after=None):
                run_projection(dve, name, RING - 1, split, before, after, None,
                               [("split", 0), ("split", 1), ("before", 0), ("before", 1), ("split", 2),
                                ("after", 0), ("before", 2), ("after", 1), ("after", 2)])

            def rstd_next(norm):
                dve.wait_ge(rstd_ready, NORMS[norm] + 1)

            def add_normed(norm, operands):
                if operands:
                    split_early(operands[0][0])
                rstd_next(norm)
                a = n_x[0]

                def lows(k):
                    for operand, hi, lo in operands:
                        low(operand, X, hi, lo, 0, 0, k)

                for k in range(KT):
                    if k % 2 == 0:
                        nc.vector.tensor_tensor(H[:, k, :], H[:, k, :], rstd[:], ALU.mult).then_inc(y_even, 1)
                        dve.wait_ge(y_even, (a - KT + k) // 2 + 1)
                    else:
                        dve.wait_ge(y_odd, (a - KT + k) // 2 + 1)
                    nc.vector.tensor_tensor(X[:, k, :], X[:, k, :], H[:, k, :], ALU.add).then_inc(x_changed, 1)
                    if k:
                        lows(k - 1)
                lows(KT - 1)
                n_x[0] += KT

            def attention(name):
                units, ahead = attention_units(name), AHEAD[name]
                stick = name == "in_sb"
                no_mask = mask_in[:, P:2 * P].unsqueeze(1).broadcast_to([P, 2, P])

                def query_tiles(u):
                    w0, whole = geometry(u)
                    return slice(0, w0), slice(w0, whole)

                def masked(u):
                    n, mem = u["n"], u["mem"]
                    _, whole = geometry(u)

                    def pieces(ap):
                        return ap.rearrange("p (a c) -> p a c", c=P) if mem else ap
                    b = bank[4 + n % 2]
                    dve.wait_ge(s_done, n + 1)
                    if n >= 2:
                        dve.wait_ge(exp_done, n - 1)
                    if stick:
                        if n - u["first"] >= 2:
                            dve.wait_ge(scanned, n - u["first"] - 1)
                        if n - u["first"] >= 3:
                            dve.wait_ge(arg_ready, n - u["first"] - 2)
                        z = s_buf[:, n % 3, 0:whole]
                        link(nc.vector.scalar_tensor_tensor(z, b[:, 0:whole], SCALE, mask_ex[:], ALU.mult, ALU.add))
                        nc.vector.scalar_tensor_tensor(n_buf[:, n % 2, 0:whole], z, -1.0, z, ALU.mult,
                                                       ALU.min).then_inc(s_out, 1)
                        return
                    for qt, cols in enumerate(query_tiles(u)):
                        last = nc.vector.tensor_tensor_reduce(
                            out=pieces(s_buf[:, n % 3, cols]), in0=pieces(b[:, cols]),
                            in1=no_mask if mem else mask_in[:, cols], scale=1.0, scalar=-3.0e38, op0=ALU.add, op1=ALU.max,
                            accum_out=unit_max[:, n % 4, qt:qt + 1])
                    link(last)
                    nc.vector.tensor_scalar(unit_bias[:, n % 4, :], unit_max[:, n % 4, :], -SCALE, None,
                                            ALU.mult).then_inc(s_out, 1)

                def normalised(u):
                    n = u["n"]
                    rcp = unit_rcp[:, n % 4, :]
                    dve.wait_ge(exp_done, n + 1)
                    link(nc.vector.reciprocal(rcp, unit_sum[:, n % 4, :]))
                    second = u["diff"] and u["half"]
                    if second:
                        link(nc.vector.tensor_scalar(rcp, rcp, neg_lam[:], None, ALU.mult))
                        dve.wait_ge(p_ready, n)
                    for qt, cols in enumerate(query_tiles(u)):
                        p = p_buf[:, n % 3, cols]
                        if second:
                            last = nc.vector.scalar_tensor_tensor(p, p, rcp[:, qt:qt + 1],
                                                                  p_buf[:, (n - 1) % 3, cols], ALU.mult, ALU.add)
                        else:
                            last = nc.vector.tensor_scalar(p, p, rcp[:, qt:qt + 1], None, ALU.mult)
                    last.then_inc(p_ready, 1)

                def log_weights(u):
                    n = u["n"]
                    _, whole = geometry(u)
                    z, sp, c = s_buf[:, n % 3, 0:whole], n_buf[:, n % 2, 0:whole], c_buf[:, n % 2, 0:whole]
                    dve.wait_ge(exp_done, n + 1)
                    link(nc.vector.scalar_tensor_tensor(sp, z, 0.0, sp, ALU.max, ALU.add))
                    if n - units[0]["n"] >= 2:
                        dve.wait_ge(p_ready, n - 1)
                    for cols in query_tiles(u):
                        last = nc.vector.tensor_tensor_scan(c[:, cols][:, ::-1], ones[:, 0:cols.stop - cols.start],
                                                            sp[:, cols][:, ::-1], 0.0, ALU.mult, ALU.subtract)
                    last.then_inc(scanned, 1)

                def out_lo(u):
                    dve.wait_ge(o_hi_out, u["plain"] + 1)
                    j = output_feature_tile(u)
                    nc.vector.tensor_tensor(o_lo[:, j, :], bank[(7, 3)[u["tile"] % 2]][:, 0:TOK],
                                            o_hi[:, j, :].bitcast(f32), ALU.subtract).then_inc(o_out, 1)

                def sub_scale(u):
                    j = u["j"]
                    dve.wait_ge(sub_rstd, j + 1)
                    nc.vector.scalar_tensor_tensor(H[:, j, :], H[:, j, :], subln_s[:], sub_rms[:, j % 2, :],
                                                   ALU.mult, ALU.mult).then_inc(sub_scaled, 1)

                def rope_sin(j):
                    pair = ROPE_PAIRS * list(FUSED).index(name) + j
                    rot = ROT[:, 2 * (pair % 2):2 * (pair % 2) + 2, :]
                    dve.wait_ge(rot_in[pair % 2], 64 * (pair // 2 + 1))
                    nc.vector.tensor_tensor(rot, rot, rope_s[:].unsqueeze(1).broadcast_to([P, 2, TOK]),
                                            ALU.mult).then_inc(sin_done, 1)

                def sub_low(u):
                    j = u["j"]
                    dve.wait_ge(sub_hi, j + 1)
                    nc.vector.tensor_tensor(o_lo[:, j, :], H[:, j, :], o_hi[:, j, :].bitcast(f32),
                                            ALU.subtract).then_inc(sub_lo, 1)

                def step(i):
                    if i < len(units):
                        masked(units[i])
                    if 0 <= i - 1 < len(units):
                        log_weights(units[i - 1]) if stick else normalised(units[i - 1])
                    if 0 <= i - ahead - 2 < len(units):
                        done = units[i - ahead - 2]
                        if done["half"] and not done["diff"]:
                            out_lo(done)
                    if 0 <= i - 5 < len(units) and units[i - 5]["half"] and units[i - 5]["diff"]:
                        sub_scale(units[i - 5])
                    if 0 <= i - 6 < len(units) and units[i - 6]["half"] and units[i - 6]["diff"]:
                        sub_low(units[i - 6])
                    j, odd = divmod(i + LAG[name] - 4, 2)
                    if "mem_" in FUSED[name][0] and odd == 0 and 0 <= j < ROPE_PAIRS:
                        rope_sin(j)
                return step

            nc.vector.memset(log_ms[:], 0.0).then_inc(warm_ready, 1)
            nc.vector.memset(eps_col[:], EPS).then_inc(a_ready, RING)
            for k in range(KT):
                low("mem_a", ZM, a_hi, a_lo, 0, 0, k)
            for u in range(RING - 1):
                split(0, RING, u, KT)
            for k in range(KT):
                low("mem_b", ZM, h2_hi, h2_lo, 0, 0, k)
            for k in range(KT):
                low("in_a", X, h1_hi, h1_lo, 0, 0, k)
            dve.wait_ge(h_lo, 2 * KT)
            project("mem_a", before=take("mem_a", "mem_a", ZM))
            nc.vector.tensor_copy(rstd_mem[:], rstd[:]).then_inc(rstd_kept, 1)
            values("in_a")
            dve.wait_ge(consts_in, 16 * len(CONSTS))
            nc.vector.tensor_scalar(subln_s[:], subln[:], 1.0 - LAM_INIT, None, ALU.mult)
            for pair in range(2):
                last = nc.vector.tensor_tensor(lam_prod[:, pair, :], lam_in[:, 2 * pair, :],
                                               lam_in[:, 2 * pair + 1, :], ALU.mult)
            link(last)
            nc.vector.tensor_reduce(lam_sum[:], lam_prod[:], AX.X, ALU.add).then_inc(lam_ready, 1)
            dve.wait_ge(lam_ready, 2)
            link(nc.vector.tensor_tensor(neg_lam[:], lam_exp[:, 1:2], lam_exp[:, 0:1], ALU.subtract))
            nc.vector.tensor_scalar(neg_lam[:], neg_lam[:], -LAM_INIT, None, ALU.add).then_inc(lam_ready, 1)
            dve.wait_ge(wf_split, 1)
            nc.vector.tensor_tensor(wf_lo[:], H[:, 0:KT // 2, :].rearrange("p a (b c) -> p (a b) c", c=P),
                                    wf_hi[:].bitcast(f32), ALU.subtract).then_inc(wf_split, 1)
            dve.wait_ge(lam_ready, 3)
            fused("in_a", lambda s: query_key_tile("in_a", s), attention("in_a"), 6)
            project("out_a", before=residual("out_a", [("up_a", h2_hi, h2_lo)]))
            project("up_a", *relu("up_a"))
            project("down_a", before=residual("down_a", [("in_b", h1_hi, h1_lo), ("q_b", h2_hi, h2_lo)]))
            values("in_b")
            fused("in_b", lambda s: query_key_tile("in_b", s), attention("in_b"), 4)
            project("out_b", before=residual("out_b", [("up_b", h2_hi, h2_lo)]))
            project("up_b", *relu("up_b"))
            project("down_b", before=residual("down_b", []))
            split_early("in_sb")
            rstd_next("final")
            for k in range(KT):
                nc.vector.scalar_tensor_tensor(X[:, k, :], X[:, k, :], gain("final_norm", k), rstd[:], ALU.mult,
                                               ALU.mult).then_inc(x_changed, 1)
                if k:
                    dve.wait_ge(x_changed, k)
                    low("in_sb", X, h1_hi, h1_lo, 0, 0, k - 1)
            dve.wait_ge(x_changed, KT)
            low("in_sb", X, h1_hi, h1_lo, 0, 0, KT - 1)
            n_x[0] += KT
            values("in_sb")
            fused("in_sb", lambda s: query_key_tile("in_sb", s), attention("in_sb"), 5)
            project("out_sb")
            add_normed("post_sb", [("up_sb", h2_hi, h2_lo)])
            project("up_sb", *conv_taps("up_sb"))
            conv_low("up_sb", plan["up_sb"]["trips"], 0)
            project("down_sb")
            add_normed("post_ffn_sb", [("in_fox", h1_hi, h1_lo), ("q_fox", h2_hi, h2_lo)])
            values("in_fox")
            dve.wait_ge(f_logits, 1)
            dve.wait_ge(rstd_ready, NORMS["in_fox"] + 1)
            link(nc.vector.tensor_tensor(f_x[:], bank[6][:, 0:TOK], rstd[:], ALU.mult))
            link(nc.vector.tensor_scalar(f_x[:], f_x[:], b_f[:], -1.0, ALU.add, ALU.mult))
            nc.vector.scalar_tensor_tensor(f_n[:], f_x[:], -1.0, f_x[:], ALU.mult, ALU.min).then_inc(f_abs, 1)
            dve.wait_ge(f_log, 1)
            link(nc.vector.scalar_tensor_tensor(f_p[:], f_x[:], 0.0, f_n[:], ALU.max, ALU.add))
            link(nc.vector.tensor_tensor_scan(f_sum[:], ones[:], f_p[:], 0.0, ALU.mult, ALU.add))
            nc.vector.tensor_scalar(f_x[:], f_sum[:], 1.0 / SCALE, None, ALU.mult).then_inc(f_cum, 1)
            dve.wait_ge(f_high, 1)
            dve.wait_ge(f_cum, 1)
            nc.vector.tensor_tensor(fcum_lo[:], f_x[:], fcum_hi[:].bitcast(f32), ALU.subtract).then_inc(f_ready, 1)
            fused("in_fox", lambda s: query_key_tile("in_fox", s), attention("in_fox"), 4)
            project("out_fox")
            add_normed("post_fox", [("up_fox", h2_hi, h2_lo)])
            project("up_fox", *conv_taps("up_fox"))
            conv_low("up_fox", plan["up_fox"]["trips"], 0)
            project("down_fox")
            add_normed("post_ffn_fox", [])

        @block.gpsimd
        def _(pool):
            steps, n_odd = [0], [0]

            def link(instruction):
                steps[0] += 1
                instruction.then_inc(pool_step, 1)
                pool.wait_ge(pool_step, steps[0])

            def sum_squares(norm):
                n = NORMS[norm]
                if n:
                    pool.wait_ge(ms_done, n)
                if n and list(NORMS)[n - 1] in DIRECT:
                    nc.gpsimd.memset(sumsq[:], 0.0).then_inc(sum_done, 1)
                else:
                    link(nc.gpsimd.memset(sumsq[:], 0.0))

                def add(i, b, first):
                    pool.wait_ge(sq_done, i * 2 + (KT * n + b + 1))
                    if n or not first:
                        pool.wait_ge(sum_done, i * 2 + (KT * n + b))
                    nc.gpsimd.tensor_tensor(sumsq[:], sumsq[:], square[:, b, :], ALU.add).then_inc(sum_done, 1)

                add(0, 0, True)
                add(0, 1, False)
                with pool.Fori(1, KT // 2 - 1) as i:
                    add(i, 0, False)
                    add(i, 1, False)
                add(KT // 2 - 1, 0, False)
                if norm not in DIRECT:
                    add(KT // 2 - 1, 1, False)

            def rope(layer):
                for j in range(ROPE_PAIRS):
                    pair = ROPE_PAIRS * layer + j
                    at = 2 * (pair % 2)
                    z, rot = Z[:, 2 + 2 * j:4 + 2 * j, :], ROT[:, at:at + 2, :]
                    pool.wait_ge(rot_in[pair % 2], 64 * (pair // 2 + 1))
                    link(nc.gpsimd.tensor_tensor(z, z, rope_c[:].unsqueeze(1).broadcast_to([P, 2, TOK]), ALU.mult))
                    pool.wait_ge(sin_done, pair + 1)
                    nc.gpsimd.tensor_tensor(z, z, rot, ALU.add).then_inc(roped, 1)

            def stick_weights():
                for u in heads["stick"]:
                    n = u["n"]
                    _, whole = geometry(u)
                    c = c_buf[:, n % 2, 0:whole]
                    pool.wait_ge(scanned, n - u["first"] + 1)
                    nc.gpsimd.tensor_tensor(c, c, s_buf[:, n % 3, 0:whole], ALU.add).then_inc(arg_ready, 1)

            def scale_odd(norm):
                pool.wait_ge(rstd_ready, NORMS[norm] + 1)
                for k in range(1, KT, 2):
                    nc.gpsimd.tensor_tensor(H[:, k, :], H[:, k, :], rstd[:], ALU.mult).then_inc(y_odd, 1)

            def relu(name):
                base, first_tile = PRODUCTS[name], plan[name]["tile"]
                with pool.Fori(0, plan[name]["trips"]) as i:
                    for b in range(4):
                        pool.wait_ge(tile_out, i * 4 + (first_tile + b + 1))
                        pool.wait_ge(a_ready, i * 4 + (base + b + RING - 1))
                        nc.gpsimd.tensor_tensor(prod[:, b % 2, :], u_buf[:, b, :], u_buf[:, b, :],
                                                ALU.mult).then_inc(prod_ready, 1)

            def conv_products(name):
                base, tap0, first_tile = PRODUCTS[name], FIRST_TAP[name], plan[name]["tile"]
                layer = 0 if name == "up_sb" else 1

                def trip(i, first):
                    for b in range(4):
                        pair = base + b // 2
                        pool.wait_ge(tile_out, i * 4 + (first_tile + b + 1))
                        if not (first and b < 2):
                            pool.wait_ge(taps_done, i * 4 + (tap0 + b - 1))
                        nc.gpsimd.tensor_tensor(m_buf[:, b % 2, :], u_buf[:, b % 2, :],
                                                conv[:, layer, 0, bass.ds(i * 4 + b, 1)].broadcast_to([P, TOK]),
                                                ALU.mult).then_inc(m_ready, 1)
                        pool.wait_ge(m_ready, i * 4 + (tap0 + b + 1))
                        pool.wait_ge(tap1_ready, i * 4 + (tap0 + b + 1))
                        c = c_buf2[:, b, 2:TOK]
                        nc.gpsimd.tensor_tensor(c, c, m_buf[:, b % 2, 0:TOK - 2], ALU.add).then_inc(taps_done, 1)
                        if b % 2:
                            pool.wait_ge(taps_done, i * 4 + (tap0 + b + 1))
                            pool.wait_ge(gelu_ready, i * 2 + (pair - PRODUCTS["up_sb"] + 1))
                            pool.wait_ge(a_ready, i * 2 + (pair + RING - 1))
                            nc.gpsimd.tensor_tensor(prod[:, b // 2, :], gate[:, b // 2, :], c_buf2[:, b, :],
                                                    ALU.mult).then_inc(prod_ready, 1)

                trip(0, True)
                with pool.Fori(1, plan[name]["trips"]) as i:
                    trip(i, False)

            sum_squares("mem_a")
            sum_squares("in_a")
            pool.wait_ge(consts_in, 16 * len(CONSTS))
            rope(0)
            sum_squares("up_a")
            relu("up_a")
            sum_squares("in_b")
            rope(1)
            sum_squares("up_b")
            relu("up_b")
            sum_squares("final")
            sum_squares("in_sb")
            stick_weights()
            sum_squares("post_sb")
            scale_odd("post_sb")
            sum_squares("up_sb")
            conv_products("up_sb")
            sum_squares("post_ffn_sb")
            scale_odd("post_ffn_sb")
            sum_squares("in_fox")
            sum_squares("post_fox")
            scale_odd("post_fox")
            sum_squares("up_fox")
            conv_products("up_fox")
            sum_squares("post_ffn_fox")
            scale_odd("post_ffn_fox")


def tiles_of(w):
    k, n = w.shape
    return np.ascontiguousarray(w.reshape(k // P, P, n // P, P).transpose(2, 1, 0, 3).reshape(n // P, P, k))


def in_units(name, v, q, k, q_mem=None):
    values = [np.concatenate([v[P * kt:P * (kt + 1), first:first + width] for kt in k_tiles], axis=1)[None]
              for _, first, width, k_tiles in value_units(name)]
    n = q.shape[1] // P
    pairs = np.stack([tiles_of(q), tiles_of(k)], axis=1).reshape(2 * n, P, D)
    return np.concatenate(values + ([] if q_mem is None else [tiles_of(q_mem)]) + [pairs])


def feature_major(t):
    return np.ascontiguousarray(t.T.reshape(KT, P, TOK).transpose(1, 0, 2))


def shape_constants():
    half = HEAD // 2
    inv = (1.0 / (np.float32(10000.0) ** (np.arange(half, dtype=np.float32) / np.float32(half)))).astype(np.float32)
    angle = (np.arange(TOK, dtype=np.float32)[:, None] * inv[None, :]).T
    cos, sin = np.cos(angle).astype(np.float32), np.sin(angle).astype(np.float32)
    q, k = np.arange(P)[:, None], np.arange(P)[None, :]
    inclusive = np.where(k <= q, 0.0, NEG).astype(np.float32)
    strict = np.where(k < q, 0.0, NEG).astype(np.float32)
    seen = np.zeros((P, P), np.float32)
    return {"ones": np.ones((P, TOK), np.float32),
            "ident": np.eye(P, dtype=np.float32), "rope_c": np.concatenate([cos] * 4),
            "rope_s": np.concatenate([-sin, sin] * 2),
            "mask_in": np.concatenate([inclusive, seen, inclusive], axis=1),
            "mask_ex": np.concatenate([strict, seen, strict], axis=1)}


def kernel(**inputs):
    import concourse.bacc as bacc
    from concourse.bass_utils import run_bass_kernel_spmd

    a = {k: np.asarray(v) for k, v in inputs.items()}
    up2 = [a["w_up_2"][i].reshape(D, 2, D_FF2 // P, P).transpose(0, 2, 1, 3).reshape(D, 2 * D_FF2)
           for i in range(2)]
    qkv = a["w_kvf_2"]
    weights = {"mem_a": a["a_w_mem_kv"][0], "mem_b": a["b_w_mem_kv"][0],
               "out_a": a["a_w_out"][0], "up_a": a["a_w_up"][0], "down_a": a["a_w_down"][0],
               "out_b": a["b_w_out"][0], "up_b": a["b_w_up"][0],
               "down_b": a["b_w_down"][0], "out_sb": a["sb_w_o_2"][0],
               "up_sb": up2[0], "down_sb": a["w_down_2"][0],
               "out_fox": a["fox_w_o_2"][0], "up_fox": up2[1], "down_fox": a["w_down_2"][1]}
    arrays = {"w_" + name: tiles_of(w) for name, w in weights.items()}
    a_in, b_in, sb_in = a["a_w_in"][0], a["b_w_in"][0], a["sb_w_qkv_2"][0]
    s = SELF_W
    arrays["w_in_a"] = in_units("in_a", a_in[:, 2 * s:3 * s], a_in[:, :s], a_in[:, s:2 * s], a_in[:, 3 * s:])
    arrays["w_in_b"] = in_units("in_b", a["w_kv"][:, s:], b_in[:, :s], a["w_kv"][:, :s], b_in[:, s:])
    arrays["w_in_sb"] = in_units("in_sb", sb_in[:, 2 * D:], sb_in[:, :D], sb_in[:, D:2 * D])
    arrays["w_in_fox"] = in_units("in_fox", qkv[:, D:2 * D], a["fox_w_q_2"][0], qkv[:, :D])
    arrays["x"] = feature_major(a["x"][0])
    arrays["mem"] = feature_major(a["mem"][0])

    def row(name):
        base, _, at = name.partition(".")
        return a[base][int(at)] if at else a[base].reshape(D)

    arrays["gains"] = np.ascontiguousarray(np.stack([row(n) for n in GAINS]).reshape(len(GAINS), KT, P)
                                           .transpose(2, 0, 1))
    arrays["subln"] = np.ascontiguousarray(a["a_subln"].reshape(P, 1))
    taps = np.concatenate([a["conv_w_2"], a["conv_b_2"][:, None, :]], axis=1)
    arrays["conv"] = np.ascontiguousarray(taps.reshape(2, 4, 2, D_FF2 // P, P).transpose(4, 0, 1, 3, 2)
                                          .reshape(P, 2, 4, 2 * D_FF2 // P))
    arrays["lam"] = np.ascontiguousarray(np.broadcast_to(a["a_lambda"][0], (P, 4, HEAD)))
    w_f, b_f = np.zeros((D, P), np.float32), np.zeros((P, 1), np.float32)
    for at in (0, HEAD):
        w_f[:, at:at + HEADS2] = qkv[:, 2 * D:]
        b_f[at:at + HEADS2, 0] = a["b_f_2"]
    arrays["w_f"] = np.ascontiguousarray(w_f.reshape(KT, P, P).transpose(1, 0, 2))
    arrays["b_f"] = b_f
    arrays.update(shape_constants())

    nc = bacc.Bacc("TRN2", target_bir_lowering=False, num_devices=1)
    ins = {name: nc.dram_tensor("in_" + name, v.shape, mybir.dt.from_np(v.dtype), kind="ExternalInput").ap()
           for name, v in arrays.items()}
    out = nc.dram_tensor("out_x", (P, KT, TOK), mybir.dt.float32, kind="ExternalOutput").ap()
    build_program(nc, ins, out)
    r = run_bass_kernel_spmd(nc, [{"in_" + name: v for name, v in arrays.items()}], core_ids=[0])
    got = np.asarray(r.results[0]["out_x"])
    return np.ascontiguousarray(got.transpose(1, 0, 2).reshape(D, TOK).T).reshape(1, TOK, D)
```
